# Optimizing a Trainium2 kernel written in Bass

```python
import jax
import jax.numpy as jnp
from jax import lax
import numpy as np

D_MODEL = 1024
BATCH = 1
SEQ = 128
DEPTH = 1
DEC_BATCH = 1
DEC_SEQ = 1024
PAST_LEN = 128

GRID_W = 64
MIX_W = D_MODEL
GLA_WIDTH = 512
GLA_HEADS = 4
GLA_DK = 64
GLA_DV = 128
GLA_LORA = 16
GLA_GATE_NORM = 16.0
GLA_CHUNK = 64
SWA_WIDTH = 512
SWA_HEAD_DIM = 64
SWA_HEADS = 8
SWA_KV_HEADS = 2
SWA_GROUP = 4
WINDOW = 128
ATTN_BLOCK = 128
ROPE_BASE = 10000.0
N_EXPERTS = 64
TOP_K = 8
N_EXPERT_GROUPS = 8
TOPK_GROUPS = 4
EXPERT_FF = 128
SHARED_FF = 256
ROUTED_SCALE = 2.5
EPS = 1e-6
IN_SIZES = (256, 256, 512, 512, 32, 512, 128, 128)
IN_COLS = 2336

kernel_name = "hybrid_gla_swa_moe_diffusion_step"

def rms_norm(x, g):
    xf = x.astype(jnp.float32)
    y = xf * lax.rsqrt(jnp.mean(xf * xf, axis=-1, keepdims=True) + EPS)
    return (y * g.astype(jnp.float32)).astype(x.dtype)

def adaln_params(cond, w_ada, b_ada):
    mod = jax.nn.silu(cond) @ w_ada + b_ada
    return [m[:, None, :] for m in jnp.split(mod, 6, axis=-1)]

def modulate(xn, shift, scale):
    return xn * (1 + scale) + shift

def split_cols(h):
    offs = np.cumsum(IN_SIZES)[:-1].tolist()
    return jnp.split(h, offs, axis=-1)

def axial_rope(x):
    t = x.shape[1]
    rows = t // GRID_W
    row = jnp.repeat(jnp.arange(rows), GRID_W)
    col = jnp.tile(jnp.arange(GRID_W), rows)
    half = SWA_HEAD_DIM // 2
    quarter = half // 2
    inv_freq = ROPE_BASE ** (-jnp.arange(quarter, dtype=jnp.float32) / quarter)

    def rot(xa, pos):
        ang = pos.astype(jnp.float32)[:, None] * inv_freq[None, :]
        cos = jnp.cos(ang)[None, :, None, :]
        sin = jnp.sin(ang)[None, :, None, :]
        x1, x2 = xa[..., :quarter], xa[..., quarter:]
        return jnp.concatenate([x1 * cos - x2 * sin, x1 * sin + x2 * cos], axis=-1)

    xf = x.astype(jnp.float32)
    out = jnp.concatenate([rot(xf[..., :half], row), rot(xf[..., half:], col)], axis=-1)
    return out.astype(x.dtype)

def sink_softmax(scores, sink, mask=None):
    if mask is not None:
        scores = jnp.where(mask, scores, -jnp.inf)
    m = jnp.maximum(jnp.max(scores, axis=-1, keepdims=True), sink)
    p = jnp.exp(scores - m)
    return p / (jnp.sum(p, axis=-1, keepdims=True) + jnp.exp(sink - m))

def gla_chunked(q, k, v, log_a, s0):
    b, t, h, dk = q.shape
    dv = v.shape[-1]
    n = t // GLA_CHUNK

    def to_chunks(z):
        return z.astype(jnp.float32).reshape(b, n, GLA_CHUNK, h, z.shape[-1]).transpose(1, 0, 3, 2, 4)

    causal = jnp.tril(jnp.ones((GLA_CHUNK, GLA_CHUNK), dtype=bool))

    def step(s, inp):
        qc, kc, vc, ac = inp
        cum = jnp.cumsum(ac, axis=2)
        o_inter = jnp.einsum('bhtk,bhkv->bhtv', qc * jnp.exp(cum), s)
        diff = cum[:, :, :, None, :] - cum[:, :, None, :, :]
        decay = jnp.exp(jnp.where(causal[None, None, :, :, None], diff, -jnp.inf))
        att = jnp.einsum('bhtk,bhsk,bhtsk->bhts', qc, kc, decay)
        o_intra = jnp.einsum('bhts,bhsv->bhtv', att, vc)
        last = cum[:, :, -1:, :]
        s_new = jnp.exp(last[:, :, 0, :, None]) * s + jnp.einsum(
            'bhsk,bhsv->bhkv', kc * jnp.exp(last - cum), vc)
        return s_new, o_inter + o_intra

    s_fin, o = lax.scan(step, s0.astype(jnp.float32),
                        (to_chunks(q), to_chunks(k), to_chunks(v), to_chunks(log_a)))
    o = o.transpose(1, 0, 3, 2, 4).reshape(b, t, h, dv)
    return o, s_fin

def gla_branch(q, k, v, g, lora, s0_f, s0_b, wa_f, ba_f, wa_b, ba_b, norm_g):
    b, t, _ = q.shape
    q = q.reshape(b, t, GLA_HEADS, GLA_DK) * (GLA_DK ** -0.5)
    k = k.reshape(b, t, GLA_HEADS, GLA_DK)
    v = v.reshape(b, t, GLA_HEADS, GLA_DV)
    lora_f, lora_b = jnp.split(lora, 2, axis=-1)

    def log_gate(z, wa, ba):
        pre = (z @ wa + ba).astype(jnp.float32)
        return (jax.nn.log_sigmoid(pre) / GLA_GATE_NORM).reshape(b, t, GLA_HEADS, GLA_DK)

    la_f = log_gate(lora_f, wa_f, ba_f)
    la_b = log_gate(lora_b, wa_b, ba_b)
    o_f, s_f = gla_chunked(q, k, v, la_f, s0_f)
    flip = lambda z: jnp.flip(z, axis=1)
    o_b, s_b = gla_chunked(flip(q), flip(k), flip(v), flip(la_b), s0_b)
    o = rms_norm(o_f + flip(o_b), norm_g)
    gate = jax.nn.silu(g.reshape(b, t, GLA_HEADS, GLA_DV).astype(jnp.float32))
    out = (o * gate).reshape(b, t, GLA_WIDTH).astype(g.dtype)
    return out, s_f.astype(v.dtype), s_b.astype(v.dtype)

def context_attention(q, k, v, sink):
    b, t = q.shape[:2]
    nb = t // ATTN_BLOCK
    qb = q.reshape(b, nb, ATTN_BLOCK, SWA_KV_HEADS, SWA_GROUP, SWA_HEAD_DIM).transpose(1, 0, 2, 3, 4, 5)
    sink_b = sink.astype(jnp.float32).reshape(SWA_KV_HEADS, SWA_GROUP)[None, :, :, None, None]
    scale = SWA_HEAD_DIM ** -0.5

    def one_block(qi):
        s = jnp.einsum('bqkgd,bskd->bkgqs', qi, k, preferred_element_type=jnp.float32) * scale
        p = sink_softmax(s, sink_b)
        return jnp.einsum('bkgqs,bskd->bqkgd', p.astype(v.dtype), v)

    o = lax.map(one_block, qb)
    return o.transpose(1, 0, 2, 3, 4, 5).reshape(b, t, SWA_WIDTH)

def latent_attention(q, k, v, k_ctx, v_ctx, sink):
    b, t = q.shape[:2]
    nb = t // ATTN_BLOCK
    lc = k_ctx.shape[1]
    qb = q.reshape(b, nb, ATTN_BLOCK, SWA_KV_HEADS, SWA_GROUP, SWA_HEAD_DIM)
    pad = ((0, 0), (ATTN_BLOCK, ATTN_BLOCK), (0, 0), (0, 0))
    kb = jnp.pad(k, pad).reshape(b, nb + 2, ATTN_BLOCK, SWA_KV_HEADS, SWA_HEAD_DIM)
    vb = jnp.pad(v, pad).reshape(b, nb + 2, ATTN_BLOCK, SWA_KV_HEADS, SWA_HEAD_DIM)
    kwin = jnp.concatenate([kb[:, :-2], kb[:, 1:-1], kb[:, 2:]], axis=2)
    vwin = jnp.concatenate([vb[:, :-2], vb[:, 1:-1], vb[:, 2:]], axis=2)
    blk = jnp.arange(nb)
    t_abs = blk[:, None] * ATTN_BLOCK + jnp.arange(ATTN_BLOCK)[None, :]
    s_abs = blk[:, None] * ATTN_BLOCK - ATTN_BLOCK + jnp.arange(3 * ATTN_BLOCK)[None, :]
    band = ((jnp.abs(t_abs[:, :, None] - s_abs[:, None, :]) <= WINDOW)
            & (s_abs[:, None, :] >= 0) & (s_abs[:, None, :] < t))
    mask = jnp.concatenate([jnp.ones((nb, ATTN_BLOCK, lc), dtype=bool), band], axis=-1)
    mask = mask[None, :, None, None, :, :]
    scale = SWA_HEAD_DIM ** -0.5
    s_ctx = jnp.einsum('bnqkgd,bskd->bnkgqs', qb, k_ctx, preferred_element_type=jnp.float32)
    s_band = jnp.einsum('bnqkgd,bnskd->bnkgqs', qb, kwin, preferred_element_type=jnp.float32)
    scores = jnp.concatenate([s_ctx, s_band], axis=-1) * scale
    sink_b = sink.astype(jnp.float32).reshape(SWA_KV_HEADS, SWA_GROUP)[None, None, :, :, None, None]
    p = sink_softmax(scores, sink_b, mask).astype(v.dtype)
    o = (jnp.einsum('bnkgqs,bskd->bnqkgd', p[..., :lc], v_ctx)
         + jnp.einsum('bnkgqs,bnskd->bnqkgd', p[..., lc:], vwin))
    return o.reshape(b, t, SWA_WIDTH)

def moe(x, router_w, router_bias, wg, wu, wd, swg, swu, swd):
    b, t, d = x.shape
    xt = x.reshape(b * t, d)
    scores = jax.nn.sigmoid((xt @ router_w).astype(jnp.float32))
    sel = scores + router_bias.astype(jnp.float32)
    grouped = sel.reshape(b * t, N_EXPERT_GROUPS, N_EXPERTS // N_EXPERT_GROUPS)
    group_score = jnp.sum(lax.top_k(grouped, 2)[0], axis=-1)
    _, top_groups = lax.top_k(group_score, TOPK_GROUPS)
    gmask = jnp.any(top_groups[..., None] == jnp.arange(N_EXPERT_GROUPS), axis=-2)
    emask = jnp.repeat(gmask, N_EXPERTS // N_EXPERT_GROUPS, axis=-1)
    _, idx = lax.top_k(jnp.where(emask, sel, -jnp.inf), TOP_K)
    w = jnp.take_along_axis(scores, idx, axis=-1)
    w = w / jnp.sum(w, axis=-1, keepdims=True) * ROUTED_SCALE
    gates = jnp.sum((idx[..., None] == jnp.arange(N_EXPERTS)).astype(jnp.float32) * w[..., None], axis=-2)
    h = jax.nn.silu(jnp.einsum('td,edf->tef', xt, wg)) * jnp.einsum('td,edf->tef', xt, wu)
    routed = jnp.einsum('tef,efd->td', h * gates[..., None].astype(h.dtype), wd)
    shared = (jax.nn.silu(xt @ swg) * (xt @ swu)) @ swd
    return (routed + shared).reshape(b, t, d)

def setup_inputs(seed: int = 0) -> dict:
    key = jax.random.key(seed)
    ks = jax.random.split(key, 32)
    L, D = DEPTH, D_MODEL

    def nrm(k, shape, scale):
        return jax.random.normal(k, shape, jnp.float32) * scale

    return {
        "x_prompt": nrm(ks[0], (BATCH, SEQ, D), 1.0),
        "x_sample": nrm(ks[1], (DEC_BATCH, DEC_SEQ, D), 1.0),
        "c": nrm(ks[2], (DEC_BATCH, D), 1.0),
        "cache_swa_k": nrm(ks[3], (DEC_BATCH, L, PAST_LEN, SWA_KV_HEADS, SWA_HEAD_DIM), 1.0),
        "cache_swa_v": nrm(ks[4], (DEC_BATCH, L, PAST_LEN, SWA_KV_HEADS, SWA_HEAD_DIM), 1.0),
        "state_gla_fwd": nrm(ks[5], (DEC_BATCH, L, GLA_HEADS, GLA_DK, GLA_DV), 0.5),
        "state_gla_bwd": nrm(ks[6], (DEC_BATCH, L, GLA_HEADS, GLA_DK, GLA_DV), 0.5),
        "c_ctx": nrm(ks[7], (D,), 1.0),
        "w_ada": nrm(ks[8], (L, D, 6 * D), 0.5 * D ** -0.5),
        "b_ada": nrm(ks[9], (L, 6 * D), 0.02),
        "norm_attn_g": 1.0 + nrm(ks[10], (L, D), 0.05),
        "norm_ffn_g": 1.0 + nrm(ks[11], (L, D), 0.05),
        "w_in": nrm(ks[12], (L, D, IN_COLS), D ** -0.5),
        "gla_wa_f": nrm(ks[13], (L, GLA_LORA, GLA_HEADS * GLA_DK), GLA_LORA ** -0.5),
        "gla_ba_f": nrm(ks[14], (L, GLA_HEADS * GLA_DK), 0.1),
        "gla_wa_b": nrm(ks[15], (L, GLA_LORA, GLA_HEADS * GLA_DK), GLA_LORA ** -0.5),
        "gla_ba_b": nrm(ks[16], (L, GLA_HEADS * GLA_DK), 0.1),
        "gla_norm_g": 1.0 + nrm(ks[17], (L, GLA_DV), 0.05),
        "swa_sink": nrm(ks[18], (L, SWA_HEADS), 0.5),
        "w_out": nrm(ks[19], (L, MIX_W, D), MIX_W ** -0.5),
        "router_w": nrm(ks[20], (L, D, N_EXPERTS), D ** -0.5),
        "router_bias": nrm(ks[21], (L, N_EXPERTS), 0.01),
        "exp_w_gate": nrm(ks[22], (L, N_EXPERTS, D, EXPERT_FF), D ** -0.5),
        "exp_w_up": nrm(ks[23], (L, N_EXPERTS, D, EXPERT_FF), D ** -0.5),
        "exp_w_down": nrm(ks[24], (L, N_EXPERTS, EXPERT_FF, D), EXPERT_FF ** -0.5),
        "sh_w_gate": nrm(ks[25], (L, D, SHARED_FF), D ** -0.5),
        "sh_w_up": nrm(ks[26], (L, D, SHARED_FF), D ** -0.5),
        "sh_w_down": nrm(ks[27], (L, SHARED_FF, D), SHARED_FF ** -0.5),
        "final_norm_g": 1.0 + nrm(ks[28], (D,), 0.05),
    }

def reference(x_prompt, x_sample, c, cache_swa_k, cache_swa_v, state_gla_fwd, state_gla_bwd,
              c_ctx, w_ada, b_ada, norm_attn_g, norm_ffn_g, w_in, gla_wa_f, gla_ba_f,
              gla_wa_b, gla_ba_b, gla_norm_g, swa_sink, w_out, router_w, router_bias,
              exp_w_gate, exp_w_up, exp_w_down, sh_w_gate, sh_w_up, sh_w_down, final_norm_g):
    xc = x_prompt
    xl = x_sample
    new_k, new_v, new_sf, new_sb = [], [], [], []
    for l in range(DEPTH):
        gla_p = (gla_wa_f[l], gla_ba_f[l], gla_wa_b[l], gla_ba_b[l], gla_norm_g[l])
        moe_p = (router_w[l], router_bias[l], exp_w_gate[l], exp_w_up[l], exp_w_down[l],
                 sh_w_gate[l], sh_w_up[l], sh_w_down[l])

        b, t, _ = xc.shape
        sh1, sc1, g1, sh2, sc2, g2 = adaln_params(c_ctx[None, :], w_ada[l], b_ada[l])
        h = modulate(rms_norm(xc, norm_attn_g[l]), sh1, sc1)
        q_g, k_g, v_g, g_g, lora, q_s, k_s, v_s = split_cols(h @ w_in[l])
        s_zero = jnp.zeros((b, GLA_HEADS, GLA_DK, GLA_DV), jnp.float32)
        gla_out, s_f, s_b = gla_branch(q_g, k_g, v_g, g_g, lora, s_zero, s_zero, *gla_p)
        kc = k_s.reshape(b, t, SWA_KV_HEADS, SWA_HEAD_DIM)
        vc = v_s.reshape(b, t, SWA_KV_HEADS, SWA_HEAD_DIM)
        attn_out = context_attention(q_s.reshape(b, t, SWA_HEADS, SWA_HEAD_DIM), kc, vc, swa_sink[l])
        xc = xc + g1 * (jnp.concatenate([gla_out, attn_out], axis=-1) @ w_out[l])
        xc = xc + g2 * moe(modulate(rms_norm(xc, norm_ffn_g[l]), sh2, sc2), *moe_p)
        new_k.append(kc)
        new_v.append(vc)
        new_sf.append(s_f)
        new_sb.append(s_b)

        b, t, _ = xl.shape
        sh1, sc1, g1, sh2, sc2, g2 = adaln_params(c, w_ada[l], b_ada[l])
        h = modulate(rms_norm(xl, norm_attn_g[l]), sh1, sc1)
        q_g, k_g, v_g, g_g, lora, q_s, k_s, v_s = split_cols(h @ w_in[l])
        gla_out, _, _ = gla_branch(q_g, k_g, v_g, g_g, lora,
                                   state_gla_fwd[:, l], state_gla_bwd[:, l], *gla_p)
        ql = axial_rope(q_s.reshape(b, t, SWA_HEADS, SWA_HEAD_DIM))
        kl = axial_rope(k_s.reshape(b, t, SWA_KV_HEADS, SWA_HEAD_DIM))
        vl = v_s.reshape(b, t, SWA_KV_HEADS, SWA_HEAD_DIM)
        attn_out = latent_attention(ql, kl, vl, cache_swa_k[:, l], cache_swa_v[:, l], swa_sink[l])
        xl = xl + g1 * (jnp.concatenate([gla_out, attn_out], axis=-1) @ w_out[l])
        xl = xl + g2 * moe(modulate(rms_norm(xl, norm_ffn_g[l]), sh2, sc2), *moe_p)

    y_prompt = rms_norm(xc, final_norm_g)
    y_sample = rms_norm(xl, final_norm_g)
    new_cache_swa_k = jnp.stack(new_k, axis=1)
    new_cache_swa_v = jnp.stack(new_v, axis=1)
    new_state_gla_fwd = jnp.stack(new_sf, axis=1)
    new_state_gla_bwd = jnp.stack(new_sb, axis=1)
    return (y_prompt, y_sample, new_cache_swa_k, new_cache_swa_v, new_state_gla_fwd, new_state_gla_bwd)


_drawn_inputs = setup_inputs


def setup_inputs(seed=0):
    import zlib

    import numpy as np

    out = dict(_drawn_inputs(seed))
    spreads = {}
    factors = {'state_gla_fwd': 8.0, 'state_gla_bwd': 8.0, 'gla_norm_g': 2.678, 'swa_sink': 8.0}
    for name, (base, spread) in spreads.items():
        noise = np.random.default_rng([zlib.crc32(name.encode()), seed]).standard_normal(out[name].shape)
        drawn = base * np.exp(spread * noise) if base else spread * noise
        out[name] = jnp.asarray(drawn.astype(out[name].dtype))
    for name, factor in factors.items():
        out[name] = (out[name] * factor).astype(out[name].dtype)
    return out
```

```python
from contextlib import ExitStack

import concourse.bass as bass
from concourse import mybir

F32 = mybir.dt.float32
BF16 = mybir.dt.bfloat16
I32 = mybir.dt.int32
U8 = mybir.dt.uint8
ALU = mybir.AluOpType
ACT = mybir.ActivationFunctionType
AX = mybir.AxisListType

P = 128
D = 1024
KD = D // P
NT = 9
T = NT * P
EPS = 1e-6
HEADS = 4
DK, DV = 64, 128
FF = 128
NE = 64
TOPK = 8

C_QK, C_VG, C_GG, C_LORA, C_QS, C_KV = (0, 512), (512, 512), (1024, 512), (1536, 32), (1568, 512), (2080, 256)

V_CTX, V_C, V_NA, V_NF, V_BADA, V_BAF, V_BAB, V_ROWS = 0, 8, 16, 24, 32, 80, 82, 84


def cond_of(t):
    return 0 if t == 0 else 1


def project(nc, dram, keep):
    with ExitStack() as ctx:
        def sb(name, shape, dt=F32):
            return ctx.enter_context(nc.sbuf_tensor(name, shape, dt))

        def sem(name):
            return nc.alloc_semaphore(name)

        RING = 3
        vec = sb("vec", [V_ROWS, P])
        condT = sb("condT", [P, KD, 2])
        modA1 = sb("modA1", [P, KD, 2])
        ring = [sb(f"wring{i}", [P, KD, 512]) for i in range(RING)]
        NX = 3
        xin = sb("xin", [P, NX, D])
        xn = sb("xn", [P, 2, D])
        junk = sb("junk", [P, D])
        ssq = sb("ssq", [P, NT])
        std = sb("std", [P, NT])
        rstd = sb("rstd", [P, NT])
        hT = sb("hT", [P, KD, T])
        psA = ctx.enter_context(nc.psum_tensor("psA", [P, 512], F32))
        psT = ctx.enter_context(nc.psum_tensor("psT", [P, 2, D], F32))
        NB = 3
        psP = ctx.enter_context(nc.psum_tensor("psP", [P, NB, 512], F32))
        modps = psA[:, 0:96].rearrange("p (c k) -> p c k", k=2)
        vecps = psA[:, 128:128 + V_ROWS]

        vec_in, ident_in, x_in = sem("vec_in"), sem("ident_in"), [sem(f"x_in{i}") for i in range(NX)]
        ring_in = [sem(f"ring_in{i}") for i in range(RING)]
        ada_done = sem("ada_done")
        vecT_done, vec_cols, cond_done = sem("vecT_done"), sem("vec_cols"), sem("cond_done")
        modA_done, mod_cols = sem("modA_done"), sem("mod_cols")
        ssq_done, std_done, rstd_done, xn_done = sem("ssq_done"), sem("std_done"), sem("rstd_done"), sem("xn_done")
        xT_done, hT_act, hT_dve = sem("xT_done"), sem("hT_act"), sem("hT_dve")
        proj_done, evac_act, evac_dve = sem("proj_done"), sem("evac_act"), sem("evac_dve")
        out_done = sem("kv_out_done")

        w_ada = dram["w_ada"].rearrange("(j p) n -> p j n", p=P)
        w_in = dram["w_in"].rearrange("(j p) n -> p j n", p=P)
        items = [("ada", i) for i in range(4)]
        items += [("qk", C_QK), ("lora", C_LORA), ("vg", C_VG), ("gg", C_GG), ("qs", C_QS), ("kv", C_KV)]
        items += [("ada", i) for i in range(4, 12)]

        def landed(eng, n):
            eng.wait_ge(ring_in[n % RING], 16 * (n // RING + 1))

        outs = []
        for kind, what in items:
            if kind in ("qk", "lora"):
                for m in range(4 if kind == "qk" else 1):
                    for g in range(3):
                        outs.append((kind, m, g))
            elif kind != "ada":
                for t in range(NT):
                    outs.append((kind, 0, t))

        def used(eng, n):
            if items[n][0] == "ada":
                eng.wait_ge(ada_done, items[n][1] + 1)
            else:
                eng.wait_ge(proj_done, max(k for k, o in enumerate(outs) if o[0] == items[n][0]) + 1)

        def dest(kind, m, t):
            if kind == "qk":
                return keep["qkT"][:, m, t * 384:(t + 1) * 384]
            if kind == "lora":
                return keep["loraT"][:, t * 384:(t + 1) * 384]
            if kind == "qs":
                return keep["qs"][:, t, :].rearrange("p (r g d) -> p g r d", r=4, g=2)
            return keep[kind][:, t, :]

        def source(kind, k):
            if kind == "lora":
                return psP[0:32, k % NB, 0:384]
            if kind == "qs":
                return psP[:, k % NB, :].rearrange("p (g r d) -> p g r d", r=4, g=2)
            return psP[:, k % NB, 0:{"qk": 384, "kv": 256}.get(kind, 512)]

        def by_act(k):
            return outs[k][0] == "gg" or k % 2 == 0

        def evacs_before(k, act):
            return sum(1 for i in range(k) if by_act(i) == act)

        block = ctx.enter_context(nc.Block())

        @block.sync
        def _(sp):
            for n, (kind, what) in enumerate(items):
                if n == 0:
                    sp.dma_start(vec[:], dram["vectors"]).then_inc(vec_in, 16)
                    sp.dma_start(keep["ident"][:], dram["ident"]).then_inc(ident_in, 16)
                if n >= RING:
                    used(sp, n - RING)
                c0, cn = (what * 512, 512) if kind == "ada" else what
                src = w_ada if kind == "ada" else w_in
                sp.dma_start(ring[n % RING][:, :, 0:cn], src[:, :, c0:c0 + cn]).then_inc(ring_in[n % RING], 16)
                if n == 1:
                    for t in range(NX):
                        sp.dma_start(xin[:, t, :], dram["x"](t)).then_inc(x_in[t], 16)
                if n == 3:
                    for t in range(NX, NT):
                        sp.wait_ge(xn_done, t - NX + 1)
                        sp.dma_start(xin[:, t % NX, :], dram["x"](t)).then_inc(x_in[t % NX], 16)
            kv0 = outs.index(("kv", 0, 0))
            sp.wait_ge(evac_act if by_act(kv0) else evac_dve, evacs_before(kv0 + 1, by_act(kv0)))
            sp.dma_start(dram["new_k"], keep["kv"][:, 0, 0:128]).then_inc(out_done, 16)
            sp.dma_start(dram["new_v"], keep["kv"][:, 0, 128:256]).then_inc(out_done, 16)
            sp.wait_ge(out_done, 32)

        @block.tensor
        def _(pe):
            pe.wait_ge(vec_in, 16)
            pe.wait_ge(ident_in, 16)
            pe.transpose(vecps, vec[:], keep["ident"][0:V_ROWS, 0:V_ROWS]).then_inc(vecT_done, 1)

            def ada(n, i):
                landed(pe, n)
                for c in range(4):
                    for j in range(KD):
                        last = pe.matmul(modps[:, 4 * i + c, :], ring[n % RING][:, j, c * P:(c + 1) * P],
                                         condT[:, j, :], start=(j == 0), stop=(j == KD - 1))
                last.then_inc(ada_done, 1)

            def xT(t):
                pe.wait_ge(xn_done, t + 1)
                if t >= 2:
                    pe.wait_ge(hT_act, t - 1)
                    pe.wait_ge(hT_dve, t - 1)
                for j in range(KD):
                    last = pe.transpose(psT[:, t % 2, j * P:(j + 1) * P], xn[:, t % 2, j * P:(j + 1) * P], keep["ident"][:])
                last.then_inc(xT_done, 1)

            k = 0
            for n, (kind, what) in enumerate(items):
                if kind == "ada":
                    if n == 0:
                        pe.wait_ge(cond_done, 1)
                    ada(n, what)
                    if n == 3:
                        for t in range(NT):
                            xT(t)
                    continue
                landed(pe, n)
                if kind == "qk":
                    pe.wait_ge(hT_act, NT)
                    pe.wait_ge(hT_dve, NT)
                w = ring[n % RING]
                for kk in range(k, len(outs)):
                    if outs[kk][0] != kind:
                        break
                    _, m, t = outs[kk]
                    if kk >= NB:
                        a = by_act(kk - NB)
                        pe.wait_ge(evac_act if a else evac_dve, evacs_before(kk - NB + 1, a))
                    for j in range(KD):
                        bank = psP[:, kk % NB, 0:512] if kind == "qs" else source(kind, kk)
                        if kind in ("qk", "lora"):
                            width = P if kind == "qk" else 32
                            last = pe.matmul(bank, w[:, j, m * P:m * P + width],
                                             hT[:, j, t * 384:(t + 1) * 384], start=(j == 0), stop=(j == KD - 1))
                        else:
                            last = pe.matmul(bank, hT[:, j, t * P:(t + 1) * P],
                                             w[:, j, 0:what[1]], start=(j == 0), stop=(j == KD - 1))
                    last.then_inc(proj_done, 1)
                    k = kk + 1

        def scale_of(kind, m):
            return DK ** -0.5 if kind == "qk" and m < 2 else 1.0

        def hT_half(act, t):
            act.wait_ge(xT_done, t + 1)
            if t == 0:
                act.wait_ge(modA_done, 1)
            c = cond_of(t)
            for j in range(4, KD):
                last = act.activation(hT[:, j, t * P:(t + 1) * P], psT[:, t % 2, j * P:(j + 1) * P], ACT.Identity,
                                      scale=modA1[:, j, c:c + 1], bias=keep["mod"][:, j, c:c + 1])
            last.then_inc(hT_act, 1)

        @block.scalar
        def _(act):
            act.wait_ge(vec_cols, 2)
            act.activation(condT[:].rearrange("p j k -> p k j"),
                           keep["vcol"][:, 0:16].rearrange("p (k j) -> p k j", k=2), ACT.Silu).then_inc(cond_done, 1)
            for t in range(NT):
                act.wait_ge(x_in[t % NX], 16 * (t // NX + 1))
                if t >= 1:
                    act.wait_ge(ssq_done, t)
                act.activation(junk[:], xin[:, t % NX, :], ACT.Square, accum_out=ssq[:, t:t + 1]).then_inc(ssq_done, 1)
                act.wait_ge(ssq_done, t + 1)
                act.activation(std[:, t:t + 1], ssq[:, t:t + 1], ACT.Sqrt, scale=1.0 / D,
                               bias=keep["eps"][:]).then_inc(std_done, 1)
                if t >= 2:
                    hT_half(act, t - 2)
            hT_half(act, NT - 2)
            hT_half(act, NT - 1)
            for k, (kind, m, t) in enumerate(outs):
                if by_act(k):
                    act.wait_ge(proj_done, k + 1)
                    act.activation(dest(kind, m, t), source(kind, k), ACT.Silu if kind == "gg" else ACT.Copy,
                                   scale=scale_of(kind, m)).then_inc(evac_act, 1)

        @block.vector
        def _(dve):
            dve.memset(keep["eps"][:], EPS).then_inc(vec_cols, 1)
            dve.wait_ge(vecT_done, 1)
            dve.tensor_copy(keep["vcol"][:], vecps).then_inc(vec_cols, 1)

            def norm(t):
                dve.wait_ge(std_done, t + 1)
                dve.reciprocal(rstd[:, t:t + 1], std[:, t:t + 1]).then_inc(rstd_done, 1)
                dve.wait_ge(rstd_done, t + 1)
                if t >= 2:
                    dve.wait_ge(xT_done, t - 1)
                dve.tensor_scalar(xn[:, t % 2, :], xin[:, t % NX, :], rstd[:, t:t + 1], None, ALU.mult).then_inc(xn_done, 1)

            def hT_low(t):
                dve.wait_ge(xT_done, t + 1)
                c = cond_of(t)
                for j in range(4):
                    last = dve.tensor_scalar(hT[:, j, t * P:(t + 1) * P], psT[:, t % 2, j * P:(j + 1) * P],
                                             modA1[:, j, c:c + 1], keep["mod"][:, j, c:c + 1], ALU.mult, ALU.add)
                last.then_inc(hT_dve, 1)

            norm(0)
            norm(1)
            dve.wait_ge(ada_done, 4)
            dve.wait_ge(vec_cols, 2)
            bada = keep["vcol"][:, V_BADA:V_BADA + 48]
            dve.tensor_tensor(keep["mod"][:, 0:16, :], modps[:, 0:16, :],
                              bada[:, 0:16].unsqueeze(2).to_broadcast([P, 16, 2]), ALU.add).then_inc(mod_cols, 1)
            dve.wait_ge(mod_cols, 1)
            dve.scalar_tensor_tensor(out=modA1[:], in0=keep["mod"][:, 8:16, :], scalar=1.0,
                                     in1=keep["vcol"][:, V_NA:V_NA + 8].unsqueeze(2).to_broadcast([P, KD, 2]),
                                     op0=ALU.add, op1=ALU.mult).then_inc(modA_done, 1)
            dve.wait_ge(modA_done, 1)
            for t in range(2, NT):
                norm(t)
                hT_low(t - 2)
            hT_low(NT - 2)
            hT_low(NT - 1)
            for k, (kind, m, t) in enumerate(outs):
                if not by_act(k):
                    dve.wait_ge(proj_done, k + 1)
                    dve.tensor_scalar(dest(kind, m, t), source(kind, k), scale_of(kind, m), None,
                                      ALU.mult).then_inc(evac_dve, 1)
            dve.wait_ge(ada_done, 12)
            dve.tensor_tensor(keep["mod"][:, 16:48, :], modps[:, 16:48, :],
                              bada[:, 16:48].unsqueeze(2).to_broadcast([P, 32, 2]), ALU.add).then_inc(mod_cols, 1)


def linear_attention(nc, dram, keep):
    with ExitStack() as ctx:
        def sb(name, shape, dt=F32):
            return ctx.enter_context(nc.sbuf_tensor(name, shape, dt))

        def ps(name, shape):
            return ctx.enter_context(nc.psum_tensor(name, shape, F32))

        def sem(name):
            return nc.alloc_semaphore(name)

        G = 3
        W = G * P
        NG = NT // G
        UNITS = [(g, m) for g in range(NG) for m in range(4)]
        NU = len(UNITS)
        CAP = 80.0 * 16.0

        wab = sb("wab", [32, 512])
        restart = sb("restart", [P, W])
        mask = sb("gla_mask", [P, 2, P], I32)
        normg = sb("normg", [P, P])
        ab = sb("ab", [P, W])
        ex = lg = ab
        mn = sb("mn", [P, W])
        la = sb("la", [P, W])
        tmp = sb("tmp", [P, W])
        cum = sb("cum", [P, 2, W])
        dif = sb("dif", [P, 5, W])
        fac = [sb(f"fac{i}", [P, 7, W]) for i in range(2)]
        (F64, F32L, F16, FQD, FKD, FQI, FKS) = range(7)
        pr = [sb(f"pr{i}", [P, 4, W]) for i in range(2)]
        kz = [sb(f"kz{i}", [P, 3, W]) for i in range(2)]
        ksT = [sb(f"ksT{i}", [P, W]) for i in range(2)]
        ks = [sb(f"ks{i}", [P, G, P]) for i in range(2)]
        qi = sb("qi", [P, 4, T])
        elast = sb("elast", [P, 4, NT])
        AT = [sb(f"AT{m}", [P, G, 2, P]) for m in range(4)]
        S = sb("S", [P, 4, NT, P])
        S0 = sb("S0", [P, 4, P])
        osum = [AT[i][:].rearrange("p i h t -> p (i h t)")[:, 0:512] for i in range(2)]
        sq = AT[2][:].rearrange("p i h t -> p (i h t)")[:, 0:512]
        ms = sb("gla_ms", [P, NT, 4])
        lnm = sb("gla_lnm", [P, NT, 4])
        rs = sb("gla_rs", [P, NT, 4])

        ps_pre = ps("ps_pre", [P, 512])
        ps_a = [ps(f"ps_a{i}", [P, 2, 512]) for i in range(2)]
        ps_t = ps("ps_kt", [P, 512])
        ps_d = ps("ps_d", [P, 512])
        ps_o = ps("ps_o", [P, 512])
        ps_i = [ps_a[i][:, :, 0:2 * DV].rearrange("p h (m v) -> p h m v", v=DV) for i in range(2)]

        const_in, zeroed = sem("gla_const_in"), sem("gla_zeroed")
        pre_done, soft_done, cum_done, dif_done = sem("pre_done"), sem("soft_done"), sem("cum_done"), sem("dif_done")
        act_step, dve_step = sem("gla_act_step"), sem("gla_dve_step")
        fac_done, prod_done = sem("fac_done"), sem("prod_done")
        score_done, kst_done, at_done, ks_done = sem("score_done"), sem("kst_done"), sem("at_done"), sem("ks_done")
        delta_done, s_done, pv_done, intra_done = sem("delta_done"), sem("s_done"), sem("pv_done"), sem("intra_done")
        rec_done, inter_done, osum_done = sem("rec_done"), sem("inter_done"), sem("osum_done")
        sq_done, rs_done, gate_done, out_ready, gla_done = sem("sq_done"), sem("rs_done"), sem("gate_done"), sem("out_ready"), sem("gla_done")
        state_out = sem("state_out")

        def halves(ap, b):
            v = ap.rearrange("p (n h b) -> p n h b", h=2, b=b)
            return v[:, :, 0, :], v[:, :, 1, :]

        def sides(ap, b, m):
            lo, hi = halves(ap, b)
            return (hi, lo) if m < 2 else (lo, hi)

        block = ctx.enter_context(nc.Block())

        @block.sync
        def _(sp):
            sp.wait_ge(zeroed, 1)
            sp.dma_start(wab[0:16, 0:256], dram["gla_wa_f"]).then_inc(const_in, 16)
            sp.dma_start(wab[16:32, 256:512], dram["gla_wa_b"]).then_inc(const_in, 16)
            sp.dma_start(mask[:], dram["gla_mask"]).then_inc(const_in, 16)
            sp.dma_start(normg[:], dram["gla_norm_g"].to_broadcast([P, P])).then_inc(const_in, 16)
            sp.dma_start(S0[:, 0:2, :], dram["state_f"].rearrange("(m p) v -> p m v", p=P)).then_inc(const_in, 16)
            sp.dma_start(S0[:, 2:4, :], dram["state_b"].rearrange("(m p) v -> p m v", p=P)).then_inc(const_in, 16)
            sp.wait_ge(s_done, 4)
            sp.dma_start(dram["new_f"].rearrange("(m p) v -> p m v", p=P), S[:, 0:2, 0, :]).then_inc(state_out, 16)
            sp.dma_start(dram["new_b"].rearrange("(m p) v -> p m v", p=P), S[:, 2:4, 0, :]).then_inc(state_out, 16)
            sp.wait_ge(state_out, 32)

        @block.tensor
        def _(pe):
            def pre(u):
                g, m = UNITS[u]
                if u >= 1:
                    pe.wait_ge(soft_done, u)
                    pe.wait_ge(cum_done, u)
                else:
                    pe.wait_ge(const_in, 96)
                pe.matmul(ps_pre[:, 0:W], wab[:, m * P:(m + 1) * P], keep["loraT"][:, g * W:(g + 1) * W],
                          start=True, stop=True).then_inc(pre_done, 1)

            def scores(u):
                g, m = UNITS[u]
                b = u % 2
                pe.wait_ge(prod_done, u + 1)
                if u >= 2:
                    pe.wait_ge(at_done, u - 1)
                z = kz[m // 2]
                for i in range(G):
                    for h in range(2):
                        rows = slice(DK * h, DK * h + DK)
                        tile = slice(i * P, (i + 1) * P)
                        out = ps_a[b][:, h, i * P:(i + 1) * P]
                        oq, ok = sides(out, 16, m)
                        qd = pr[b][rows, 3, tile]
                        qdq, qdk = sides(qd, 16, m)
                        q16, _ = sides(pr[b][rows, 2, tile], 16, m)
                        pe.matmul(ok, z[rows, 0, tile], qdk, start=True, stop=True)
                        pe.matmul(oq, z[rows, 1, tile], qdq, start=True, stop=False)
                        pe.matmul(oq, z[rows, 2, tile], q16, start=False, stop=True)
                        for lv, size in ((1, 32), (0, 64)):
                            for n in range(P // (2 * size)):
                                lo = slice(2 * size * n, 2 * size * n + size)
                                hi = slice(2 * size * n + size, 2 * size * (n + 1))
                                q, k = (hi, lo) if m < 2 else (lo, hi)
                                w = pr[b][rows, lv, tile]
                                last = pe.matmul(out[k, q], w[:, k], w[:, q], start=True, stop=True)
                last.then_inc(score_done, 1)

            def turn_keys(u):
                b = u % 2
                if u >= 1:
                    pe.wait_ge(ks_done, u)
                for i in range(G):
                    last = pe.transpose(ps_t[:, i * P:(i + 1) * P], ksT[b][:, i * P:(i + 1) * P], keep["ident"][:])
                last.then_inc(kst_done, 1)

            def delta(u):
                g, m = UNITS[u]
                pe.wait_ge(ks_done, u + 1)
                if u >= 1:
                    pe.wait_ge(s_done, u)
                for i in range(G):
                    for h in range(2):
                        head = 2 * (m % 2) + h
                        last = pe.matmul(ps_d[DK * h:DK * h + DK, i * P:(i + 1) * P], ks[u % 2][:, i, DK * h:DK * h + DK],
                                         keep["vg"][:, g * G + i, head * DV:(head + 1) * DV], start=True, stop=True)
                last.then_inc(delta_done, 1)

            def intra(g):
                pe.wait_ge(at_done, 4 * g + 4)
                for i in range(G):
                    t = g * G + i
                    if t >= 1:
                        pe.wait_ge(intra_done, t)
                    for head in range(HEADS):
                        for d in range(2):
                            last = pe.matmul(ps_o[:, head * DV:(head + 1) * DV], AT[2 * d + head // 2][:, i, head % 2, :],
                                             keep["vg"][:, t, head * DV:(head + 1) * DV], start=(d == 0), stop=(d == 1))
                    last.then_inc(pv_done, 1)

            pre(0)
            for u in range(NU + 1):
                if u + 1 < NU:
                    pre(u + 1)
                if u < NU:
                    scores(u)
                    turn_keys(u)
                if u >= 1:
                    delta(u - 1)
                    if UNITS[u - 1][1] == 3:
                        intra(UNITS[u - 1][0])
            for n, t in enumerate(range(1, NT)):
                pe.wait_ge(rec_done, 29)
                if n >= 2:
                    pe.wait_ge(osum_done, n - 1)
                for head in range(HEADS):
                    rows = slice(DK * (head % 2), DK * (head % 2) + DK)
                    for d in range(2):
                        m = 2 * d + head // 2
                        edge = t == (1, NT - 1)[d]
                        st = S0[rows, m, :] if edge else S[rows, m, t + (-1, 1)[d], :]
                        last = pe.matmul(ps_i[n % 2][:, head % 2, head // 2, :], qi[rows, m, t * P:(t + 1) * P], st,
                                         start=(d == 0), stop=(d == 1))
                last.then_inc(inter_done, 1)

        @block.scalar
        def _(act):
            nc.scalar.preload_act_table_set("natural_log_exp_and_others")
            steps = [0]

            def step(ins):
                steps[0] += 1
                ins.then_inc(act_step, 1)
                act.wait_ge(act_step, steps[0])

            def soft(u):
                g, m = UNITS[u]
                ba = keep["vcol"][:, V_BAF + m:V_BAF + m + 1]
                act.wait_ge(pre_done, u + 1)
                if u >= 1:
                    act.wait_ge(cum_done, u)
                step(act.activation(ab[:], ps_pre[:, 0:W], ACT.Abs, bias=ba))
                step(act.activation(ex[:], ab[:], ACT.Exp, scale=-1.0))
                act.activation(lg[:], ex[:], ACT.Ln, bias=1.0).then_inc(soft_done, 1)

            def factors(u):
                g, m = UNITS[u]
                b = u % 2
                act.wait_ge(dif_done, u + 1)
                if u >= 2:
                    act.wait_ge(prod_done, u - 1)
                c = 1.0 / 16.0
                for f, lv, size in ((F64, 0, 64), (F32L, 1, 32), (F16, 2, 16)):
                    dq, dk = sides(dif[:, lv, :], size, m)
                    fq, fk = sides(fac[b][:, f, :], size, m)
                    act.activation(fq, dq, ACT.Exp, scale=c)
                    act.activation(fk, dk, ACT.Exp, scale=-c)
                act.activation(fac[b][:, FQD, :], dif[:, 3, :], ACT.Exp, scale=c)
                act.activation(fac[b][:, FKD, :], dif[:, 3, :], ACT.Exp, scale=-c)
                act.activation(fac[b][:, FQI, :], cum[:, b, :], ACT.Exp, scale=c)
                act.activation(fac[b][:, FKS, :], dif[:, 4, :], ACT.Exp, scale=c)
                end = cum[:, b, :].rearrange("p (n b) -> p n b", b=P)[:, :, (P - 1 if m < 2 else 0)]
                act.activation(elast[:, m, g * G:(g + 1) * G], end, ACT.Exp, scale=c).then_inc(fac_done, 1)

            def move_keys(u):
                act.wait_ge(kst_done, u + 1)
                if u >= 2:
                    act.wait_ge(delta_done, u - 1)
                act.activation(ks[u % 2][:].rearrange("p i k -> p (i k)"), ps_t[:, 0:W], ACT.Copy).then_inc(ks_done, 1)

            soft(0)
            for u in range(NU + 1):
                if u < NU:
                    factors(u)
                if u + 1 < NU:
                    soft(u + 1)
                if u >= 1:
                    move_keys(u - 1)
            act.wait_ge(pv_done, NT)
            for t in range(NT):
                src = keep["vg"][:, t, :] if t == 0 else osum[t % 2]
                act.wait_ge(intra_done if t == 0 else osum_done, 1 if t == 0 else t)
                for head in range(HEADS):
                    step(act.activation(sq[:, head * DV:(head + 1) * DV], src[:, head * DV:(head + 1) * DV], ACT.Square,
                                        accum_out=ms[:, t, head:head + 1]))
                step(act.activation(lnm[:, t, :], ms[:, t, :], ACT.Ln, scale=1.0 / DV, bias=keep["eps"][:]))
                act.activation(rs[:, t, :], lnm[:, t, :], ACT.Exp, scale=-0.5).then_inc(rs_done, 1)

        @block.gpsimd
        def _(pool):
            pool.memset(wab[:], 0.0).then_inc(zeroed, 1)
            pool.memset(kz[0][:], 0.0).then_inc(zeroed, 1)
            pool.memset(kz[1][:], 0.0).then_inc(zeroed, 1)
            pool.wait_ge(zeroed, 3)
            for u, (g, m) in enumerate(UNITS):
                b = u % 2
                q = keep["qkT"][:, m % 2, g * W:(g + 1) * W]
                k = keep["qkT"][:, 2 + m % 2, g * W:(g + 1) * W]
                z = kz[m // 2]
                pool.wait_ge(fac_done, u + 1)
                if u >= 2:
                    pool.wait_ge(kst_done, u - 1)
                if u >= 1 and m % 2 == 1:
                    pool.wait_ge(score_done, u)
                for lv, f, size in ((0, F64, 64), (1, F32L, 32)):
                    for src, wq in ((q, 0), (k, 1)):
                        pool.tensor_tensor(sides(pr[b][:, lv, :], size, m)[wq], sides(src, size, m)[wq],
                                           sides(fac[b][:, f, :], size, m)[wq], ALU.mult)
                pool.tensor_tensor(sides(pr[b][:, 2, :], 16, m)[0], sides(q, 16, m)[0], sides(fac[b][:, F16, :], 16, m)[0], ALU.mult)
                pool.tensor_tensor(pr[b][:, 3, :], q, fac[b][:, FQD, :], ALU.mult)
                pool.tensor_tensor(sides(z[:, 0, :], 16, m)[1], sides(k, 16, m)[1], sides(fac[b][:, FKD, :], 16, m)[1], ALU.mult)
                pool.tensor_tensor(sides(z[:, 1, :], 16, m)[0], sides(k, 16, m)[0], sides(fac[b][:, FKD, :], 16, m)[0], ALU.mult)
                pool.tensor_tensor(sides(z[:, 2, :], 16, m)[1], sides(k, 16, m)[1], sides(fac[b][:, F16, :], 16, m)[1], ALU.mult)
                pool.tensor_tensor(qi[:, m, g * W:(g + 1) * W], q, fac[b][:, FQI, :], ALU.mult)
                pool.tensor_tensor(ksT[b][:], k, fac[b][:, FKS, :], ALU.mult).then_inc(prod_done, 1)
            for t in range(NT):
                g3 = keep["gg"][:, t, :].rearrange("p (h v) -> p h v", h=HEADS)
                pool.tensor_tensor(g3, g3, normg[:].unsqueeze(1).to_broadcast([P, HEADS, DV]), ALU.mult).then_inc(gate_done, 1)

        @block.vector
        def _(dve):
            steps = [0]

            def step(ins):
                steps[0] += 1
                ins.then_inc(dve_step, 1)
                dve.wait_ge(dve_step, steps[0])

            dve.memset(restart[:], 1.0).then_inc(dve_step, 1)
            steps[0] = 1
            dve.wait_ge(dve_step, 1)
            step(dve.memset(restart[:].rearrange("p (n b) -> p n b", b=P)[:, :, 0:1], 0.0))
            for m in range(3):
                dve.memset(AT[m][:], 0.0)
            step(dve.memset(AT[3][:], 0.0))

            def cumulate(u):
                g, m = UNITS[u]
                b = u % 2
                ba = keep["vcol"][:, V_BAF + m:V_BAF + m + 1]
                dve.wait_ge(soft_done, u + 1)
                step(dve.tensor_scalar(mn[:], ps_pre[:, 0:W], ba, 0.0, ALU.add, ALU.min))
                step(dve.tensor_tensor(la[:], mn[:], lg[:], ALU.subtract))
                if u >= 1:
                    dve.wait_ge(fac_done, u)
                c = cum[:, b, :]
                c3 = c.rearrange("p (n b) -> p n b", b=P)
                if m < 2:
                    dve.tensor_tensor_scan(c, restart[:], la[:], 0.0, ALU.mult, ALU.add).then_inc(cum_done, 1)
                    dve.wait_ge(cum_done, u + 1)
                else:
                    step(dve.tensor_tensor_scan(tmp[:], restart[:], la[:], 0.0, ALU.mult, ALU.add))
                    step(dve.tensor_tensor(c, la[:], tmp[:], ALU.subtract))
                    tot = tmp[:].rearrange("p (n b) -> p n b", b=P)[:, :, P - 1:P]
                    dve.tensor_tensor(c3, c3, tot.to_broadcast([P, G, P]), ALU.add).then_inc(cum_done, 1)
                    dve.wait_ge(cum_done, u + 1)
                for lv, size in ((0, 64), (1, 32), (2, 16), (3, 8)):
                    n = 2 * size
                    cv = c.rearrange("p (n b) -> p n b", b=n)
                    at = size - 1 if m < 2 else size
                    last = dve.tensor_tensor(dif[:, lv, :].rearrange("p (n b) -> p n b", b=n), cv,
                                             cv[:, :, at:at + 1].to_broadcast([P, W // n, n]), ALU.subtract)
                at = P - 1 if m < 2 else 0
                step(last)
                dve.tensor_tensor(dif[:, 4, :].rearrange("p (n b) -> p n b", b=P),
                                  c3[:, :, at:at + 1].to_broadcast([P, G, P]), c3, ALU.subtract)
                dve.tensor_scalar(dif[:, 3, :], dif[:, 3, :], CAP, -CAP, ALU.min, ALU.max).then_inc(dif_done, 1)

            def keep_scores(u):
                g, m = UNITS[u]
                dve.wait_ge(score_done, u + 1)
                if u >= 4:
                    dve.wait_ge(pv_done, G * g)
                sel = mask[:, m // 2, :].unsqueeze(1).to_broadcast([P, 2, P])
                for i in range(G):
                    last = dve.copy_predicated(AT[m][:, i, :, :], sel, ps_a[u % 2][:, :, i * P:(i + 1) * P])
                last.then_inc(at_done, 1)

            def keep_delta(u):
                g, m = UNITS[u]
                dve.wait_ge(delta_done, u + 1)
                dve.tensor_copy(S[:, m, g * G:(g + 1) * G, :],
                                ps_d[:, 0:W].rearrange("p (i v) -> p i v", i=G)).then_inc(s_done, 1)

            def keep_intra(g):
                for i in range(G):
                    t = g * G + i
                    dve.wait_ge(pv_done, t + 1)
                    dve.tensor_copy(keep["vg"][:, t, :], ps_o[:]).then_inc(intra_done, 1)

            dve.wait_ge(const_in, 96)
            cumulate(0)
            for u in range(NU + 1):
                if u + 1 < NU:
                    cumulate(u + 1)
                if u >= 1:
                    keep_delta(u - 1)
                    if UNITS[u - 1][1] == 3:
                        keep_intra(UNITS[u - 1][0])
                if u < NU:
                    keep_scores(u)
            dve.wait_ge(s_done, NU)
            done = 0
            for n in range(7):
                for m in range(4):
                    t = 1 + n if m < 2 else NT - 1 - n
                    before = S0[:, m, :] if n == 0 else S[:, m, t + (-1 if m < 2 else 1), :]
                    if n:
                        dve.wait_ge(rec_done, done - 3)
                    dve.scalar_tensor_tensor(out=S[:, m, t, :], in0=before, scalar=elast[:, m, t:t + 1], in1=S[:, m, t, :],
                                             op0=ALU.mult, op1=ALU.add).then_inc(rec_done, 1)
                    done += 1
            dve.wait_ge(rec_done, done)
            dve.memset(tmp[:, 0:1], 0.0).then_inc(rec_done, 1)

            def finish(t):
                src = keep["vg"][:, t, :] if t == 0 else osum[t % 2]
                s3 = src.rearrange("p (h v) -> p h v", h=HEADS)
                dve.wait_ge(rs_done, t + 1)
                step(dve.tensor_tensor(s3, s3, rs[:, t, :].unsqueeze(2).to_broadcast([P, HEADS, DV]), ALU.mult))
                dve.wait_ge(gate_done, t + 1)
                dve.tensor_tensor(keep["gg"][:, t, :], src, keep["gg"][:, t, :], ALU.mult).then_inc(gla_done, 1)

            for t in range(1, NT + 1):
                if t < NT:
                    dve.wait_ge(inter_done, t)
                    if t >= 3:
                        dve.wait_ge(gla_done, t - 1)
                    for h in range(2):
                        def mine(ap):
                            return ap.rearrange("p (m h v) -> p h m v", h=2, v=DV)[:, h, :, :]
                        last = dve.tensor_tensor(mine(osum[t % 2]), ps_i[(t - 1) % 2][:, h, :, :],
                                                 mine(keep["vg"][:, t, :]), ALU.add)
                    last.then_inc(osum_done, 1)
                finish(t - 1)


def window_attention(nc, dram, keep):
    with ExitStack() as ctx:
        def sb(name, shape, dt=F32):
            return ctx.enter_context(nc.sbuf_tensor(name, shape, dt))

        def ps(name, shape):
            return ctx.enter_context(nc.psum_tensor(name, shape, F32))

        def sem(name):
            return nc.alloc_semaphore(name)

        NH, HD = 8, 64
        SLOTS = 10
        SCALE = HD ** -0.5
        ck = sb("cache_k", [P, P])
        cv = sb("cache_v", [P, P])
        rope = sb("rope", [P, 8, 2, HD])
        bias = sb("band", [P, 896])
        sink = sb("sink", [P, NH])
        rq = [sb(f"rq{i}", [P, 640]) for i in range(2)]
        rt = sb("rt", [P, 640])
        kT = sb("kT", [P, SLOTS * P])
        NQ = 2
        qT = [sb(f"qT{i}", [P, 4, P]) for i in range(NQ)]
        NP_ = 4
        sc = [sb(f"sc{i}", [P, 512]) for i in range(NP_)]
        prT = [sb(f"prT{i}", [P, 512]) for i in range(2)]
        mx = sb("att_mx", [P, NT, NH])
        nmx = sb("att_nmx", [P, NT, NH])
        sm = sb("att_sm", [P, NT, NH])
        es = sb("att_es", [P, NT, NH])
        rden = sb("att_rden", [P, NT, NH])
        ps_q = ps("ps_q", [P, 512])
        ps_k = ps("ps_k", [P, 512])
        ps_s = [ps(f"ps_s{i}", [P, 512]) for i in range(2)]
        ps_p = [ps(f"ps_p{i}", [P, 512]) for i in range(2)]
        ps_o = [ps(f"ps_ao{i}", [P, 512]) for i in range(2)]

        const_in = sem("att_const_in")
        rope_step, rope_done = sem("rope_step"), sem("rope_done")
        kT_done, kT_kept, qT_done, qT_kept = sem("kT_done"), sem("kT_kept"), sem("qT_done"), sem("qT_kept")
        s_done, m_done, p_done, pT_done, pT_kept = sem("qk_done"), sem("max_done"), sem("p_done"), sem("pT_done"), sem("pT_kept")
        o_done, es_in, es_done, den_done, att_done, step_done = (sem("o_done"), sem("es_in"), sem("es_done"),
                                                                 sem("den_done"), sem("att_done"), sem("att_step"))

        STEPS = [(t, g * 4 + r) for t in range(NT) for r in range(4) for g in range(2)]

        def windows(t):
            if t == 0:
                return [(0, 9, 1)]
            lo, hi = max(1, t - 1), min(8, t + 1)
            return [(0, 0, 1), (P, lo, hi - lo + 1)]

        def width(t):
            return P * sum(n for _, _, n in windows(t))

        def values(slot, g):
            cols = slice(P + g * HD, P + g * HD + HD)
            if slot == 0:
                return cv[:, g * HD:(g + 1) * HD]
            return keep["kv"][:, slot % 9, cols]

        block = ctx.enter_context(nc.Block())

        @block.sync
        def _(sp):
            sp.dma_start(ck[:], dram["cache_k"]).then_inc(const_in, 16)
            sp.dma_start(cv[:], dram["cache_v"]).then_inc(const_in, 16)
            sp.dma_start(rope[:], dram["rope"]).then_inc(const_in, 16)
            sp.dma_start(bias[:], dram["band"]).then_inc(const_in, 16)
            sp.dma_start(sink[:], dram["sink"].to_broadcast([P, NH])).then_inc(const_in, 16)

        @block.gpsimd
        def _(pool):
            pool.wait_ge(const_in, 80)
            for n, t in enumerate(range(1, NT)):
                if n >= 2:
                    pool.wait_ge(qT_done, n)
                    pool.wait_ge(kT_done, n + 1)
                r = rq[n % 2]
                for src, dst, heads in ((keep["qs"][:, t, :], slice(0, 512), 8), (keep["kv"][:, t, 0:128], slice(512, 640), 2)):
                    cos = rope[:, t - 1, 0, :].unsqueeze(1).to_broadcast([P, heads, HD])
                    o3 = r[:, dst].rearrange("p (h d) -> p h d", d=HD)
                    pool.tensor_tensor(o3, src.rearrange("p (h d) -> p h d", d=HD), cos, ALU.mult)
                    x4 = src.rearrange("p (h a b d) -> p h a b d", a=2, b=2, d=16)
                    t4 = rt[:, dst].rearrange("p (h a b d) -> p h a b d", a=2, b=2, d=16)
                    s4 = rope[:, t - 1, 1, :].rearrange("p (a b d) -> p a b d", a=2, b=2)
                    for b in range(2):
                        last = pool.tensor_tensor(t4[:, :, :, b, :], x4[:, :, :, 1 - b, :],
                                                  s4[:, :, b, :].unsqueeze(1).to_broadcast([P, heads, 2, 16]), ALU.mult)
                last.then_inc(rope_step, 1)
                pool.wait_ge(rope_step, n + 1)
                pool.tensor_tensor(r[:], r[:], rt[:], ALU.add).then_inc(rope_done, 1)
                pool.wait_ge(rope_done, n + 1)

        @block.tensor
        def _(pe):
            turned = [0]

            def turn_k(slot):
                if turned[0]:
                    pe.wait_ge(kT_kept, turned[0])
                src = {0: ck[:], 9: keep["kv"][:, 0, 0:P]}.get(slot)
                if src is None:
                    pe.wait_ge(rope_done, slot)
                    src = rq[(slot - 1) % 2][:, 512:640]
                pe.transpose(ps_k[:, 0:P], src, keep["ident"][:]).then_inc(kT_done, 1)
                turned[0] += 1

            def turn_q(t):
                if t == 0:
                    src = keep["qs"][:, 0, :]
                else:
                    src = rq[(t - 1) % 2][:, 0:512]
                if t >= 1:
                    pe.wait_ge(qT_kept, t)
                for r in range(4):
                    last = pe.transpose(ps_q[:, r * P:(r + 1) * P], src[:, r * P:(r + 1) * P], keep["ident"][:])
                last.then_inc(qT_done, 1)

            def scores(n):
                t, h = STEPS[n]
                g, r = h // 4, h % 4
                rows = slice(HD * g, HD * g + HD)
                pe.wait_ge(qT_kept, t + 1)
                pe.wait_ge(kT_kept, 1 if t == 0 else min(t + 3, SLOTS))
                if n >= 2:
                    pe.wait_ge(m_done, n - 1)
                for c, slot, tiles in windows(t):
                    last = pe.matmul(ps_s[n % 2][:, c:c + tiles * P], qT[t % NQ][rows, r, :],
                                     kT[rows, slot * P:(slot + tiles) * P], start=True, stop=True)
                last.then_inc(s_done, 1)

            def turn_p(n):
                t, h = STEPS[n]
                pe.wait_ge(p_done, n + 1)
                if n >= 2:
                    pe.wait_ge(pT_kept, n - 1)
                for c in range(0, width(t), P):
                    last = pe.transpose(ps_p[n % 2][:, c:c + P], sc[n % NP_][:, c:c + P], keep["ident"][:])
                last.then_inc(pT_done, 1)

            def output(n):
                t, h = STEPS[n]
                pe.wait_ge(pT_kept, n + 1)
                if n % NH == 0 and t >= 2:
                    pe.wait_ge(att_done, t - 1)
                slots = [s + i for _, s, n_ in windows(t) for i in range(n_)]
                for i, slot in enumerate(slots):
                    last = pe.matmul(ps_o[t % 2][:, h * HD:(h + 1) * HD], prT[n % 2][:, i * P:(i + 1) * P],
                                     values(slot, h // 4), start=(i == 0), stop=(i == len(slots) - 1))
                last.then_inc(o_done, 1)

            pe.wait_ge(const_in, 80)
            turn_k(9)
            turn_q(0)
            turn_k(0)
            N = len(STEPS)
            for n in range(N + 3):
                if n < N:
                    t = STEPS[n][0]
                    if n == 0:
                        turn_k(1)
                    if n % NH == 4 and t + 1 < NT:
                        turn_q(t + 1)
                        if t + 2 < NT:
                            turn_k(t + 2)
                    scores(n)
                if n >= 2 and n - 2 < N:
                    turn_p(n - 2)
                if n >= 3:
                    output(n - 3)

        @block.scalar
        def _(act):
            def keep_q(t):
                act.wait_ge(qT_done, t + 1)
                if t >= NQ:
                    act.wait_ge(s_done, NH * (t - NQ + 1))
                act.activation(qT[t % NQ][:].rearrange("p r t -> p (r t)"), ps_q[:], ACT.Copy).then_inc(qT_kept, 1)

            def keep_k(i, slot):
                act.wait_ge(kT_done, i + 1)
                act.activation(kT[:, slot * P:(slot + 1) * P], ps_k[:, 0:P], ACT.Copy).then_inc(kT_kept, 1)

            def probs(n):
                t, h = STEPS[n]
                act.wait_ge(m_done, n + 1)
                act.activation(sc[n % NP_][:, 0:width(t)], sc[n % NP_][:, 0:width(t)], ACT.Exp,
                               bias=nmx[:, t, h:h + 1], accum_out=sm[:, t, h:h + 1]).then_inc(p_done, 1)

            keep_k(0, 9)
            keep_q(0)
            keep_k(1, 0)
            N = len(STEPS)
            for n in range(N):
                t = STEPS[n][0]
                if n == 0:
                    keep_k(2, 1)
                if n % NH == 4 and t + 1 < NT:
                    keep_q(t + 1)
                    if t + 2 < NT:
                        keep_k(t + 3, t + 2)
                probs(n)
                if n % NH == NH - 1:
                    act.wait_ge(es_in, t + 1)
                    act.activation(es[:, t, :], es[:, t, :], ACT.Exp).then_inc(es_done, 1)

        @block.vector
        def _(dve):
            dve.wait_ge(const_in, 80)

            steps = [0]

            def step(ins):
                steps[0] += 1
                ins.then_inc(step_done, 1)
                dve.wait_ge(step_done, steps[0])

            def maxima(n):
                t, h = STEPS[n]
                w = width(t)
                dve.wait_ge(s_done, n + 1)
                if n >= NP_:
                    dve.wait_ge(pT_done, n - NP_ + 1)
                c = 512 if t == 1 else 0
                mask = bias[:, c:c + w]
                step(dve.tensor_tensor_reduce(sc[n % NP_][:, 0:w], ps_s[n % 2][:, 0:w], mask, SCALE, sink[:, h:h + 1],
                                              ALU.add, ALU.max, mx[:, t, h:h + 1]))
                dve.tensor_scalar(nmx[:, t, h:h + 1], mx[:, t, h:h + 1], -1.0, None, ALU.mult).then_inc(m_done, 1)

            def keep_p(n):
                t, h = STEPS[n]
                dve.wait_ge(pT_done, n + 1)
                if n >= 2:
                    dve.wait_ge(o_done, n - 1)
                dve.tensor_copy(prT[n % 2][:, 0:width(t)], ps_p[n % 2][:, 0:width(t)]).then_inc(pT_kept, 1)

            def sink_part(t):
                dve.tensor_tensor(es[:, t, :], sink[:], mx[:, t, :], ALU.subtract).then_inc(es_in, 1)

            def finish(t):
                dve.wait_ge(es_done, t + 1)
                step(dve.tensor_tensor(sm[:, t, :], sm[:, t, :], es[:, t, :], ALU.add))
                step(dve.reciprocal(rden[:, t, :], sm[:, t, :]))
                dve.wait_ge(o_done, NH * (t + 1))
                dve.tensor_tensor(keep["qs"][:, t, :].rearrange("p (h d) -> p h d", d=HD),
                                  ps_o[t % 2][:].rearrange("p (h d) -> p h d", d=HD),
                                  rden[:, t, :].unsqueeze(2).to_broadcast([P, NH, HD]), ALU.mult).then_inc(att_done, 1)

            N = len(STEPS)
            for n in range(N + 4):
                if n < N:
                    maxima(n)
                    if n % NH == NH - 1:
                        sink_part(STEPS[n][0])
                if n >= 2 and n - 2 < N:
                    keep_p(n - 2)
                if n >= 4 and (n - 4) % NH == NH - 1:
                    finish(STEPS[n - 4][0])


NBMAX = 136
TAB = NBMAX + 4
NOWHERE = 1 << 20


def project_out(nc, dram, keep):
    with ExitStack() as ctx:
        def sb(name, shape, dt=F32):
            return ctx.enter_context(nc.sbuf_tensor(name, shape, dt))

        def ps(name, shape):
            return ctx.enter_context(nc.psum_tensor(name, shape, F32))

        def sem(name):
            return nc.alloc_semaphore(name)

        wo = sb("wo", [P, KD, D])
        rw = sb("rw", [P, KD, NE])
        a2col = sb("a2col", [P, KD, 2])
        xin = [sb(f"xin2_{i}", [P, D]) for i in range(2)]
        mixT = [sb(f"mixT{i}", [P, KD, P]) for i in range(2)]
        g2rows = keep["g2"]
        rows = sb("rows", [P, 3, 2, D])
        h2 = [sb(f"h2_{i}", [P, D]) for i in range(2)]
        ssq = sb("ssq2", [P, NT])
        std = sb("std2", [P, NT])
        rstd = sb("rstd2", [P, NT])
        ps_t = ps("ps_t4", [P, D])
        ps_o = ps("ps_o4", [P, 2, 512])
        ps_h = ps("ps_h4", [P, D])
        ps_r = ps("ps_r4", [P, 512])
        ps_b = ps("ps_b4", [P, 512])

        w_in, x_in = sem("wo_in"), [sem(f"x2_in{i}") for i in range(2)]
        a2_done, row_made, row_kept = sem("a2_done"), sem("row_made"), sem("row_kept")
        mixT_done, mixT_act, mixT_dve, o_done, x1_done = sem("mixT_done"), sem("mixT_act"), sem("mixT_dve"), sem("o4_done"), sem("x1_done")
        dve_step, gx_done, ssq_done, std_done = sem("dve_step4"), sem("gx_done"), sem("ssq2_done"), sem("std2_done")
        sc_done, h2_done, h2T_done, h2T_act, h2T_dve = sem("sc2_done"), sem("h2_done"), sem("h2T_done"), sem("h2T_act"), sem("h2T_dve")
        r_done, score_done, h2_out = sem("r_done"), sem("score4_done"), [sem(f"h2_out{i}") for i in range(2)]

        def piece(w, c, j):
            if w == 1:
                return a2col[:, j, c:c + 1]
            return keep["mod"][:, {0: 16, 2: 24, 3: 40}[w] + j, c:c + 1]

        QUARTERS = [(w, c, q) for w in range(4) for c in range(2) for q in range(2)]

        block = ctx.enter_context(nc.Block())

        @block.sync
        def _(sp):
            sp.dma_start(wo[:], dram["w_out"].rearrange("(j p) n -> p j n", p=P)).then_inc(w_in, 16)
            sp.dma_start(rw[:], dram["router_w"].rearrange("(p j) n -> p j n", j=KD)).then_inc(w_in, 16)
            for t in range(2):
                sp.dma_start(xin[t][:], dram["x"](t)).then_inc(x_in[t], 16)
            for t in range(NT):
                sp.wait_ge(h2_done, t + 1)
                sp.dma_start(dram["h2"][t * P:(t + 1) * P, :], h2[t % 2][:]).then_inc(h2_out[t % 2], 16)
                if t + 2 < NT:
                    sp.wait_ge(x1_done, t + 1)
                    sp.dma_start(xin[t % 2][:], dram["x"](t + 2)).then_inc(x_in[t % 2], 16)
            sp.wait_ge(h2_out[0], 16 * 5)
            sp.wait_ge(h2_out[1], 16 * 4)

        @block.tensor
        def _(pe):
            pe.wait_ge(a2_done, 1)
            for n, (w, c, q) in enumerate(QUARTERS):
                if n >= 1:
                    pe.wait_ge(row_kept, n)
                for i in range(4):
                    last = pe.matmul(ps_b[:, i * P:(i + 1) * P], piece(w, c, 4 * q + i).to_broadcast([P, P]),
                                     keep["ident"][:], start=True, stop=True)
                last.then_inc(row_made, 1)
            pe.wait_ge(w_in, 32)

            def turn_mix(t):
                if t >= 1:
                    pe.wait_ge(mixT_act, t)
                    pe.wait_ge(mixT_dve, t)
                for j in range(KD):
                    src = (keep["gg"] if j < 4 else keep["qs"])[:, t, (j % 4) * P:(j % 4 + 1) * P]
                    last = pe.transpose(ps_t[:, j * P:(j + 1) * P], src, keep["ident"][:])
                last.then_inc(mixT_done, 1)

            def out(t):
                pe.wait_ge(mixT_act, t + 1)
                pe.wait_ge(mixT_dve, t + 1)
                if t >= 1:
                    pe.wait_ge(gx_done, t)
                for j in range(KD):
                    for n in range(2):
                        last = pe.matmul(ps_o[:, n, :], mixT[t % 2][:, j, :], wo[:, j, n * 512:(n + 1) * 512],
                                         start=(j == 0), stop=(j == KD - 1))
                last.then_inc(o_done, 1)

            def turn_h(t):
                pe.wait_ge(h2_done, t + 1)
                if t >= 1:
                    pe.wait_ge(h2T_act, t)
                    pe.wait_ge(h2T_dve, t)
                for j in range(KD):
                    last = pe.transpose(ps_h[:, j * P:(j + 1) * P], h2[t % 2][:, j:D:KD], keep["ident"][:])
                last.then_inc(h2T_done, 1)

            def route(t):
                pe.wait_ge(h2T_act, t + 1)
                pe.wait_ge(h2T_dve, t + 1)
                if t >= 1:
                    pe.wait_ge(score_done, t)
                for j in range(KD):
                    last = pe.matmul(ps_r[:, 0:NE], keep["h2T"][:, j, t * P:(t + 1) * P], rw[:, j, :],
                                     start=(j == 0), stop=(j == KD - 1))
                last.then_inc(r_done, 1)

            turn_mix(0)
            for t in range(NT + 2):
                if t + 1 < NT:
                    turn_mix(t + 1)
                if t < NT:
                    out(t)
                if t >= 2:
                    route(t - 2)
                if 1 <= t <= NT:
                    turn_h(t - 1)

        @block.scalar
        def _(act):
            nc.scalar.preload_act_table_set("sqrt_and_others")

            def mix_half(t):
                act.wait_ge(mixT_done, t + 1)
                if t >= 2:
                    act.wait_ge(o_done, t - 1)
                act.activation(mixT[t % 2][:, 0:4, :].rearrange("p j t -> p (j t)"), ps_t[:, 0:512], ACT.Copy).then_inc(mixT_act, 1)

            def square(t):
                act.wait_ge(x1_done, t + 1)
                if t >= 2:
                    act.wait_ge(h2_out[t % 2], 16 * (t // 2))
                    act.wait_ge(h2T_done, t - 1)
                act.activation(h2[t % 2][:], keep["x1"][:, t, :], ACT.Square, accum_out=ssq[:, t:t + 1]).then_inc(ssq_done, 1)
                act.wait_ge(ssq_done, t + 1)
                act.activation(std[:, t:t + 1], ssq[:, t:t + 1], ACT.Sqrt, scale=1.0 / D, bias=keep["eps"][:]).then_inc(std_done, 1)

            def h_half(t):
                act.wait_ge(h2T_done, t + 1)
                act.activation(keep["h2T"][:, 0:4, t * P:(t + 1) * P], ps_h[:, 0:512].rearrange("p (j t) -> p j t", j=4),
                               ACT.Copy).then_inc(h2T_act, 1)

            def logits(t):
                act.wait_ge(r_done, t + 1)
                act.activation(keep["logit"][:, t, :], ps_r[:, 0:NE], ACT.Copy).then_inc(score_done, 1)

            mix_half(0)
            for t in range(NT + 2):
                if t + 1 < NT:
                    mix_half(t + 1)
                if t >= 2:
                    logits(t - 2)
                if t < NT:
                    square(t)
                if 1 <= t <= NT:
                    h_half(t - 1)

        @block.gpsimd
        def _(pool):
            for t in range(NT):
                pool.wait_ge(sc_done, t + 1)
                pool.tensor_tensor(h2[t % 2][:], h2[t % 2][:], rows[:, 2, cond_of(t), :], ALU.add).then_inc(h2_done, 1)

        @block.vector
        def _(dve):
            steps = [0]

            def step(ins):
                steps[0] += 1
                ins.then_inc(dve_step, 1)
                dve.wait_ge(dve_step, steps[0])

            dve.scalar_tensor_tensor(out=a2col[:], in0=keep["mod"][:, 32:40, :], scalar=1.0,
                                     in1=keep["vcol"][:, V_NF:V_NF + 8].unsqueeze(2).to_broadcast([P, KD, 2]),
                                     op0=ALU.add, op1=ALU.mult).then_inc(a2_done, 1)
            for n, (w, c, q) in enumerate(QUARTERS):
                dve.wait_ge(row_made, n + 1)
                dst = rows[:, w, c, :] if w < 3 else g2rows[:, c, :]
                dve.tensor_copy(dst[:, q * 512:(q + 1) * 512], ps_b[:]).then_inc(row_kept, 1)
            dve.wait_ge(row_kept, len(QUARTERS))

            def mix_half(t):
                dve.wait_ge(mixT_done, t + 1)
                if t >= 2:
                    dve.wait_ge(o_done, t - 1)
                dve.tensor_copy(mixT[t % 2][:, 4:8, :].rearrange("p j t -> p (j t)"), ps_t[:, 512:1024]).then_inc(mixT_dve, 1)

            def residual(t):
                c = cond_of(t)
                dve.wait_ge(o_done, t + 1)
                dve.tensor_tensor(keep["x1"][:, t, :], ps_o[:].rearrange("p n k -> p (n k)"), rows[:, 0, c, :], ALU.mult).then_inc(gx_done, 1)
                dve.wait_ge(gx_done, t + 1)
                dve.wait_ge(x_in[t % 2], 16 * (t // 2 + 1))
                dve.tensor_tensor(keep["x1"][:, t, :], keep["x1"][:, t, :], xin[t % 2][:], ALU.add).then_inc(x1_done, 1)

            def scale(t):
                dve.wait_ge(std_done, t + 1)
                step(dve.reciprocal(rstd[:, t:t + 1], std[:, t:t + 1]))
                dve.scalar_tensor_tensor(out=h2[t % 2][:], in0=keep["x1"][:, t, :], scalar=rstd[:, t:t + 1],
                                         in1=rows[:, 1, cond_of(t), :], op0=ALU.mult, op1=ALU.mult).then_inc(sc_done, 1)

            def h_half(t):
                dve.wait_ge(h2T_done, t + 1)
                dve.tensor_copy(keep["h2T"][:, 4:8, t * P:(t + 1) * P],
                                ps_h[:, 512:1024].rearrange("p (j t) -> p j t", j=4)).then_inc(h2T_dve, 1)

            mix_half(0)
            for t in range(NT + 1):
                if t + 1 < NT:
                    mix_half(t + 1)
                if t < NT:
                    residual(t)
                    scale(t)
                if t >= 1:
                    h_half(t - 1)


def route(nc, dram, keep):
    with ExitStack() as ctx:
        def sb(name, shape, dt=F32):
            return ctx.enter_context(nc.sbuf_tensor(name, shape, dt))

        def ps(name, shape):
            return ctx.enter_context(nc.psum_tensor(name, shape, F32))

        def sem(name):
            return nc.alloc_semaphore(name)

        GE = 8
        rb = sb("rb", [P, NE])
        before = sb("before", [P, GE * GE])
        upperf = sb("upperf", [P, P])
        upper = sb("upper", [P, P], BF16)
        ones = sb("ones", [P, P], BF16)
        onesf = sb("onesf", [P, NE])
        thr = sb("thr", [P, GE])
        blk = sb("blk", [P, 2])
        tok8 = sb("tok8", [P, NT, GE], I32)
        fill = sb("fill", [P, TAB, 4], I32)
        sc = sb("r_sc", [P, NT, NE])
        sel = sb("r_sel", [P, NT, NE])
        top = sb("r_top", [P, NT, GE, GE])
        gs = sb("r_gs", [P, NT, GE])
        cmp_ = sb("r_cmp", [P, NT, GE, GE])
        cm2 = sb("r_cm2", [P, NT, GE, GE])
        rank = sb("r_rank", [P, NT, GE])
        gm = sb("r_gm", [P, NT, GE])
        best = sb("r_best", [P, NT, TOPK])
        M = sb("r_M", [P, NT, NE])
        Mb = sb("r_Mb", [P, NT, NE], BF16)
        gate = sb("r_gate", [P, NT, NE])
        wsum = sb("r_wsum", [P, NT])
        over = sb("r_over", [P, NE, GE])
        nb = sb("r_nb", [P, NE])
        inc = sb("r_inc", [P, NE])
        start = sb("r_start", [P, NE])
        slot = sb("r_slot", [P, NT, NE])
        s8 = sb("r_s8", [P, NT, TOPK])
        s8i = sb("r_s8i", [P, NT, TOPK], I32)
        r8i = sb("r_r8i", [P, NT, TOPK], I32)
        r8 = sb("r_r8", [P, NT, TOPK])
        b8 = sb("r_b8", [P, NT, TOPK])
        row = sb("r_row", [P, NT, TOPK], I32)
        eq = sb("r_eq", [P, TOPK, NE])
        g8 = sb("r_g8", [P, NT, TOPK])
        recs = sb("r_recs", [P, NT, TOPK, 4], I32)
        ebc = sb("r_ebc", [P, 2, NE])
        ebf = sb("r_ebf", [P, 2])
        ebi = sb("r_ebi", [P, 2], I32)
        lasti = sb("r_lasti", [1, 1], I32)
        lastf = sb("r_lastf", [1, 3])
        ps_n = [ps("ps_n0", [P, 512]), ps("ps_n1", [P, 512])]

        const_in, fill_in, dve_step, sig_done = sem("r_const_in"), sem("fill_in"), sem("r_step"), sem("sig_done")
        ones_done, m_done, rank_done, recs_done, eb_done = sem("ones_done"), sem("M_done"), sem("rank_done"), sem("recs_done"), sem("eb_done")
        tab_fill, scattered, eb_out, tabs_in = sem("tab_fill"), sem("scattered"), sem("eb_out"), sem("tabs_in")

        block = ctx.enter_context(nc.Block())

        @block.sync
        def _(sp):
            sp.dma_start(rb[:], dram["router_bias"].to_broadcast([P, NE])).then_inc(const_in, 16)
            sp.dma_start(before[:], dram["before"].to_broadcast([P, GE * GE])).then_inc(const_in, 16)
            sp.dma_start(upperf[:], dram["upper"]).then_inc(const_in, 16)
            sp.dma_start(blk[:], dram["blk"]).then_inc(const_in, 16)
            sp.dma_start(tok8[:], dram["tok8"]).then_inc(const_in, 16)
            sp.dma_start(thr[:], dram["thr"].to_broadcast([P, GE])).then_inc(const_in, 16)
            sp.dma_start(fill[:], dram["fill"].to_broadcast([P, TAB * 4]).rearrange("p (b k) -> p b k", k=4)).then_inc(fill_in, 16)
            sp.wait_ge(fill_in, 16)
            sp.dma_start(dram["table"].rearrange("(p b) k -> p b k", b=TAB), fill[:]).then_inc(tab_fill, 16)
            sp.wait_ge(eb_done, 1)
            sp.dma_start(dram["block_expert"].rearrange("(p c) -> p c", p=P), ebi[:]).then_inc(eb_out, 16)
            sp.wait_ge(eb_out, 16)
            sp.dma_start(keep["bexp"][:], dram["block_expert"].rearrange("(a n) -> a n", a=1)).then_inc(eb_out, 16)
            sp.wait_ge(scattered, 16 * NT * TOPK)
            sp.dma_start(keep["tab"][:], dram["table"].rearrange("(p b) k -> p b k", b=TAB)).then_inc(tabs_in, 16)
            sp.wait_ge(eb_out, 32)
            sp.wait_ge(tabs_in, 16)

        @block.gpsimd
        def _(pool):
            pool.wait_ge(tab_fill, 16)
            for t in range(NT):
                pool.wait_ge(recs_done, t + 1)
                for j in range(TOPK):
                    pool.indirect_dma_start(out=dram["table"], out_offset=bass.IndirectOffsetOnAxis(ap=row[:, t, j:j + 1], axis=0),
                                            in_=recs[:, t, j, :], in_offset=None).then_inc(scattered, 16)
            pool.wait_ge(scattered, 16 * NT * TOPK)

        @block.scalar
        def _(act):
            act.activation(sc[:], keep["logit"][:], ACT.Sigmoid).then_inc(sig_done, 1)

        @block.tensor
        def _(pe):
            pe.wait_ge(m_done, 1)
            pe.wait_ge(const_in, 96)
            for t in range(NT):
                out = ps_n[t // 8][:, (t % 8) * NE:(t % 8 + 1) * NE]
                for s in range(t):
                    pe.matmul(out, ones[:], Mb[:, s, :], start=(s == 0), stop=False)
                pe.matmul(out, upper[:], Mb[:, t, :], start=(t == 0), stop=True)
            for s in range(NT):
                last = pe.matmul(ps_n[1][:, NE:2 * NE], ones[:], Mb[:, s, :], start=(s == 0), stop=(s == NT - 1))
            last.then_inc(rank_done, 1)

        @block.vector
        def _(dve):
            steps = [0]

            def step(ins):
                steps[0] += 1
                ins.then_inc(dve_step, 1)
                dve.wait_ge(dve_step, steps[0])

            def per_expert(ap):
                return ap.unsqueeze(1).to_broadcast([P, NT, NE])

            dve.memset(ones[:], 1.0)
            step(dve.memset(onesf[:], 1.0))
            dve.wait_ge(const_in, 96)
            dve.tensor_copy(upper[:], upperf[:])
            dve.wait_ge(sig_done, 1)
            step(dve.tensor_tensor(sel[:], sc[:], per_expert(rb[:]), ALU.add))
            for t in range(NT):
                for g in range(GE):
                    last = dve.max(top[:, t, g, :], sel[:, t, g * GE:(g + 1) * GE])
            step(last)
            step(dve.tensor_tensor(gs[:], top[:, :, :, 0], top[:, :, :, 1], ALU.add))
            other = gs[:].unsqueeze(2).to_broadcast([P, NT, GE, GE])
            own = gs[:].unsqueeze(3).to_broadcast([P, NT, GE, GE])
            dve.tensor_tensor(cmp_[:], other, own, ALU.is_gt)
            step(dve.tensor_tensor(cm2[:], other, own, ALU.is_equal))
            step(dve.tensor_tensor(cm2[:].rearrange("p t a b -> p t (a b)"), cm2[:].rearrange("p t a b -> p t (a b)"),
                                   before[:].unsqueeze(1).to_broadcast([P, NT, GE * GE]), ALU.mult))
            step(dve.tensor_tensor(cmp_[:], cmp_[:], cm2[:], ALU.add))
            step(dve.tensor_reduce(rank[:], cmp_[:], AX.X, ALU.add))
            step(dve.tensor_scalar(gm[:], rank[:], 3.5, None, ALU.is_lt))
            mask = gm[:].unsqueeze(3).to_broadcast([P, NT, GE, GE])
            step(dve.tensor_tensor(sel[:].rearrange("p t (g e) -> p t g e", g=GE), sel[:].rearrange("p t (g e) -> p t g e", g=GE), mask, ALU.mult))
            step(dve.tensor_scalar(gm[:], gm[:], -1.0, 1e30, ALU.add, ALU.mult))
            step(dve.tensor_tensor(sel[:].rearrange("p t (g e) -> p t g e", g=GE), sel[:].rearrange("p t (g e) -> p t g e", g=GE), mask, ALU.add))
            for t in range(NT):
                last = dve.max(best[:, t, :], sel[:, t, :])
            step(last)
            for t in range(NT):
                last = dve.match_replace(M[:, t, :], best[:, t, :], sel[:, t, :], -3e38)
            step(last)
            step(dve.tensor_tensor(M[:], M[:], sel[:], ALU.not_equal))
            dve.tensor_copy(Mb[:], M[:]).then_inc(m_done, 1)
            step(dve.tensor_tensor(gate[:], sc[:], M[:], ALU.mult))
            step(dve.tensor_reduce(wsum[:], gate[:], AX.X, ALU.add))
            step(dve.reciprocal(wsum[:], wsum[:]))
            step(dve.tensor_scalar(wsum[:], wsum[:], 2.5, None, ALU.mult))
            step(dve.tensor_tensor(gate[:], gate[:], wsum[:].unsqueeze(2).to_broadcast([P, NT, NE]), ALU.mult))
            dve.wait_ge(rank_done, 1)
            step(dve.tensor_tensor(over[:], ps_n[1][:, NE:2 * NE].unsqueeze(2).to_broadcast([P, NE, GE]),
                                   thr[:].unsqueeze(1).to_broadcast([P, NE, GE]), ALU.is_gt))
            step(dve.tensor_reduce(nb[:], over[:], AX.X, ALU.add))
            step(dve.tensor_scalar(nb[:], nb[:], 1.0, None, ALU.add))
            step(dve.tensor_tensor_scan(inc[:], onesf[:], nb[:], 0.0, ALU.mult, ALU.add))
            step(dve.tensor_tensor(start[:], inc[:], nb[:], ALU.subtract))
            step(dve.tensor_scalar(start[:], start[:], float(P), 1.0, ALU.mult, ALU.add))
            dve.tensor_tensor(slot[:, 0:8, :], ps_n[0][:].rearrange("p (t e) -> p t e", e=NE),
                              start[:].unsqueeze(1).to_broadcast([P, 8, NE]), ALU.add)
            step(dve.tensor_tensor(slot[:, 8, :], ps_n[1][:, 0:NE], start[:], ALU.add))
            step(dve.tensor_tensor(slot[:], slot[:], M[:], ALU.mult))
            for t in range(NT):
                last = dve.max(s8[:, t, :], slot[:, t, :])
            step(last)
            for c in range(2):
                last = dve.tensor_scalar(ebc[:, c, :], inc[:], blk[:, c:c + 1], None, ALU.is_le)
            step(last)
            step(dve.tensor_reduce(ebf[:], ebc[:], AX.X, ALU.add))
            step(dve.tensor_scalar(ebf[:], ebf[:], float(NE - 1), None, ALU.min))
            dve.tensor_copy(keep["bend"][:, 0:NE], inc[0:1, :])
            step(dve.tensor_scalar(lasti[:], inc[0:1, NE - 1:NE], 3.0, None, ALU.add))
            step(dve.tensor_scalar(lasti[:], lasti[:], 2, None, ALU.logical_shift_right))
            step(dve.tensor_copy(lastf[:, 0:1], lasti[:]))
            dve.tensor_scalar(lastf[:, 1:2], lastf[:, 0:1], 4.0, -1.0, ALU.mult, ALU.add)
            step(dve.tensor_scalar(lastf[:, 2:3], lastf[:, 0:1], 16.0, -16.0, ALU.mult, ALU.add))
            dve.tensor_copy(keep["bend"][:, NE:NE + 2], lastf[:, 1:3])
            dve.tensor_copy(ebi[:], ebf[:]).then_inc(eb_done, 1)
            dve.tensor_scalar(b8[:], s8[:], -1.0, None, ALU.add)
            step(dve.tensor_scalar(s8i[:], s8[:], -1.0, None, ALU.add))
            step(dve.tensor_scalar(r8i[:], s8i[:], P - 1, None, ALU.bitwise_and))
            step(dve.tensor_copy(r8[:], r8i[:]))
            step(dve.tensor_tensor(b8[:], b8[:], r8[:], ALU.subtract))
            step(dve.tensor_scalar(b8[:], b8[:], 1.0 / P, None, ALU.mult))
            step(dve.scalar_tensor_tensor(out=row[:], in0=r8[:], scalar=float(TAB), in1=b8[:], op0=ALU.mult, op1=ALU.add))
            dve.tensor_scalar(recs[:, :, :, 0], tok8[:], 3, None, ALU.logical_shift_right)
            step(dve.tensor_copy(recs[:, :, :, 1], tok8[:]))
            for t in range(NT):
                step(dve.tensor_tensor(eq[:], slot[:, t, :].unsqueeze(1).to_broadcast([P, TOPK, NE]),
                                       s8[:, t, :].unsqueeze(2).to_broadcast([P, TOPK, NE]), ALU.is_equal))
                step(dve.tensor_tensor(eq[:], eq[:], gate[:, t, :].unsqueeze(1).to_broadcast([P, TOPK, NE]), ALU.mult))
                step(dve.tensor_reduce(g8[:, t, :], eq[:], AX.X, ALU.add))
                dve.tensor_copy(recs[:, t, :, 3], tok8[:, t, :])
                dve.tensor_copy(recs[:, t, :, 2].bitcast(F32), g8[:, t, :]).then_inc(recs_done, 1)


def experts(nc, dram, keep):
    with ExitStack() as ctx:
        def sb(name, shape, dt=F32):
            return ctx.enter_context(nc.sbuf_tensor(name, shape, dt))

        def ps(name, shape):
            return ctx.enter_context(nc.psum_tensor(name, shape, F32))

        def sem(name):
            return nc.alloc_semaphore(name)

        NW = 8
        AHEAD = 4
        FOURS = NBMAX // 4
        w = sb("w_exp", [P, NW * 3, D])
        buf = keep["mix"]
        x = [buf[:, i * D:(i + 1) * D] for i in range(4)]
        xT = [buf[:, (4 + i) * D:(5 + i) * D] for i in range(2)]
        y = [buf[:, (6 + i) * D:(7 + i) * D] for i in range(3)] + [sb("y5_3", [P, D])[:]]
        gi = [sb(f"gather_row{i}", [P, 1], I32) for i in range(4)]
        si = [sb(f"scatter_row{i}", [P, 1], I32) for i in range(4)]
        s = [sb(f"silu{i}", [P, FF]) for i in range(2)]
        h = [sb(f"hid{i}", [P, FF]) for i in range(2)]
        hT = [sb(f"hidT{i}", [P, P]) for i in range(2)]
        ps_x = ps("ps_x5", [P, D])
        ps_g = [ps(f"ps_g5_{i}", [P, 512]) for i in range(2)]
        ps_h = ps("ps_h5", [P, 512])
        ps_y = ps("ps_y5", [P, D])

        w_in = [sem(f"w_in{i}") for i in range(NW)]
        w_ready = sem("w_ready")
        x_in = [sem(f"x5_in{i}") for i in range(4)]
        y_out = [sem(f"y_out{i}") for i in range(4)]
        passed = sem("pool_passed")
        zeroed, gi_done, si_done = sem("x_zeroed"), sem("gi_done"), sem("si_done")
        xT_done, xT_act, xT_dve = sem("xT5_done"), sem("xT5_act"), sem("xT5_dve")
        gu_done, silu_done, h_done, hT_done, hT_kept = sem("gu_done"), sem("silu_done"), sem("h_done"), sem("hT_done"), sem("hT_kept")
        down_done, y_act, y_dve = sem("down_done"), sem("y_act"), sem("y_dve")

        wg = dram["exp_w_gate"].rearrange("(e p j) f -> e p (j f)", p=P, j=KD)
        wu = dram["exp_w_up"].rearrange("(e p j) f -> e p (j f)", p=P, j=KD)
        wd = dram["exp_w_down"].rearrange("(e p) n -> e p n", p=P)

        def fours(eng, body):
            blocks = eng.value_load(keep["bend"][0:1, NE - 1:NE], min_val=NE, max_val=NBMAX)
            body(0)
            with eng.Fori(1, FOURS) as i:
                with eng.If(i * 4 < blocks):
                    body(i)
            return (eng.value_load(keep["bend"][0:1, NE:NE + 1], min_val=NE - 1, max_val=NBMAX - 1),
                    eng.value_load(keep["bend"][0:1, NE + 1:NE + 2], min_val=16, max_val=16 * FOURS - 16))

        def first(i):
            return isinstance(i, int)

        block = ctx.enter_context(nc.Block())

        @block.sync
        def _(sp):
            def issue(e, slot):
                for k, src in enumerate((wg, wu, wd)):
                    sp.dma_start(w[:, 3 * slot + k, :], src[e, :, :]).then_inc(w_in[slot], 16)

            def ready(o, i):
                sp.wait_ge(w_in[i], (o + 1) * 48)
                sp.sem_inc(w_ready, 1)

            def replace(o, i, wait=True):
                if wait:
                    last = sp.value_load(keep["bend"][0:1, bass.ds(o * NW + (i - 1), 1)], min_val=0, max_val=NBMAX)
                    sp.wait_ge(down_done, last)
                issue(o * NW + (i + NW - 1), (i + NW - 1) % NW)

            for e in range(NW - 1):
                issue(e, e)
            for i in range(AHEAD):
                ready(0, i)
            for i in range(NW):
                ready((i + AHEAD) // NW, (i + AHEAD) % NW)
                replace(0, i, wait=i > 0)
            with sp.Fori(1, NE // NW - 1) as o:
                for i in range(NW):
                    ready(o + (i + AHEAD) // NW, (i + AHEAD) % NW)
                    replace(o, i)
            replace(NE // NW - 1, 0)
            for i in range(AHEAD, NW):
                ready(NE // NW - 1, i)

        @block.gpsimd
        def _(pool):
            def gather(k, b):
                pool.tensor_copy(gi[k][:], keep["tab"][:, b, 0:1]).then_inc(gi_done, 1)
                pool.wait_ge(gi_done, b + 1)
                pool.sem_inc(passed, 1)
                pool.indirect_dma_start(out=x[k], out_offset=None, in_=dram["h2"],
                                        in_offset=bass.IndirectOffsetOnAxis(ap=gi[k][:], axis=0),
                                        bounds_check=T - 1, oob_is_err=False).then_inc(x_in[k], 16)

            pool.memset(buf[:, 0:4 * D], 0.0).then_inc(zeroed, 1)
            pool.wait_ge(zeroed, 1)
            for k in range(4):
                gather(k, k)

            def body(i):
                for k in range(4):
                    b = i * 4 + k
                    pool.wait_ge(xT_done, b + 1)
                    pool.sem_inc(passed, 1)
                    gather(k, b + 4)
                    if not first(i):
                        pool.wait_ge(y_out[k], i * 16)
                        pool.sem_inc(passed, 1)
                    pool.tensor_copy(si[k][:], keep["tab"][:, b, 1:2]).then_inc(si_done, 1)
                    pool.wait_ge(si_done, b + 1)
                    pool.wait_ge(y_act, b + 1)
                    pool.wait_ge(y_dve, b + 1)
                    pool.sem_inc(passed, 1)
                    pool.indirect_dma_start(out=dram["y"], out_offset=bass.IndirectOffsetOnAxis(ap=si[k][:], axis=0),
                                            in_=y[k], in_offset=None,
                                            bounds_check=T * TOPK - 1, oob_is_err=False).then_inc(y_out[k], 16)

            last, before = fours(pool, body)
            for k in range(4):
                pool.wait_ge(y_out[k], before + 16)
                pool.wait_ge(x_in[k], before + 32)

        @block.tensor
        def _(pe):
            def expert_of(b):
                return pe.value_load(keep["bexp"][0:1, bass.ds(b, 1)], min_val=0, max_val=NE - 1)

            def turn_x(k, b, n):
                pe.wait_ge(x_in[k], n * 16 + 16)
                for j in range(KD):
                    last = pe.transpose(ps_x[:, j * P:(j + 1) * P], x[k][:, j:D:KD], keep["ident"][:])
                last.then_inc(xT_done, 1)

            def down(par, b, slot):
                pe.wait_ge(hT_kept, b + 1)
                for n in range(2):
                    last = pe.matmul(ps_y[:, n * 512:(n + 1) * 512], hT[par][:],
                                     w[:, slot * 3 + 2, n * 512:(n + 1) * 512], start=True, stop=True)
                last.then_inc(down_done, 1)

            turn_x(0, 0, 0)

            def body(i):
                for k in range(4):
                    b, par = i * 4 + k, k % 2
                    slot = expert_of(b) % NW
                    former = None if first(i) and k == 0 else expert_of(b - 1) % NW
                    pe.wait_ge(w_ready, expert_of(b) + 1)
                    pe.wait_ge(xT_act, b + 1)
                    pe.wait_ge(xT_dve, b + 1)
                    if not (first(i) and k < 2):
                        pe.wait_ge(h_done, b - 1)
                    for j in range(KD):
                        last = pe.matmul(ps_g[par][:, 0:2 * FF].rearrange("p (k f) -> p k f", k=2),
                                         xT[par][:, j * P:(j + 1) * P],
                                         w[:, bass.ds(slot * 3, 2), j * FF:(j + 1) * FF],
                                         start=(j == 0), stop=(j == KD - 1))
                    last.then_inc(gu_done, 1)
                    turn_x((k + 1) % 4, b + 1, i + (k + 1) // 4)
                    if not (first(i) and k == 0):
                        if not (first(i) and k == 1):
                            pe.wait_ge(y_act, b - 1)
                            pe.wait_ge(y_dve, b - 1)
                        down(1 - par, b - 1, former)
                    pe.wait_ge(h_done, b + 1)
                    pe.transpose(ps_h[:, 0:P], h[par][:], keep["ident"][:]).then_inc(hT_done, 1)

            last, _ = fours(pe, body)
            slot = expert_of(last) % NW
            pe.wait_ge(y_act, last)
            pe.wait_ge(y_dve, last)
            down(1, last, slot)

        def move_x(eng, copy, done, half, par, b, wait):
            eng.wait_ge(xT_done, b + 1)
            if wait:
                eng.wait_ge(gu_done, b - 1)
            copy(xT[par][:, half * 512:(half + 1) * 512], ps_x[:, half * 512:(half + 1) * 512]).then_inc(done, 1)

        def move_y(eng, copy, done, half, k, b, n):
            eng.wait_ge(down_done, b + 1)
            if n is not None:
                eng.wait_ge(y_out[k], n)
            copy(y[k][:, half * 512:(half + 1) * 512], ps_y[:, half * 512:(half + 1) * 512]).then_inc(done, 1)

        def stores_before(i, k):
            if first(i):
                return None
            return (i - 1) * 16 if k == 0 else i * 16

        @block.scalar
        def _(act):
            nc.scalar.preload_act_table_set("silu_and_others")

            def copy(out, in_):
                return act.activation(out, in_, ACT.Copy)

            move_x(act, copy, xT_act, 0, 0, 0, False)

            def body(i):
                for k in range(4):
                    b, par = i * 4 + k, k % 2
                    act.wait_ge(gu_done, b + 1)
                    if not (first(i) and k < 2):
                        act.wait_ge(h_done, b - 1)
                    act.activation(s[par][:], ps_g[par][:, 0:FF], ACT.Silu).then_inc(silu_done, 1)
                    move_x(act, copy, xT_act, 0, 1 - par, b + 1, not (first(i) and k == 0))
                    if not (first(i) and k == 0):
                        move_y(act, copy, y_act, 0, (k + 3) % 4, b - 1, stores_before(i, k))
                    act.wait_ge(hT_done, b + 1)
                    if not (first(i) and k < 2):
                        act.wait_ge(down_done, b - 1)
                    copy(hT[par][:], ps_h[:, 0:P]).then_inc(hT_kept, 1)

            last, before = fours(act, body)
            move_y(act, copy, y_act, 0, 3, last, before)

        @block.vector
        def _(dve):
            move_x(dve, dve.tensor_copy, xT_dve, 1, 0, 0, False)

            def body(i):
                for k in range(4):
                    b, par = i * 4 + k, k % 2
                    dve.wait_ge(silu_done, b + 1)
                    if not (first(i) and k < 2):
                        dve.wait_ge(hT_done, b - 1)
                    dve.scalar_tensor_tensor(out=h[par][:], in0=s[par][:], scalar=keep["tab"][:, b, 2:3].bitcast(F32),
                                             in1=ps_g[par][:, FF:2 * FF], op0=ALU.mult, op1=ALU.mult).then_inc(h_done, 1)
                    move_x(dve, dve.tensor_copy, xT_dve, 1, 1 - par, b + 1, not (first(i) and k == 0))
                    if not (first(i) and k == 0):
                        move_y(dve, dve.tensor_copy, y_dve, 1, (k + 3) % 4, b - 1, stores_before(i, k))

            last, before = fours(dve, body)
            move_y(dve, dve.tensor_copy, y_dve, 1, 3, last, before)


def shared_expert(nc, dram, keep):
    with ExitStack() as ctx:
        def sb(name, shape, dt=F32):
            return ctx.enter_context(nc.sbuf_tensor(name, shape, dt))

        def ps(name, shape):
            return ctx.enter_context(nc.psum_tensor(name, shape, F32))

        def sem(name):
            return nc.alloc_semaphore(name)

        FS = 256
        wgu = sb("wgu", [P, 2, KD * FS])
        wd = sb("wd_s", [P, 2, D])
        s = [sb(f"s6_{i}", [P, FS]) for i in range(2)]
        h = [sb(f"h6_{i}", [P, FS]) for i in range(2)]
        hT = [sb(f"hT6_{i}", [P, FS]) for i in range(2)]
        t6 = sb("t6", [P, D])
        ps_g = [ps(f"ps_g6_{i}", [P, 512]) for i in range(2)]
        ps_h = ps("ps_h6", [P, 512])
        ps_y = [ps(f"ps_y6_{i}", [P, D]) for i in range(2)]
        w_in = sem("ws_in")
        gu_done, silu_done, h_done, hT_done, hT_kept = sem("gu6"), sem("silu6"), sem("h6"), sem("hT6"), sem("hTk6")
        down_done, t_done, x_done = sem("down6"), sem("t6_done"), sem("x6_done")
        block = ctx.enter_context(nc.Block())

        @block.sync
        def _(sp):
            sp.dma_start(wgu[:, 0, :], dram["sh_w_gate"].rearrange("(p j) f -> p (j f)", j=KD)).then_inc(w_in, 16)
            sp.dma_start(wgu[:, 1, :], dram["sh_w_up"].rearrange("(p j) f -> p (j f)", j=KD)).then_inc(w_in, 16)
            sp.dma_start(wd[:], dram["sh_w_down"].rearrange("(k p) n -> p k n", p=P)).then_inc(w_in, 16)

        @block.tensor
        def _(pe):
            pe.wait_ge(w_in, 48)
            for t in range(NT + 1):
                if t < NT:
                    if t >= 2:
                        pe.wait_ge(h_done, t - 1)
                    for j in range(KD):
                        last = pe.matmul(ps_g[t % 2][:].rearrange("p (k f) -> p k f", k=2), keep["h2T"][:, j, t * P:(t + 1) * P],
                                         wgu[:, :, j * FS:(j + 1) * FS], start=(j == 0), stop=(j == KD - 1))
                    last.then_inc(gu_done, 1)
                if t >= 1:
                    n = t - 1
                    pe.wait_ge(hT_kept, n + 1)
                    if n >= 2:
                        pe.wait_ge(t_done, n - 1)
                    for q in range(2):
                        for k in range(2):
                            last = pe.matmul(ps_y[n % 2][:, q * 512:(q + 1) * 512], hT[n % 2][:, k * P:(k + 1) * P],
                                             wd[:, k, q * 512:(q + 1) * 512], start=(k == 0), stop=(k == 1))
                    last.then_inc(down_done, 1)
                if t < NT:
                    pe.wait_ge(h_done, t + 1)
                    for k in range(2):
                        last = pe.transpose(ps_h[:, k * P:(k + 1) * P], h[t % 2][:, k * P:(k + 1) * P], keep["ident"][:])
                    last.then_inc(hT_done, 1)

        @block.scalar
        def _(act):
            for t in range(NT):
                act.wait_ge(gu_done, t + 1)
                if t >= 2:
                    act.wait_ge(h_done, t - 1)
                act.activation(s[t % 2][:], ps_g[t % 2][:, 0:FS], ACT.Silu).then_inc(silu_done, 1)
                act.wait_ge(hT_done, t + 1)
                if t >= 2:
                    act.wait_ge(down_done, t - 1)
                act.activation(hT[t % 2][:], ps_h[:, 0:FS], ACT.Copy).then_inc(hT_kept, 1)

        @block.gpsimd
        def _(pool):
            for t in range(NT):
                pool.wait_ge(t_done, t + 1)
                pool.tensor_tensor(keep["x1"][:, t, :], keep["x1"][:, t, :], t6[:], ALU.add).then_inc(x_done, 1)

        @block.vector
        def _(dve):
            for t in range(NT + 1):
                if t < NT:
                    dve.wait_ge(silu_done, t + 1)
                    if t >= 2:
                        dve.wait_ge(hT_done, t - 1)
                    dve.tensor_tensor(h[t % 2][:], s[t % 2][:], ps_g[t % 2][:, FS:2 * FS], ALU.mult).then_inc(h_done, 1)
                if t >= 1:
                    n = t - 1
                    dve.wait_ge(down_done, n + 1)
                    if n >= 1:
                        dve.wait_ge(x_done, n)
                    dve.tensor_tensor(t6[:], ps_y[n % 2][:], keep["g2"][:, cond_of(n), :], ALU.mult).then_inc(t_done, 1)


def combine(nc, dram, keep):
    with ExitStack() as ctx:
        def sb(name, shape, dt=F32):
            return ctx.enter_context(nc.sbuf_tensor(name, shape, dt))

        def sem(name):
            return nc.alloc_semaphore(name)

        NB = 2
        H = D // 2
        y8 = [sb(f"y8_{i}", [P, TOPK, D]) for i in range(NB)]
        r = [sb(f"r7_{i}", [P, D]) for i in range(2)]
        out = [sb(f"out7_{i}", [P, D]) for i in range(2)]
        fg = sb("fg", [P, D])
        ssq = sb("ssq7", [P, NT])
        std = sb("std7", [P, NT])
        rstd = sb("rstd7", [P, NT])
        ps_r = [ctx.enter_context(nc.psum_tensor(f"ps_r7_{i}", [P, 512], F32)) for i in range(2)]
        y_in, fg_in = [sem(f"y8_in{i}") for i in range(NB)], sem("fg_in")
        sum_pe, sum_dve, g_done, x_done, ssq_done, std_done, rstd_done, out_done = (
            sem("sum_pe"), sem("sum_dve"), sem("g7_done"), sem("x7_done"), sem("ssq7_done"), sem("std7_done"), sem("rstd7_done"), sem("out7_done"))
        stored = [sem(f"stored{i}") for i in range(2)]
        block = ctx.enter_context(nc.Block())

        @block.sync
        def _(sp):
            sp.dma_start(fg[:], dram["final_g"].to_broadcast([P, D])).then_inc(fg_in, 16)
            for t in range(NT):
                if t >= NB:
                    sp.wait_ge(sum_pe, t - NB + 1)
                    sp.wait_ge(sum_dve, t - NB + 1)
                sp.dma_start(y8[t % NB][:].rearrange("p j n -> p (j n)"),
                             dram["y"][t * P * TOPK:(t + 1) * P * TOPK, :].rearrange("(p j) n -> p (j n)", j=TOPK)).then_inc(y_in[t % NB], 16)

        @block.tensor
        def _(pe):
            for t in range(NT):
                pe.wait_ge(y_in[t % NB], 16 * (t // NB + 1))
                if t >= 2:
                    pe.wait_ge(g_done, t - 1)
                for j in range(TOPK):
                    last = pe.matmul(ps_r[t % 2][:], keep["ident"][:], y8[t % NB][:, j, 0:H], start=(j == 0), stop=(j == TOPK - 1))
                last.then_inc(sum_pe, 1)

        @block.vector
        def _(dve):
            dve.wait_ge(fg_in, 16)

            def total(t):
                dve.wait_ge(y_in[t % NB], 16 * (t // NB + 1))
                if t >= 2:
                    dve.wait_ge(x_done, t - 1)
                dve.tensor_reduce(r[t % 2][:, H:D], y8[t % NB][:, :, H:D].rearrange("p j n -> p n j"), AX.X, ALU.add).then_inc(sum_dve, 1)
                dve.wait_ge(sum_dve, t + 1)
                g2 = keep["g2"][:, cond_of(t), :]
                dve.wait_ge(sum_pe, t + 1)
                dve.tensor_tensor(r[t % 2][:, 0:H], ps_r[t % 2][:], g2[:, 0:H], ALU.mult)
                dve.tensor_tensor(r[t % 2][:, H:D], r[t % 2][:, H:D], g2[:, H:D], ALU.mult).then_inc(g_done, 1)

            def norm(t):
                dve.wait_ge(std_done, t + 1)
                dve.reciprocal(rstd[:, t:t + 1], std[:, t:t + 1]).then_inc(rstd_done, 1)
                dve.wait_ge(rstd_done, t + 1)
                dve.scalar_tensor_tensor(out=out[t % 2][:], in0=keep["x1"][:, t, :], scalar=rstd[:, t:t + 1], in1=fg[:],
                                         op0=ALU.mult, op1=ALU.mult).then_inc(out_done, 1)

            for t in range(NT + 1):
                if t < NT:
                    total(t)
                if t >= 1:
                    norm(t - 1)

        @block.gpsimd
        def _(pool):
            for t in range(NT):
                pool.wait_ge(g_done, t + 1)
                pool.tensor_tensor(keep["x1"][:, t, :], keep["x1"][:, t, :], r[t % 2][:], ALU.add).then_inc(x_done, 1)

        @block.scalar
        def _(act):
            nc.scalar.preload_act_table_set("sqrt_and_others")
            for t in range(NT):
                act.wait_ge(x_done, t + 1)
                if t >= 2:
                    act.wait_ge(stored[t % 2], 16 * (t // 2))
                act.activation(out[t % 2][:], keep["x1"][:, t, :], ACT.Square, accum_out=ssq[:, t:t + 1]).then_inc(ssq_done, 1)
                act.wait_ge(ssq_done, t + 1)
                act.activation(std[:, t:t + 1], ssq[:, t:t + 1], ACT.Sqrt, scale=1.0 / D, bias=keep["eps"][:]).then_inc(std_done, 1)
                if t >= 1:
                    act.wait_ge(out_done, t)
                    act.dma_start(dram["y_out"](t - 1), out[(t - 1) % 2][:]).then_inc(stored[(t - 1) % 2], 16)
            act.wait_ge(out_done, NT)
            act.dma_start(dram["y_out"](NT - 1), out[(NT - 1) % 2][:]).then_inc(stored[(NT - 1) % 2], 16)
            act.wait_ge(stored[0], 16 * 5)
            act.wait_ge(stored[1], 16 * 4)


def program(nc, dram, debug=()):
    with ExitStack() as ctx:
        def sb(name, shape, dt=F32):
            return ctx.enter_context(nc.sbuf_tensor(name, shape, dt))

        keep = {
            "ident": sb("ident", [P, P]),
            "eps": sb("eps", [P, 1]),
            "vcol": sb("vcol", [P, V_ROWS]),
            "mod": sb("mod", [P, 48, 2]),
        }
        dram["h2"] = nc.dram_tensor("h2_rows", (T, D), F32, kind="Internal").ap()
        dram["y"] = nc.dram_tensor("pair_rows", (T * TOPK, D), F32, kind="Internal").ap()
        dram["table"] = nc.dram_tensor("slot_table", (P * TAB, 4), I32, kind="Internal").ap()
        dram["block_expert"] = nc.dram_tensor("block_expert", (2 * P,), I32, kind="Internal").ap()

        def stage(build):
            with nc.cleanup_on_exit():
                build(nc, dram, keep)

        with ExitStack() as mixer:
            def sb(name, shape, dt=F32):
                return mixer.enter_context(nc.sbuf_tensor(name, shape, dt))

            keep["mix"] = sb("mix", [P, 2 * NT * 512])
            keep["gg"] = keep["mix"][:, 0:NT * 512].rearrange("p (t n) -> p t n", n=512)
            keep["qs"] = keep["mix"][:, NT * 512:].rearrange("p (t n) -> p t n", n=512)
            with ExitStack() as inner:
                def sb(name, shape, dt=F32):
                    return inner.enter_context(nc.sbuf_tensor(name, shape, dt))

                keep["vg"] = sb("vg", [P, NT, 512])
                keep["kv"] = sb("kv", [P, NT, 256])
                keep["qkT"] = sb("qkT", [P, 4, T])
                keep["loraT"] = sb("loraT", [32, T])
                stage(project)
                stage(linear_attention)
                stage(window_attention)
            with ExitStack() as late:
                def sb(name, shape, dt=F32):
                    return late.enter_context(nc.sbuf_tensor(name, shape, dt))

                keep["logit"] = sb("logit", [P, NT, NE])
                keep["tab"] = sb("tab", [P, TAB, 4], I32)
                keep["bexp"] = sb("bexp", [1, 2 * P], I32)
                keep["bend"] = sb("bend", [1, NE + 2], I32)
                keep["g2"] = sb("g2_rows", [P, 2, D])
                keep["x1"] = sb("x1", [P, NT, D])
                with nc.sbuf_tensor("h2T", [P, KD, T], F32) as h2T:
                    keep["h2T"] = h2T
                    stage(project_out)
                    stage(route)
                    stage(shared_expert)
                stage(experts)
                stage(combine)
                dump(nc, dram, keep, debug)


def dump(nc, dram, keep, debug):
        if debug:
            with nc.semaphore("dbg") as dbg, nc.Block() as block:
                @block.sync
                def _(sp):
                    for n in debug:
                        sp.dma_start(dram["dbg_" + n], keep[n][:]).then_inc(dbg, 16)
                    sp.wait_ge(dbg, 16 * len(debug))


def rope_table():
    import numpy as np

    quarter, grid_w = 16, 64
    inv_freq = (np.float32(10000.0) ** (-np.arange(quarter, dtype=np.float32) / quarter)).astype(np.float32)
    pos = np.arange(8 * P)
    table = np.zeros((8 * P, 2, 2, 2, quarter), np.float32)
    for half, at in enumerate((pos // grid_w, pos % grid_w)):
        ang = at.astype(np.float32)[:, None] * inv_freq[None, :]
        table[:, 0, half, :, :] = np.cos(ang)[:, None, :]
        table[:, 1, half, 0, :] = -np.sin(ang)
        table[:, 1, half, 1, :] = np.sin(ang)
    return np.ascontiguousarray(table.reshape(8, P, 2, 64).transpose(1, 0, 2, 3))


def band_table():
    import numpy as np

    t, s = np.arange(P)[:, None], np.arange(P)[None, :]
    band = np.zeros((P, 896), np.float32)
    band[:, P:2 * P] = np.where(s >= t, 0.0, -1e30)
    band[:, 3 * P:4 * P] = band[:, 6 * P:] = np.where(s <= t, 0.0, -1e30)
    return band


def kernel(**inputs):
    import numpy as np
    import concourse.bacc as bacc
    from concourse.bass_utils import run_bass_kernel_spmd

    debug = inputs.pop("_debug", {})
    a = {k: np.asarray(v) for k, v in inputs.items()}
    rows = [a["c_ctx"].reshape(8, P), a["c"].reshape(8, P), a["norm_attn_g"].reshape(8, P), a["norm_ffn_g"].reshape(8, P),
            a["b_ada"].reshape(48, P), a["gla_ba_f"].reshape(2, P), a["gla_ba_b"].reshape(2, P)]
    host = {
        "vectors": np.concatenate(rows),
        "ident": np.eye(P, dtype=np.float32),
        "gla_wa_f": a["gla_wa_f"][0], "gla_wa_b": a["gla_wa_b"][0], "gla_norm_g": a["gla_norm_g"],
        "gla_mask": np.stack([np.triu(np.ones((P, P))), np.tril(np.ones((P, P)))], 1).astype(np.int32),
        "state_f": a["state_gla_fwd"].reshape(256, P), "state_b": a["state_gla_bwd"].reshape(256, P),
        "cache_k": a["cache_swa_k"].reshape(P, P), "cache_v": a["cache_swa_v"].reshape(P, P),
        "sink": a["swa_sink"], "rope": rope_table(), "band": band_table(),
        "w_out": a["w_out"][0], "router_w": a["router_w"][0], "router_bias": a["router_bias"],
        "before": np.tril(np.ones((8, 8), np.float32), -1).reshape(1, 64),
        "upper": np.triu(np.ones((P, P), np.float32), 1),
        "blk": np.arange(2 * P, dtype=np.float32).reshape(P, 2),
        "thr": (P * np.arange(1, 9, dtype=np.float32)).reshape(1, 8),
        "tok8": (8 * np.arange(T).reshape(NT, P).T[:, :, None] + np.arange(8)).astype(np.int32),
        "fill": np.tile(np.array([NOWHERE, NOWHERE, 0, 0], np.int32), TAB).reshape(1, TAB * 4),
        "exp_w_gate": a["exp_w_gate"].reshape(NE * D, FF), "exp_w_up": a["exp_w_up"].reshape(NE * D, FF),
        "exp_w_down": a["exp_w_down"].reshape(NE * FF, D),
        "sh_w_gate": a["sh_w_gate"][0], "sh_w_up": a["sh_w_up"][0], "sh_w_down": a["sh_w_down"][0],
        "final_g": a["final_norm_g"].reshape(1, D),
        "xp": a["x_prompt"].reshape(P, D), "xs": a["x_sample"].reshape(8 * P, D),
        "w_ada": a["w_ada"][0], "w_in": a["w_in"][0],
    }
    outs = [("yp", (P, D)), ("ys", (8 * P, D)), ("new_k", (P, P)), ("new_v", (P, P)), ("new_f", (256, P)), ("new_b", (256, P))]
    nc = bacc.Bacc("TRN2", target_bir_lowering=False, num_devices=1)
    dram = {n: nc.dram_tensor("in_" + n, x.shape, mybir.dt.from_np(x.dtype), kind="ExternalInput").ap() for n, x in host.items()}
    dram["x"] = lambda t: dram["xp"] if t == 0 else dram["xs"][(t - 1) * P:t * P, :]
    for n, s in outs + [("dbg_" + n, s) for n, s in debug.items()]:
        dram[n] = nc.dram_tensor("out_" + n, s, I32 if n in ("dbg_tab", "dbg_bexp", "dbg_bend") else F32, kind="ExternalOutput").ap()
    dram["y_out"] = lambda t: dram["yp"] if t == 0 else dram["ys"][(t - 1) * P:t * P, :]
    program(nc, dram, tuple(debug))
    r = run_bass_kernel_spmd(nc, [{"in_" + n: x for n, x in host.items()}], core_ids=[0]).results[0]
    if debug:
        return tuple(r["out_dbg_" + n] for n in debug) + ((r["out_new_f"], r["out_new_b"]) if "gg" in debug and "mod" not in debug else ())
    shapes = [(1, P, D), (1, 8 * P, D), (1, 1, P, 2, 64), (1, 1, P, 2, 64), (1, 1, 4, DK, DV), (1, 1, 4, DK, DV)]
    return tuple(r["out_" + n].reshape(s) for (n, _), s in zip(outs, shapes))
```

```python
from contextlib import ExitStack

import concourse.bass as bass
from concourse import mybir

F32 = mybir.dt.float32
BF16 = mybir.dt.bfloat16
I32 = mybir.dt.int32
ALU = mybir.AluOpType
ACT = mybir.ActivationFunctionType
AX = mybir.AxisListType

P = 128
D = 1024
KD = D // P
NT = 9
T = NT * P
EPS = 1e-6
HEADS = 4
DK, DV = 64, 128
FF = 128
FS = 256
NE = 64
TOPK = 8

C_QK, C_VG, C_GG, C_LORA, C_QS, C_KV = (0, 512), (512, 512), (1024, 512), (1536, 32), (1568, 512), (2080, 256)

V_CTX, V_C, V_NA, V_NF, V_BADA, V_BAF, V_BAB, V_ROWS = 0, 8, 16, 24, 32, 80, 82, 84


def cond_of(t):
    return 0 if t == 0 else 1


def project(nc, dram, keep):
    with ExitStack() as ctx:
        def sb(name, shape, dt=F32):
            return ctx.enter_context(nc.sbuf_tensor(name, shape, dt))

        def sem(name):
            return nc.alloc_semaphore(name)

        RING = 3
        vec = sb("vec", [V_ROWS, P])
        condT = keep["condT"]
        modA1 = sb("modA1", [P, KD, 2])
        row = [sb(f"ada_row{i}", [2, 512]) for i in range(2)]
        ring = [sb(f"wring{i}", [P, KD, 512]) for i in range(RING)]
        NX = 3
        xin = sb("xin", [P, NX, D])
        xn = sb("xn", [P, 2, D])
        junk = sb("junk", [P, D])
        ssq = sb("ssq", [P, NT])
        std = sb("std", [P, NT])
        rstd = sb("rstd", [P, NT])
        hT = sb("hT", [P, KD, T])
        psA = ctx.enter_context(nc.psum_tensor("psA", [P, 512], F32))
        psT = ctx.enter_context(nc.psum_tensor("psT", [P, 2, D], F32))
        NB = 3
        psP = ctx.enter_context(nc.psum_tensor("psP", [P, NB, 512], F32))
        modps = psA[:, 0:96].rearrange("p (c k) -> p c k", k=2)
        vecps = psA[:, 128:128 + V_ROWS]

        vec_in, ident_in, x_in = sem("vec_in"), sem("ident_in"), [sem(f"x_in{i}") for i in range(NX)]
        ring_in = [sem(f"ring_in{i}") for i in range(RING)]
        ada_done, row_kept, row_turned = sem("ada_done"), sem("ada_row_kept"), sem("ada_row_turned")
        vecT_done, vec_cols, cond_done = sem("vecT_done"), sem("vec_cols"), sem("cond_done")
        modA_done, mod_cols = sem("modA_done"), sem("mod_cols")
        ssq_done, std_done, rstd_done, xn_done = sem("ssq_done"), sem("std_done"), sem("rstd_done"), sem("xn_done")
        xT_done, hT_act, hT_dve = sem("xT_done"), sem("hT_act"), sem("hT_dve")
        proj_done, evac_act, evac_dve = sem("proj_done"), sem("evac_act"), sem("evac_dve")
        out_done = sem("kv_out_done")

        w_ada = dram["w_ada"].rearrange("(j p) n -> p j n", p=P)
        w_in = dram["w_in"].rearrange("(j p) n -> p j n", p=P)
        items = [("ada", i) for i in range(4)]
        items += [("qk", C_QK), ("lora", C_LORA), ("vg", C_VG), ("gg", C_GG), ("qs", C_QS), ("kv", C_KV)]

        def landed(eng, n):
            eng.wait_ge(ring_in[n % RING], 16 * (n // RING + 1))

        outs = []
        for kind, what in items:
            if kind in ("qk", "lora"):
                for g in range(3):
                    for m in range(4 if kind == "qk" else 1):
                        outs.append((kind, m, g))
            elif kind != "ada":
                for t in range(NT):
                    outs.append((kind, 0, t))

        def used(eng, n):
            if items[n][0] == "ada":
                eng.wait_ge(ada_done, items[n][1] + 1)
            else:
                eng.wait_ge(proj_done, max(k for k, o in enumerate(outs) if o[0] == items[n][0]) + 1)

        def dest(kind, m, t):
            if kind == "qk":
                return keep["qkT"][:, m, t * 384:(t + 1) * 384]
            if kind == "lora":
                return keep["loraT"][:, t * 384:(t + 1) * 384]
            if kind == "qs":
                return keep["qs"][:, t, :].rearrange("p (r g d) -> p g r d", r=4, g=2)
            return keep[kind][:, t, :]

        def source(kind, k):
            if kind == "lora":
                return psP[0:32, k % NB, 0:384]
            if kind == "qs":
                return psP[:, k % NB, :].rearrange("p (g r d) -> p g r d", r=4, g=2)
            return psP[:, k % NB, 0:{"qk": 384, "kv": 256}.get(kind, 512)]

        def by_act(k):
            return outs[k][0] == "gg" or k % 2 == 0

        def evacs_before(k, act):
            return sum(1 for i in range(k) if by_act(i) == act)

        block = ctx.enter_context(nc.Block())

        @block.sync
        def _(sp):
            for n, (kind, what) in enumerate(items):
                if n == 0:
                    sp.dma_start(vec[:], dram["vectors"]).then_inc(vec_in, 16)
                    sp.dma_start(keep["ident"][:], dram["ident"]).then_inc(ident_in, 16)
                if n >= RING:
                    used(sp, n - RING)
                c0, cn = (what * 512, 512) if kind == "ada" else what
                src = w_ada if kind == "ada" else w_in
                sp.dma_start(ring[n % RING][:, :, 0:cn], src[:, :, c0:c0 + cn]).then_inc(ring_in[n % RING], 16)
                if n == 1:
                    for t in range(NX):
                        sp.dma_start(xin[:, t, :], dram["x"](t)).then_inc(x_in[t], 16)
                if n == 4:
                    for t in range(NX, NT):
                        sp.wait_ge(xn_done, t - NX + 1)
                        sp.dma_start(xin[:, t % NX, :], dram["x"](t)).then_inc(x_in[t % NX], 16)
            kv0 = outs.index(("kv", 0, 0))
            sp.wait_ge(evac_act if by_act(kv0) else evac_dve, evacs_before(kv0 + 1, by_act(kv0)))
            sp.dma_start(dram["new_k"], keep["kv"][:, 0, 0:128]).then_inc(out_done, 16)
            sp.dma_start(dram["new_v"], keep["kv"][:, 0, 128:256]).then_inc(out_done, 16)
            sp.wait_ge(out_done, 32)

        @block.tensor
        def _(pe):
            pe.wait_ge(vec_in, 16)
            pe.wait_ge(ident_in, 16)
            pe.transpose(vecps, vec[:], keep["ident"][0:V_ROWS, 0:V_ROWS]).then_inc(vecT_done, 1)

            def ada(n, i):
                landed(pe, n)
                if i >= 2:
                    pe.wait_ge(row_kept, i - 1)
                for j in range(KD):
                    last = pe.matmul(psT[0:2, i % 2, 0:512], condT[:, j, :], ring[n % RING][:, j, :],
                                     start=(j == 0), stop=(j == KD - 1))
                last.then_inc(ada_done, 1)

            def turn_row(i):
                pe.wait_ge(row_kept, i + 1)
                for c in range(4):
                    last = pe.transpose(modps[:, 4 * i + c, :], row[i % 2][:, c * P:(c + 1) * P], keep["ident"][0:2, 0:2])
                last.then_inc(row_turned, 1)

            def xT(t):
                pe.wait_ge(xn_done, t + 1)
                if t >= 2:
                    pe.wait_ge(hT_act, t - 1)
                    pe.wait_ge(hT_dve, t - 1)
                for j in range(KD):
                    last = pe.transpose(psT[:, t % 2, j * P:(j + 1) * P], xn[:, t % 2, j * P:(j + 1) * P], keep["ident"][:])
                last.then_inc(xT_done, 1)

            TURNED_BEFORE = {0: range(5), 1: (5, 6), 2: (7, 8)}
            k = 0
            for n, (kind, what) in enumerate(items):
                if kind == "ada":
                    if n == 0:
                        pe.wait_ge(cond_done, 1)
                    ada(n, what)
                    if what % 4:
                        turn_row(what - 1)
                    if what == 3:
                        turn_row(what)
                    continue
                landed(pe, n)
                w = ring[n % RING]
                for kk in range(k, len(outs)):
                    if outs[kk][0] != kind:
                        break
                    _, m, t = outs[kk]
                    for tile in TURNED_BEFORE.get(kk, ()):
                        xT(tile)
                    if kind == "qk":
                        pe.wait_ge(hT_act, 3 * t + 3)
                        pe.wait_ge(hT_dve, 3 * t + 3)
                    if kk >= NB:
                        a = by_act(kk - NB)
                        pe.wait_ge(evac_act if a else evac_dve, evacs_before(kk - NB + 1, a))
                    for j in range(KD):
                        bank = psP[:, kk % NB, 0:512] if kind == "qs" else source(kind, kk)
                        if kind in ("qk", "lora"):
                            width = P if kind == "qk" else 32
                            last = pe.matmul(bank, w[:, j, m * P:m * P + width],
                                             hT[:, j, t * 384:(t + 1) * 384], start=(j == 0), stop=(j == KD - 1))
                        else:
                            last = pe.matmul(bank, hT[:, j, t * P:(t + 1) * P],
                                             w[:, j, 0:what[1]], start=(j == 0), stop=(j == KD - 1))
                    last.then_inc(proj_done, 1)
                    k = kk + 1

        def scale_of(kind, m):
            return DK ** -0.5 if kind == "qk" and m < 2 else 1.0

        def hT_half(act, t):
            act.wait_ge(xT_done, t + 1)
            if t == 0:
                act.wait_ge(modA_done, 1)
            c = cond_of(t)
            for j in range(4, KD):
                last = act.activation(hT[:, j, t * P:(t + 1) * P], psT[:, t % 2, j * P:(j + 1) * P], ACT.Identity,
                                      scale=modA1[:, j, c:c + 1], bias=keep["mod"][:, j, c:c + 1])
            last.then_inc(hT_act, 1)

        @block.scalar
        def _(act):
            act.wait_ge(vec_cols, 2)
            act.activation(condT[:].rearrange("p j k -> p k j"),
                           keep["vcol"][:, 0:16].rearrange("p (k j) -> p k j", k=2), ACT.Silu).then_inc(cond_done, 1)
            for t in range(NT):
                act.wait_ge(x_in[t % NX], 16 * (t // NX + 1))
                if t >= 1:
                    act.wait_ge(ssq_done, t)
                act.activation(junk[:], xin[:, t % NX, :], ACT.Square, accum_out=ssq[:, t:t + 1]).then_inc(ssq_done, 1)
                act.wait_ge(ssq_done, t + 1)
                act.activation(std[:, t:t + 1], ssq[:, t:t + 1], ACT.Sqrt, scale=1.0 / D,
                               bias=keep["eps"][:]).then_inc(std_done, 1)
                if t >= 2:
                    hT_half(act, t - 2)
            hT_half(act, NT - 2)
            hT_half(act, NT - 1)
            for k, (kind, m, t) in enumerate(outs):
                if by_act(k):
                    act.wait_ge(proj_done, k + 1)
                    act.activation(dest(kind, m, t), source(kind, k), ACT.Silu if kind == "gg" else ACT.Copy,
                                   scale=scale_of(kind, m)).then_inc(evac_act, 1)

        @block.vector
        def _(dve):
            dve.memset(keep["eps"][:], EPS).then_inc(vec_cols, 1)
            dve.wait_ge(vecT_done, 1)
            dve.tensor_copy(keep["vcol"][:], vecps).then_inc(vec_cols, 1)

            def norm(t):
                dve.wait_ge(std_done, t + 1)
                dve.reciprocal(rstd[:, t:t + 1], std[:, t:t + 1]).then_inc(rstd_done, 1)
                dve.wait_ge(rstd_done, t + 1)
                if t >= 2:
                    dve.wait_ge(xT_done, t - 1)
                dve.tensor_scalar(xn[:, t % 2, :], xin[:, t % NX, :], rstd[:, t:t + 1], None, ALU.mult).then_inc(xn_done, 1)

            def hT_low(t):
                dve.wait_ge(xT_done, t + 1)
                c = cond_of(t)
                for j in range(4):
                    last = dve.tensor_scalar(hT[:, j, t * P:(t + 1) * P], psT[:, t % 2, j * P:(j + 1) * P],
                                             modA1[:, j, c:c + 1], keep["mod"][:, j, c:c + 1], ALU.mult, ALU.add)
                last.then_inc(hT_dve, 1)

            def keep_row(i):
                dve.wait_ge(ada_done, i + 1)
                if i >= 2:
                    dve.wait_ge(row_turned, i - 1)
                dve.tensor_copy(row[i % 2][:], psT[0:2, i % 2, 0:512]).then_inc(row_kept, 1)

            norm(0)
            norm(1)
            for i in range(4):
                keep_row(i)
            dve.wait_ge(row_turned, 4)
            dve.wait_ge(vec_cols, 2)
            bada = keep["vcol"][:, V_BADA:V_BADA + 48]
            dve.tensor_tensor(keep["mod"][:, 0:16, :], modps[:, 0:16, :],
                              bada[:, 0:16].unsqueeze(2).to_broadcast([P, 16, 2]), ALU.add).then_inc(mod_cols, 1)
            dve.wait_ge(mod_cols, 1)
            dve.scalar_tensor_tensor(out=modA1[:], in0=keep["mod"][:, 8:16, :], scalar=1.0,
                                     in1=keep["vcol"][:, V_NA:V_NA + 8].unsqueeze(2).to_broadcast([P, KD, 2]),
                                     op0=ALU.add, op1=ALU.mult).then_inc(modA_done, 1)
            dve.wait_ge(modA_done, 1)
            for t in range(2, NT):
                norm(t)
                hT_low(t - 2)
            hT_low(NT - 2)
            hT_low(NT - 1)
            for k, (kind, m, t) in enumerate(outs):
                if not by_act(k):
                    dve.wait_ge(proj_done, k + 1)
                    dve.tensor_scalar(dest(kind, m, t), source(kind, k), scale_of(kind, m), None,
                                      ALU.mult).then_inc(evac_dve, 1)


def linear_attention(nc, dram, keep):
    with ExitStack() as ctx:
        def sb(name, shape, dt=F32):
            return ctx.enter_context(nc.sbuf_tensor(name, shape, dt))

        def ps(name, shape):
            return ctx.enter_context(nc.psum_tensor(name, shape, F32))

        def sem(name):
            return nc.alloc_semaphore(name)

        G = 3
        W = G * P
        NG = NT // G
        UNITS = [(g, m) for g in range(NG) for m in range(4)]
        NU = len(UNITS)
        CAP = 80.0 * 16.0

        wab = sb("wab", [32, 512])
        restart = sb("restart", [P, W])
        mask = sb("gla_mask", [P, 2, P], I32)
        normg = sb("normg", [P, P])
        ab = sb("ab", [P, W])
        ex = lg = ab
        mn = sb("mn", [P, W])
        la = sb("la", [P, W])
        tmp = mn
        cum = sb("cum", [P, 2, W])
        fac = [sb(f"fac{i}", [P, 7, W]) for i in range(2)]
        (F64, F32L, F16, FQD, FKD, FQI, FKS) = range(7)
        pr = [sb(f"pr{i}", [P, 4, W]) for i in range(2)]
        kz = [sb(f"kz{i}", [P, 3, W]) for i in range(4)]
        ksT = [sb(f"ksT{i}", [P, W]) for i in range(2)]
        ks = [sb(f"ks{i}", [P, G, P]) for i in range(2)]
        qi = sb("qi", [P, 4, T])
        elast = sb("elast", [P, 4, NT])
        AT = [sb(f"AT{m}", [P, G, 2, P]) for m in range(4)]
        S = sb("S", [P, 4, NT, P])
        S0 = sb("S0", [P, 4, P])
        osum = [AT[i][:].rearrange("p i h t -> p (i h t)")[:, 0:512] for i in range(2)]
        sq = AT[2][:].rearrange("p i h t -> p (i h t)")[:, 0:512]
        ms = sb("gla_ms", [P, NT, 4])
        lnm = sb("gla_lnm", [P, NT, 4])
        rs = sb("gla_rs", [P, NT, 4])

        ps_pre = ps("ps_pre", [P, 512])
        ps_a = [ps(f"ps_a{i}", [P, 2, 512]) for i in range(2)]
        ps_t = ps("ps_kt", [P, 512])
        ps_d = ps("ps_d", [P, 512])
        ps_o = ps("ps_o", [P, 512])
        ps_i = [ps_a[i][:, :, 0:2 * DV].rearrange("p h (m v) -> p h m v", v=DV) for i in range(2)]

        const_in, zeroed = sem("gla_const_in"), sem("gla_zeroed")
        pre_done, soft_done, cum_done, dif_done = sem("pre_done"), sem("soft_done"), sem("cum_done"), sem("dif_done")
        act_step, dve_step = sem("gla_act_step"), sem("gla_dve_step")
        fac_done, prod_done = sem("fac_done"), sem("prod_done")
        score_done, kst_done, at_done, ks_done = sem("score_done"), sem("kst_done"), sem("at_done"), sem("ks_done")
        delta_done, s_done, pv_done, intra_done = sem("delta_done"), sem("s_done"), sem("pv_done"), sem("intra_done")
        rec_done, inter_done, osum_done = sem("rec_done"), sem("inter_done"), sem("osum_done")
        sq_done, rs_done, gate_done, out_ready, gla_done = sem("sq_done"), sem("rs_done"), sem("gate_done"), sem("out_ready"), sem("gla_done")
        state_out = sem("state_out")

        def halves(ap, b):
            v = ap.rearrange("p (n h b) -> p n h b", h=2, b=b)
            return v[:, :, 0, :], v[:, :, 1, :]

        def sides(ap, b, m):
            lo, hi = halves(ap, b)
            return (hi, lo) if m < 2 else (lo, hi)

        block = ctx.enter_context(nc.Block())

        @block.sync
        def _(sp):
            sp.wait_ge(zeroed, 1)
            sp.dma_start(wab[0:16, 0:256], dram["gla_wa_f"]).then_inc(const_in, 16)
            sp.dma_start(wab[16:32, 256:512], dram["gla_wa_b"]).then_inc(const_in, 16)
            sp.dma_start(mask[:], dram["gla_mask"]).then_inc(const_in, 16)
            sp.dma_start(normg[:], dram["gla_norm_g"].to_broadcast([P, P])).then_inc(const_in, 16)
            sp.dma_start(S0[:, 0:2, :], dram["state_f"].rearrange("(m p) v -> p m v", p=P)).then_inc(const_in, 16)
            sp.dma_start(S0[:, 2:4, :], dram["state_b"].rearrange("(m p) v -> p m v", p=P)).then_inc(const_in, 16)
            sp.wait_ge(s_done, 4)
            sp.dma_start(dram["new_f"].rearrange("(m p) v -> p m v", p=P), S[:, 0:2, 0, :]).then_inc(state_out, 16)
            sp.dma_start(dram["new_b"].rearrange("(m p) v -> p m v", p=P), S[:, 2:4, 0, :]).then_inc(state_out, 16)
            sp.wait_ge(state_out, 32)

        @block.tensor
        def _(pe):
            def pre(u):
                g, m = UNITS[u]
                if u >= 1:
                    pe.wait_ge(soft_done, u)
                    pe.wait_ge(cum_done, u)
                else:
                    pe.wait_ge(const_in, 96)
                pe.matmul(ps_pre[:, 0:W], wab[:, m * P:(m + 1) * P], keep["loraT"][:, g * W:(g + 1) * W],
                          start=True, stop=True).then_inc(pre_done, 1)

            def scores(u):
                g, m = UNITS[u]
                b = u % 2
                pe.wait_ge(prod_done, u + 1)
                if u >= 2:
                    pe.wait_ge(at_done, u - 1)
                z = kz[m]
                for i in range(G):
                    for h in range(2):
                        rows = slice(DK * h, DK * h + DK)
                        tile = slice(i * P, (i + 1) * P)
                        out = ps_a[b][:, h, i * P:(i + 1) * P]
                        oq, ok = sides(out, 16, m)
                        qd = pr[b][rows, 3, tile]
                        qdq, qdk = sides(qd, 16, m)
                        q16, _ = sides(pr[b][rows, 2, tile], 16, m)
                        pe.matmul(ok, z[rows, 0, tile], qdk, start=True, stop=True)
                        pe.matmul(oq, z[rows, 1, tile], qdq, start=True, stop=False)
                        pe.matmul(oq, z[rows, 2, tile], q16, start=False, stop=True)
                        for lv, size in ((1, 32), (0, 64)):
                            for n in range(P // (2 * size)):
                                lo = slice(2 * size * n, 2 * size * n + size)
                                hi = slice(2 * size * n + size, 2 * size * (n + 1))
                                q, k = (hi, lo) if m < 2 else (lo, hi)
                                w = pr[b][rows, lv, tile]
                                last = pe.matmul(out[k, q], w[:, k], w[:, q], start=True, stop=True)
                last.then_inc(score_done, 1)

            def turn_keys(u):
                b = u % 2
                if u >= 1:
                    pe.wait_ge(ks_done, u)
                for i in range(G):
                    last = pe.transpose(ps_t[:, i * P:(i + 1) * P], ksT[b][:, i * P:(i + 1) * P], keep["ident"][:])
                last.then_inc(kst_done, 1)

            def delta(u):
                g, m = UNITS[u]
                pe.wait_ge(ks_done, u + 1)
                if u >= 1:
                    pe.wait_ge(s_done, u)
                for i in range(G):
                    for h in range(2):
                        head = 2 * (m % 2) + h
                        last = pe.matmul(ps_d[DK * h:DK * h + DK, i * P:(i + 1) * P], ks[u % 2][:, i, DK * h:DK * h + DK],
                                         keep["vg"][:, g * G + i, head * DV:(head + 1) * DV], start=True, stop=True)
                last.then_inc(delta_done, 1)

            def intra(g):
                pe.wait_ge(at_done, 4 * g + 4)
                for i in range(G):
                    t = g * G + i
                    if t >= 1:
                        pe.wait_ge(intra_done, t)
                    for head in range(HEADS):
                        for d in range(2):
                            last = pe.matmul(ps_o[:, head * DV:(head + 1) * DV], AT[2 * d + head // 2][:, i, head % 2, :],
                                             keep["vg"][:, t, head * DV:(head + 1) * DV], start=(d == 0), stop=(d == 1))
                    last.then_inc(pv_done, 1)

            pre(0)
            pre(1)
            pre(2)
            for u in range(NU + 1):
                if u < NU:
                    scores(u)
                    turn_keys(u)
                if u + 3 < NU:
                    pre(u + 3)
                if u >= 1:
                    delta(u - 1)
                    if UNITS[u - 1][1] == 3:
                        intra(UNITS[u - 1][0])
            for n, t in enumerate(range(1, NT)):
                pe.wait_ge(rec_done, 29)
                if n >= 2:
                    pe.wait_ge(osum_done, n - 1)
                for head in range(HEADS):
                    rows = slice(DK * (head % 2), DK * (head % 2) + DK)
                    for d in range(2):
                        m = 2 * d + head // 2
                        edge = t == (1, NT - 1)[d]
                        st = S0[rows, m, :] if edge else S[rows, m, t + (-1, 1)[d], :]
                        last = pe.matmul(ps_i[n % 2][:, head % 2, head // 2, :], qi[rows, m, t * P:(t + 1) * P], st,
                                         start=(d == 0), stop=(d == 1))
                last.then_inc(inter_done, 1)

        @block.scalar
        def _(act):
            nc.scalar.preload_act_table_set("natural_log_exp_and_others")
            steps = [0]

            def step(ins):
                steps[0] += 1
                ins.then_inc(act_step, 1)
                act.wait_ge(act_step, steps[0])

            def soft(u):
                g, m = UNITS[u]
                ba = keep["vcol"][:, V_BAF + m:V_BAF + m + 1]
                act.wait_ge(pre_done, u + 1)
                if u >= 1:
                    act.wait_ge(cum_done, u)
                step(act.activation(ab[:], ps_pre[:, 0:W], ACT.Abs, bias=ba))
                step(act.activation(ex[:], ab[:], ACT.Exp, scale=-1.0))
                act.activation(lg[:], ex[:], ACT.Ln, bias=1.0).then_inc(soft_done, 1)

            def factors(u):
                g, m = UNITS[u]
                b = u % 2
                act.wait_ge(dif_done, u + 1)
                c = 1.0 / 16.0
                step(act.activation(fac[b][:, FQD, :], fac[b][:, FKD, :], ACT.Exp, scale=c))
                for f, size in ((F64, 64), (F32L, 32), (F16, 16)):
                    fq, fk = sides(fac[b][:, f, :], size, m)
                    act.activation(fq, fq, ACT.Exp, scale=c)
                    act.activation(fk, fk, ACT.Exp, scale=-c)
                act.activation(fac[b][:, FKD, :], fac[b][:, FKD, :], ACT.Exp, scale=-c)
                act.activation(fac[b][:, FQI, :], cum[:, b, :], ACT.Exp, scale=c)
                act.activation(fac[b][:, FKS, :], fac[b][:, FKS, :], ACT.Exp, scale=c)
                end = cum[:, b, :].rearrange("p (n b) -> p n b", b=P)[:, :, (P - 1 if m < 2 else 0)]
                act.activation(elast[:, m, g * G:(g + 1) * G], end, ACT.Exp, scale=c).then_inc(fac_done, 1)

            def move_keys(u):
                act.wait_ge(kst_done, u + 1)
                if u >= 2:
                    act.wait_ge(delta_done, u - 1)
                act.activation(ks[u % 2][:].rearrange("p i k -> p (i k)"), ps_t[:, 0:W], ACT.Copy).then_inc(ks_done, 1)

            soft(0)
            soft(1)
            factors(0)
            soft(2)
            factors(1)
            for u in range(NU + 1):
                if u >= 1:
                    move_keys(u - 1)
                    if u + 2 < NU:
                        soft(u + 2)
                if u + 2 < NU:
                    factors(u + 2)
            act.wait_ge(pv_done, NT)
            for t in range(NT):
                src = keep["vg"][:, t, :] if t == 0 else osum[t % 2]
                act.wait_ge(intra_done if t == 0 else osum_done, 1 if t == 0 else t)
                for head in range(HEADS):
                    step(act.activation(sq[:, head * DV:(head + 1) * DV], src[:, head * DV:(head + 1) * DV], ACT.Square,
                                        accum_out=ms[:, t, head:head + 1]))
                step(act.activation(lnm[:, t, :], ms[:, t, :], ACT.Ln, scale=1.0 / DV, bias=keep["eps"][:]))
                act.activation(rs[:, t, :], lnm[:, t, :], ACT.Exp, scale=-0.5).then_inc(rs_done, 1)

        @block.gpsimd
        def _(pool):
            pool.memset(wab[:], 0.0).then_inc(zeroed, 1)
            for i in range(4):
                pool.memset(kz[i][:], 0.0).then_inc(zeroed, 1)
            pool.wait_ge(zeroed, 5)
            for u, (g, m) in enumerate(UNITS):
                b = u % 2
                q = keep["qkT"][:, m % 2, g * W:(g + 1) * W]
                k = keep["qkT"][:, 2 + m % 2, g * W:(g + 1) * W]
                z = kz[m]
                pool.wait_ge(fac_done, u + 1)
                if u >= 2:
                    pool.wait_ge(kst_done, u - 1)
                for lv, f, size in ((0, F64, 64), (1, F32L, 32)):
                    for src, wq in ((q, 0), (k, 1)):
                        pool.tensor_tensor(sides(pr[b][:, lv, :], size, m)[wq], sides(src, size, m)[wq],
                                           sides(fac[b][:, f, :], size, m)[wq], ALU.mult)
                pool.tensor_tensor(sides(pr[b][:, 2, :], 16, m)[0], sides(q, 16, m)[0], sides(fac[b][:, F16, :], 16, m)[0], ALU.mult)
                pool.tensor_tensor(pr[b][:, 3, :], q, fac[b][:, FQD, :], ALU.mult)
                pool.tensor_tensor(sides(z[:, 0, :], 16, m)[1], sides(k, 16, m)[1], sides(fac[b][:, FKD, :], 16, m)[1], ALU.mult)
                pool.tensor_tensor(sides(z[:, 1, :], 16, m)[0], sides(k, 16, m)[0], sides(fac[b][:, FKD, :], 16, m)[0], ALU.mult)
                pool.tensor_tensor(sides(z[:, 2, :], 16, m)[1], sides(k, 16, m)[1], sides(fac[b][:, F16, :], 16, m)[1], ALU.mult)
                pool.tensor_tensor(qi[:, m, g * W:(g + 1) * W], q, fac[b][:, FQI, :], ALU.mult)
                pool.tensor_tensor(ksT[b][:], k, fac[b][:, FKS, :], ALU.mult).then_inc(prod_done, 1)
            for t in range(NT):
                g3 = keep["gg"][:, t, :].rearrange("p (h v) -> p h v", h=HEADS)
                pool.tensor_tensor(g3, g3, normg[:].unsqueeze(1).to_broadcast([P, HEADS, DV]), ALU.mult).then_inc(gate_done, 1)

        @block.vector
        def _(dve):
            steps = [0]

            def step(ins):
                steps[0] += 1
                ins.then_inc(dve_step, 1)
                dve.wait_ge(dve_step, steps[0])

            dve.memset(restart[:], 1.0).then_inc(dve_step, 1)
            steps[0] = 1
            dve.wait_ge(dve_step, 1)
            step(dve.memset(restart[:].rearrange("p (n b) -> p n b", b=P)[:, :, 0:1], 0.0))
            for m in range(3):
                dve.memset(AT[m][:], 0.0)
            step(dve.memset(AT[3][:], 0.0))

            def cumulate(u):
                g, m = UNITS[u]
                b = u % 2
                ba = keep["vcol"][:, V_BAF + m:V_BAF + m + 1]
                dve.wait_ge(soft_done, u + 1)
                step(dve.tensor_scalar(mn[:], ps_pre[:, 0:W], ba, 0.0, ALU.add, ALU.min))
                step(dve.tensor_tensor(la[:], mn[:], lg[:], ALU.subtract))
                if u >= 2:
                    dve.wait_ge(prod_done, u - 1)
                c = cum[:, b, :]
                c3 = c.rearrange("p (n b) -> p n b", b=P)
                if m < 2:
                    dve.tensor_tensor_scan(c, restart[:], la[:], 0.0, ALU.mult, ALU.add).then_inc(cum_done, 1)
                    dve.wait_ge(cum_done, u + 1)
                else:
                    step(dve.tensor_tensor_scan(tmp[:], restart[:], la[:], 0.0, ALU.mult, ALU.add))
                    step(dve.tensor_tensor(c, la[:], tmp[:], ALU.subtract))
                    tot = tmp[:].rearrange("p (n b) -> p n b", b=P)[:, :, P - 1:P]
                    dve.tensor_tensor(c3, c3, tot.to_broadcast([P, G, P]), ALU.add).then_inc(cum_done, 1)
                    dve.wait_ge(cum_done, u + 1)
                for f, size in ((FKD, 8), (F64, 64), (F32L, 32), (F16, 16)):
                    n = 2 * size
                    cv = c.rearrange("p (n b) -> p n b", b=n)
                    at = size - 1 if m < 2 else size
                    last = dve.tensor_tensor(fac[b][:, f, :].rearrange("p (n b) -> p n b", b=n), cv,
                                             cv[:, :, at:at + 1].to_broadcast([P, W // n, n]), ALU.subtract)
                at = P - 1 if m < 2 else 0
                step(last)
                dve.tensor_tensor(fac[b][:, FKS, :].rearrange("p (n b) -> p n b", b=P),
                                  c3[:, :, at:at + 1].to_broadcast([P, G, P]), c3, ALU.subtract)
                dve.tensor_scalar(fac[b][:, FKD, :], fac[b][:, FKD, :], CAP, -CAP, ALU.min, ALU.max).then_inc(dif_done, 1)

            def keep_scores(u):
                g, m = UNITS[u]
                dve.wait_ge(score_done, u + 1)
                if u >= 4:
                    dve.wait_ge(pv_done, G * g)
                sel = mask[:, m // 2, :].unsqueeze(1).to_broadcast([P, 2, P])
                for i in range(G):
                    last = dve.copy_predicated(AT[m][:, i, :, :], sel, ps_a[u % 2][:, :, i * P:(i + 1) * P])
                last.then_inc(at_done, 1)

            def keep_delta(u):
                g, m = UNITS[u]
                dve.wait_ge(delta_done, u + 1)
                dve.tensor_copy(S[:, m, g * G:(g + 1) * G, :],
                                ps_d[:, 0:W].rearrange("p (i v) -> p i v", i=G)).then_inc(s_done, 1)

            def keep_intra(g):
                for i in range(G):
                    t = g * G + i
                    dve.wait_ge(pv_done, t + 1)
                    dve.tensor_copy(keep["vg"][:, t, :], ps_o[:]).then_inc(intra_done, 1)

            dve.wait_ge(const_in, 96)
            cumulate(0)
            cumulate(1)
            for u in range(NU + 1):
                if u + 2 < NU:
                    cumulate(u + 2)
                if u >= 1:
                    keep_delta(u - 1)
                    if UNITS[u - 1][1] == 3:
                        keep_intra(UNITS[u - 1][0])
                if u < NU:
                    keep_scores(u)
            dve.wait_ge(s_done, NU)
            done = 0
            for n in range(7):
                for m in range(4):
                    t = 1 + n if m < 2 else NT - 1 - n
                    before = S0[:, m, :] if n == 0 else S[:, m, t + (-1 if m < 2 else 1), :]
                    if n:
                        dve.wait_ge(rec_done, done - 3)
                    dve.scalar_tensor_tensor(out=S[:, m, t, :], in0=before, scalar=elast[:, m, t:t + 1], in1=S[:, m, t, :],
                                             op0=ALU.mult, op1=ALU.add).then_inc(rec_done, 1)
                    done += 1
            dve.wait_ge(rec_done, done)
            dve.memset(tmp[:, 0:1], 0.0).then_inc(rec_done, 1)

            def finish(t):
                src = keep["vg"][:, t, :] if t == 0 else osum[t % 2]
                s3 = src.rearrange("p (h v) -> p h v", h=HEADS)
                dve.wait_ge(rs_done, t + 1)
                step(dve.tensor_tensor(s3, s3, rs[:, t, :].unsqueeze(2).to_broadcast([P, HEADS, DV]), ALU.mult))
                dve.wait_ge(gate_done, t + 1)
                dve.tensor_tensor(keep["gg"][:, t, :], src, keep["gg"][:, t, :], ALU.mult).then_inc(gla_done, 1)

            for t in range(1, NT + 1):
                if t < NT:
                    dve.wait_ge(inter_done, t)
                    if t >= 3:
                        dve.wait_ge(gla_done, t - 1)
                    for h in range(2):
                        def mine(ap):
                            return ap.rearrange("p (m h v) -> p h m v", h=2, v=DV)[:, h, :, :]
                        last = dve.tensor_tensor(mine(osum[t % 2]), ps_i[(t - 1) % 2][:, h, :, :],
                                                 mine(keep["vg"][:, t, :]), ALU.add)
                    last.then_inc(osum_done, 1)
                finish(t - 1)


def window_attention(nc, dram, keep):
    with ExitStack() as ctx:
        def sb(name, shape, dt=F32):
            return ctx.enter_context(nc.sbuf_tensor(name, shape, dt))

        def ps(name, shape):
            return ctx.enter_context(nc.psum_tensor(name, shape, F32))

        def sem(name):
            return nc.alloc_semaphore(name)

        NH, HD = 8, 64
        ITEMS, RING, FIRST = 8, 3, 16
        SLOTS = 10
        SCALE = HD ** -0.5
        ck = sb("cache_k", [P, P])
        cv = sb("cache_v", [P, P])
        rope = sb("rope", [P, 8, 2, HD])
        bias = sb("band", [P, 896])
        sink = sb("sink", [P, NH])
        rq = [sb(f"rq{i}", [P, 640]) for i in range(2)]
        rt = sb("rt", [P, 640])
        kT = sb("kT", [P, SLOTS * P])
        NQ = 2
        qT = [sb(f"qT{i}", [P, 4, P]) for i in range(NQ)]
        NP_ = 4
        sc = [sb(f"sc{i}", [P, 512]) for i in range(NP_)]
        prT = [sb(f"prT{i}", [P, 512]) for i in range(2)]
        mx = sb("att_mx", [P, NT, NH])
        nmx = sb("att_nmx", [P, NT, NH])
        sm = sb("att_sm", [P, NT, NH])
        es = sb("att_es", [P, NT, NH])
        rden = sb("att_rden", [P, NT, NH])
        ring = [sb(f"ada_ring{i}", [P, KD, 512]) for i in range(RING)]
        row = sb("ada_row", [2, 512])
        ps_q = ps("ps_q", [P, 512])
        ps_k = ps("ps_k", [P, 512])
        ps_s = [ps(f"ps_s{i}", [P, 512]) for i in range(2)]
        ps_p = [ps(f"ps_p{i}", [P, 512]) for i in range(2)]
        ps_o = [ps(f"ps_ao{i}", [P, 512]) for i in range(2)]

        const_in = sem("att_const_in")
        ring_in = [sem(f"ada_ring_in{i}") for i in range(RING)]
        ada_done, row_kept, row_turned, mod_kept = sem("ada2_done"), sem("ada2_row_kept"), sem("ada2_row_turned"), sem("mod_kept")
        rope_step, rope_done = sem("rope_step"), sem("rope_done")
        kT_done, kT_kept, qT_done, qT_kept = sem("kT_done"), sem("kT_kept"), sem("qT_done"), sem("qT_kept")
        s_done, m_done, p_done, pT_done, pT_kept = sem("qk_done"), sem("max_done"), sem("p_done"), sem("pT_done"), sem("pT_kept")
        o_done, es_in, es_done, den_done, att_done, step_done = (sem("o_done"), sem("es_in"), sem("es_done"),
                                                                 sem("den_done"), sem("att_done"), sem("att_step"))

        STEPS = [(t, g * 4 + r) for t in range(NT) for r in range(4) for g in range(2)]

        def windows(t):
            if t == 0:
                return [(0, 9, 1)]
            lo, hi = max(1, t - 1), min(8, t + 1)
            return [(0, 0, 1), (P, lo, hi - lo + 1)]

        def width(t):
            return P * sum(n for _, _, n in windows(t))

        def values(slot, g):
            cols = slice(P + g * HD, P + g * HD + HD)
            if slot == 0:
                return cv[:, g * HD:(g + 1) * HD]
            return keep["kv"][:, slot % 9, cols]

        block = ctx.enter_context(nc.Block())

        @block.sync
        def _(sp):
            sp.dma_start(ck[:], dram["cache_k"]).then_inc(const_in, 16)
            sp.dma_start(cv[:], dram["cache_v"]).then_inc(const_in, 16)
            sp.dma_start(rope[:], dram["rope"]).then_inc(const_in, 16)
            sp.dma_start(bias[:], dram["band"]).then_inc(const_in, 16)
            sp.dma_start(sink[:], dram["sink"].to_broadcast([P, NH])).then_inc(const_in, 16)
            for i in range(ITEMS):
                if i >= RING:
                    sp.wait_ge(ada_done, i - RING + 1)
                c0 = FIRST * P + i * 512
                sp.dma_start(ring[i % RING][:], dram["w_ada"].rearrange("(j p) n -> p j n", p=P)[:, :, c0:c0 + 512]).then_inc(ring_in[i % RING], 16)

        @block.gpsimd
        def _(pool):
            pool.wait_ge(const_in, 80)
            for n, t in enumerate(range(1, NT)):
                if n >= 2:
                    pool.wait_ge(qT_done, n)
                    pool.wait_ge(kT_done, n + 1)
                r = rq[n % 2]
                for src, dst, heads in ((keep["qs"][:, t, :], slice(0, 512), 8), (keep["kv"][:, t, 0:128], slice(512, 640), 2)):
                    cos = rope[:, t - 1, 0, :].unsqueeze(1).to_broadcast([P, heads, HD])
                    o3 = r[:, dst].rearrange("p (h d) -> p h d", d=HD)
                    pool.tensor_tensor(o3, src.rearrange("p (h d) -> p h d", d=HD), cos, ALU.mult)
                    x4 = src.rearrange("p (h a b d) -> p h a b d", a=2, b=2, d=16)
                    t4 = rt[:, dst].rearrange("p (h a b d) -> p h a b d", a=2, b=2, d=16)
                    s4 = rope[:, t - 1, 1, :].rearrange("p (a b d) -> p a b d", a=2, b=2)
                    for b in range(2):
                        last = pool.tensor_tensor(t4[:, :, :, b, :], x4[:, :, :, 1 - b, :],
                                                  s4[:, :, b, :].unsqueeze(1).to_broadcast([P, heads, 2, 16]), ALU.mult)
                last.then_inc(rope_step, 1)
                pool.wait_ge(rope_step, n + 1)
                pool.tensor_tensor(r[:], r[:], rt[:], ALU.add).then_inc(rope_done, 1)
                pool.wait_ge(rope_done, n + 1)

        @block.tensor
        def _(pe):
            turned = [0]

            def turn_k(slot):
                if turned[0]:
                    pe.wait_ge(kT_kept, turned[0])
                src = {0: ck[:], 9: keep["kv"][:, 0, 0:P]}.get(slot)
                if src is None:
                    pe.wait_ge(rope_done, slot)
                    src = rq[(slot - 1) % 2][:, 512:640]
                pe.transpose(ps_k[:, 0:P], src, keep["ident"][:]).then_inc(kT_done, 1)
                turned[0] += 1

            def turn_q(t):
                if t == 0:
                    src = keep["qs"][:, 0, :]
                else:
                    src = rq[(t - 1) % 2][:, 0:512]
                if t >= 1:
                    pe.wait_ge(qT_kept, t)
                for r in range(4):
                    last = pe.transpose(ps_q[:, r * P:(r + 1) * P], src[:, r * P:(r + 1) * P], keep["ident"][:])
                last.then_inc(qT_done, 1)

            def scores(n):
                t, h = STEPS[n]
                g, r = h // 4, h % 4
                rows = slice(HD * g, HD * g + HD)
                pe.wait_ge(qT_kept, t + 1)
                pe.wait_ge(kT_kept, 1 if t == 0 else min(t + 3, SLOTS))
                if n >= 2:
                    pe.wait_ge(m_done, n - 1)
                for c, slot, tiles in windows(t):
                    last = pe.matmul(ps_s[n % 2][:, c:c + tiles * P], qT[t % NQ][rows, r, :],
                                     kT[rows, slot * P:(slot + tiles) * P], start=True, stop=True)
                last.then_inc(s_done, 1)

            def turn_p(n):
                t, h = STEPS[n]
                pe.wait_ge(p_done, n + 1)
                if n >= 2:
                    pe.wait_ge(pT_kept, n - 1)
                for c in range(0, width(t), P):
                    last = pe.transpose(ps_p[n % 2][:, c:c + P], sc[n % NP_][:, c:c + P], keep["ident"][:])
                last.then_inc(pT_done, 1)

            def output(n):
                t, h = STEPS[n]
                pe.wait_ge(pT_kept, n + 1)
                if n % NH == 0 and t >= 2:
                    pe.wait_ge(att_done, t - 1)
                slots = [s + i for _, s, n_ in windows(t) for i in range(n_)]
                for i, slot in enumerate(slots):
                    last = pe.matmul(ps_o[t % 2][:, h * HD:(h + 1) * HD], prT[n % 2][:, i * P:(i + 1) * P],
                                     values(slot, h // 4), start=(i == 0), stop=(i == len(slots) - 1))
                last.then_inc(o_done, 1)

            def ada(i, part):
                if part == 0:
                    pe.wait_ge(ring_in[i % RING], 16 * (i // RING + 1))
                    pe.wait_ge(kT_kept, turned[0])
                    if i:
                        pe.wait_ge(mod_kept, i)
                for j in (2 * part, 2 * part + 1):
                    last = pe.matmul(ps_k[0:2, :], keep["condT"][:, j, :], ring[i % RING][:, j, :],
                                     start=(j == 0), stop=(j == KD - 1))
                if part == 3:
                    last.then_inc(ada_done, 1)

            def turn_row(i):
                pe.wait_ge(row_kept, i + 1)
                for c in range(4):
                    last = pe.transpose(ps_k[:, 2 * c:2 * c + 2], row[:, c * P:(c + 1) * P], keep["ident"][0:2, 0:2])
                last.then_inc(row_turned, 1)

            pe.wait_ge(const_in, 80)
            turn_k(9)
            turn_q(0)
            turn_k(0)
            N = len(STEPS)
            for n in range(N + 3):
                if n < N:
                    t = STEPS[n][0]
                    if n == 0:
                        turn_k(1)
                    if n % NH == 4 and t + 1 < NT:
                        turn_q(t + 1)
                        if t + 2 < NT:
                            if t:
                                pe.wait_ge(mod_kept, t)
                            turn_k(t + 2)
                    if n % NH == 2 and t:
                        turn_row(t - 1)
                    scores(n)
                    if n % NH >= 5 and t < ITEMS:
                        ada(t, n % NH - 5)
                    if n % NH == 0 and t:
                        ada(t - 1, 3)
                if n >= 2 and n - 2 < N:
                    turn_p(n - 2)
                if n >= 3:
                    output(n - 3)

        @block.scalar
        def _(act):
            def keep_q(t):
                act.wait_ge(qT_done, t + 1)
                if t >= NQ:
                    act.wait_ge(s_done, NH * (t - NQ + 1))
                act.activation(qT[t % NQ][:].rearrange("p r t -> p (r t)"), ps_q[:], ACT.Copy).then_inc(qT_kept, 1)

            def keep_k(i, slot):
                act.wait_ge(kT_done, i + 1)
                act.activation(kT[:, slot * P:(slot + 1) * P], ps_k[:, 0:P], ACT.Copy).then_inc(kT_kept, 1)

            def probs(n):
                t, h = STEPS[n]
                act.wait_ge(m_done, n + 1)
                act.activation(sc[n % NP_][:, 0:width(t)], sc[n % NP_][:, 0:width(t)], ACT.Exp,
                               bias=nmx[:, t, h:h + 1], accum_out=sm[:, t, h:h + 1]).then_inc(p_done, 1)

            keep_k(0, 9)
            keep_q(0)
            keep_k(1, 0)
            N = len(STEPS)
            for n in range(N):
                t = STEPS[n][0]
                if n == 0:
                    keep_k(2, 1)
                if n % NH == 4 and t + 1 < NT:
                    keep_q(t + 1)
                    if t + 2 < NT:
                        keep_k(t + 3, t + 2)
                if n % NH == 1 and t:
                    act.wait_ge(ada_done, t)
                    if t > 1:
                        act.wait_ge(row_turned, t - 1)
                    act.activation(row[:], ps_k[0:2, :], ACT.Copy).then_inc(row_kept, 1)
                probs(n)
                if n % NH == NH - 1:
                    act.wait_ge(es_in, t + 1)
                    act.activation(es[:, t, :], es[:, t, :], ACT.Exp).then_inc(es_done, 1)

        @block.vector
        def _(dve):
            dve.wait_ge(const_in, 80)

            steps = [0]

            def step(ins):
                steps[0] += 1
                ins.then_inc(step_done, 1)
                dve.wait_ge(step_done, steps[0])

            def maxima(n):
                t, h = STEPS[n]
                w = width(t)
                dve.wait_ge(s_done, n + 1)
                if n >= NP_:
                    dve.wait_ge(pT_done, n - NP_ + 1)
                c = 512 if t == 1 else 0
                mask = bias[:, c:c + w]
                step(dve.tensor_tensor_reduce(sc[n % NP_][:, 0:w], ps_s[n % 2][:, 0:w], mask, SCALE, sink[:, h:h + 1],
                                              ALU.add, ALU.max, mx[:, t, h:h + 1]))
                dve.tensor_scalar(nmx[:, t, h:h + 1], mx[:, t, h:h + 1], -1.0, None, ALU.mult).then_inc(m_done, 1)

            def keep_p(n):
                t, h = STEPS[n]
                dve.wait_ge(pT_done, n + 1)
                if n >= 2:
                    dve.wait_ge(o_done, n - 1)
                dve.tensor_copy(prT[n % 2][:, 0:width(t)], ps_p[n % 2][:, 0:width(t)]).then_inc(pT_kept, 1)

            def sink_part(t):
                dve.tensor_tensor(es[:, t, :], sink[:], mx[:, t, :], ALU.subtract).then_inc(es_in, 1)

            def finish(t):
                dve.wait_ge(es_done, t + 1)
                step(dve.tensor_tensor(sm[:, t, :], sm[:, t, :], es[:, t, :], ALU.add))
                step(dve.reciprocal(rden[:, t, :], sm[:, t, :]))
                dve.wait_ge(o_done, NH * (t + 1))
                dve.tensor_tensor(keep["qs"][:, t, :].rearrange("p (h d) -> p h d", d=HD),
                                  ps_o[t % 2][:].rearrange("p (h d) -> p h d", d=HD),
                                  rden[:, t, :].unsqueeze(2).to_broadcast([P, NH, HD]), ALU.mult).then_inc(att_done, 1)

            N = len(STEPS)
            for n in range(N + 4):
                if n < N and n % NH == 3 and STEPS[n][0]:
                    i = STEPS[n][0] - 1
                    dve.wait_ge(row_turned, i + 1)
                    c0 = FIRST + 4 * i
                    dve.tensor_tensor(keep["mod"][:, c0:c0 + 4, :], ps_k[:, 0:8].rearrange("p (c k) -> p c k", k=2),
                                      keep["vcol"][:, V_BADA + c0:V_BADA + c0 + 4].unsqueeze(2).to_broadcast([P, 4, 2]),
                                      ALU.add).then_inc(mod_kept, 1)
                if n < N:
                    maxima(n)
                    if n % NH == NH - 1:
                        sink_part(STEPS[n][0])
                if n >= 2 and n - 2 < N:
                    keep_p(n - 2)
                if n >= 4 and (n - 4) % NH == NH - 1:
                    finish(STEPS[n - 4][0])


NBMAX = 136
TAB = NBMAX + 4
NOWHERE = 1 << 20


def project_out(nc, dram, keep):
    with ExitStack() as ctx:
        def sb(name, shape, dt=F32):
            return ctx.enter_context(nc.sbuf_tensor(name, shape, dt))

        def ps(name, shape):
            return ctx.enter_context(nc.psum_tensor(name, shape, F32))

        def sem(name):
            return nc.alloc_semaphore(name)

        wo = sb("wo", [P, KD, D])
        rw = sb("rw", [P, KD, NE])
        a2col = sb("a2col", [P, KD, 2])
        mixT = [sb(f"mixT{i}", [P, KD, P]) for i in range(2)]
        g2rows = keep["g2"]
        rows = sb("rows", [P, 3, 2, D])
        h2 = [sb(f"h2_{i}", [P, D]) for i in range(2)]
        ssq = sb("ssq2", [P, NT])
        std = sb("std2", [P, NT])
        rstd = sb("rstd2", [P, NT])
        ps_t = ps("ps_t4", [P, D])
        ps_o = ps("ps_o4", [P, 2, 512])
        ps_h = ps("ps_h4", [P, D])
        ps_r = ps("ps_r4", [P, 512])
        ps_b = [ps("ps_b4", [P, 512]), ps_r]

        w_in, x_in = sem("wo_in"), [sem(f"x2_in{t}") for t in range(NT)]
        a2_done, row_made, row_kept = sem("a2_done"), sem("row_made"), sem("row_kept")
        mixT_done, mixT_act, mixT_dve, o_done, x1_done = sem("mixT_done"), sem("mixT_act"), sem("mixT_dve"), sem("o4_done"), sem("x1_done")
        dve_step, gx_done, ssq_done, std_done = sem("dve_step4"), sem("gx_done"), sem("ssq2_done"), sem("std2_done")
        sc_done, h2_done, h2T_done, h2T_act, h2T_dve = sem("sc2_done"), sem("h2_done"), sem("h2T_done"), sem("h2T_act"), sem("h2T_dve")
        r_done, score_done, h2_out = sem("r_done"), sem("score4_done"), [sem(f"h2_out{i}") for i in range(2)]

        def piece(w, c, j):
            if w == 1:
                return a2col[:, j, c:c + 1]
            return keep["mod"][:, {0: 16, 2: 24, 3: 40}[w] + j, c:c + 1]

        QUARTERS = [(w, c, q) for w in range(4) for c in range(2) for q in range(2)]

        block = ctx.enter_context(nc.Block())

        @block.sync
        def _(sp):
            sp.dma_start(wo[:], dram["w_out"].rearrange("(j p) n -> p j n", p=P)).then_inc(w_in, 16)
            sp.dma_start(rw[:], dram["router_w"].rearrange("(p j) n -> p j n", j=KD)).then_inc(w_in, 16)
            for t in range(NT):
                sp.dma_start(keep["x1"][:, t, :], dram["x"](t)).then_inc(x_in[t], 16)
            for t in range(NT):
                sp.wait_ge(h2_done, t + 1)
                sp.dma_start(dram["h2"][t * P:(t + 1) * P, :], h2[t % 2][:]).then_inc(h2_out[t % 2], 16)
            sp.wait_ge(h2_out[0], 16 * 5)
            sp.wait_ge(h2_out[1], 16 * 4)

        @block.tensor
        def _(pe):
            pe.wait_ge(a2_done, 1)
            for n, (w, c, q) in enumerate(QUARTERS):
                if n >= 2:
                    pe.wait_ge(row_kept, n - 1)
                for i in range(4):
                    last = pe.matmul(ps_b[n % 2][:, i * P:(i + 1) * P], piece(w, c, 4 * q + i).to_broadcast([P, P]),
                                     keep["ident"][:], start=True, stop=True)
                last.then_inc(row_made, 1)
            pe.wait_ge(w_in, 32)

            def turn_mix(t):
                if t >= 1:
                    pe.wait_ge(mixT_act, t)
                    pe.wait_ge(mixT_dve, t)
                for j in range(KD):
                    src = (keep["gg"] if j < 4 else keep["qs"])[:, t, (j % 4) * P:(j % 4 + 1) * P]
                    last = pe.transpose(ps_t[:, j * P:(j + 1) * P], src, keep["ident"][:])
                last.then_inc(mixT_done, 1)

            def out(t):
                pe.wait_ge(mixT_act, t + 1)
                pe.wait_ge(mixT_dve, t + 1)
                if t >= 1:
                    pe.wait_ge(gx_done, t)
                for j in range(KD):
                    for n in range(2):
                        last = pe.matmul(ps_o[:, n, :], mixT[t % 2][:, j, :], wo[:, j, n * 512:(n + 1) * 512],
                                         start=(j == 0), stop=(j == KD - 1))
                last.then_inc(o_done, 1)

            def turn_h(t):
                pe.wait_ge(h2_done, t + 1)
                if t >= 1:
                    pe.wait_ge(h2T_act, t)
                    pe.wait_ge(h2T_dve, t)
                for j in range(KD):
                    last = pe.transpose(ps_h[:, j * P:(j + 1) * P], h2[t % 2][:, j:D:KD], keep["ident"][:])
                last.then_inc(h2T_done, 1)

            def route(t):
                pe.wait_ge(h2T_act, t + 1)
                pe.wait_ge(h2T_dve, t + 1)
                if t >= 1:
                    pe.wait_ge(score_done, t)
                else:
                    pe.wait_ge(row_kept, len(QUARTERS))
                for j in range(KD):
                    last = pe.matmul(ps_r[:, 0:NE], keep["h2T"][:, j, t * P:(t + 1) * P], rw[:, j, :],
                                     start=(j == 0), stop=(j == KD - 1))
                last.then_inc(r_done, 1)

            turn_mix(0)
            for t in range(NT + 2):
                if t + 1 < NT:
                    turn_mix(t + 1)
                if t < NT:
                    out(t)
                if t >= 2:
                    route(t - 2)
                if 1 <= t <= NT:
                    turn_h(t - 1)

        @block.scalar
        def _(act):
            nc.scalar.preload_act_table_set("sqrt_and_others")

            def mix_half(t):
                act.wait_ge(mixT_done, t + 1)
                if t >= 2:
                    act.wait_ge(o_done, t - 1)
                act.activation(mixT[t % 2][:, 0:4, :].rearrange("p j t -> p (j t)"), ps_t[:, 0:512], ACT.Copy).then_inc(mixT_act, 1)

            def square(t):
                act.wait_ge(x1_done, t + 1)
                act.activation(h2[t % 2][:], keep["x1"][:, t, :], ACT.Square, accum_out=ssq[:, t:t + 1]).then_inc(ssq_done, 1)
                act.wait_ge(ssq_done, t + 1)
                act.activation(std[:, t:t + 1], ssq[:, t:t + 1], ACT.Sqrt, scale=1.0 / D, bias=keep["eps"][:]).then_inc(std_done, 1)

            def h_half(t):
                act.wait_ge(h2T_done, t + 1)
                act.activation(keep["h2T"][:, 0:4, t * P:(t + 1) * P], ps_h[:, 0:512].rearrange("p (j t) -> p j t", j=4),
                               ACT.Copy).then_inc(h2T_act, 1)

            def logits(t):
                act.wait_ge(r_done, t + 1)
                act.activation(keep["logit"][:, t, :], ps_r[:, 0:NE], ACT.Copy).then_inc(score_done, 1)

            mix_half(0)
            for t in range(NT + 2):
                if t + 1 < NT:
                    mix_half(t + 1)
                if t >= 2:
                    logits(t - 2)
                if t < NT:
                    square(t)
                if 1 <= t <= NT:
                    h_half(t - 1)

        @block.gpsimd
        def _(pool):
            for t in range(NT):
                pool.wait_ge(sc_done, t + 1)
                pool.tensor_tensor(h2[t % 2][:], h2[t % 2][:], rows[:, 2, cond_of(t), :], ALU.add).then_inc(h2_done, 1)

        @block.vector
        def _(dve):
            steps = [0]

            def step(ins):
                steps[0] += 1
                ins.then_inc(dve_step, 1)
                dve.wait_ge(dve_step, steps[0])

            dve.scalar_tensor_tensor(out=a2col[:], in0=keep["mod"][:, 32:40, :], scalar=1.0,
                                     in1=keep["vcol"][:, V_NF:V_NF + 8].unsqueeze(2).to_broadcast([P, KD, 2]),
                                     op0=ALU.add, op1=ALU.mult).then_inc(a2_done, 1)
            for n, (w, c, q) in enumerate(QUARTERS):
                dve.wait_ge(row_made, n + 1)
                dst = rows[:, w, c, :] if w < 3 else g2rows[:, c, :]
                dve.tensor_copy(dst[:, q * 512:(q + 1) * 512], ps_b[n % 2][:]).then_inc(row_kept, 1)
            dve.wait_ge(row_kept, len(QUARTERS))

            def mix_half(t):
                dve.wait_ge(mixT_done, t + 1)
                if t >= 2:
                    dve.wait_ge(o_done, t - 1)
                dve.tensor_copy(mixT[t % 2][:, 4:8, :].rearrange("p j t -> p (j t)"), ps_t[:, 512:1024]).then_inc(mixT_dve, 1)

            def residual(t):
                c = cond_of(t)
                dve.wait_ge(o_done, t + 1)
                if t >= 2:
                    dve.wait_ge(h2_out[t % 2], 16 * (t // 2))
                    dve.wait_ge(h2T_done, t - 1)
                dve.tensor_tensor(h2[t % 2][:], ps_o[:].rearrange("p n k -> p (n k)"), rows[:, 0, c, :], ALU.mult).then_inc(gx_done, 1)
                dve.wait_ge(gx_done, t + 1)
                dve.wait_ge(x_in[t], 16)
                dve.tensor_tensor(keep["x1"][:, t, :], keep["x1"][:, t, :], h2[t % 2][:], ALU.add).then_inc(x1_done, 1)

            def scale(t):
                dve.wait_ge(std_done, t + 1)
                step(dve.reciprocal(rstd[:, t:t + 1], std[:, t:t + 1]))
                dve.scalar_tensor_tensor(out=h2[t % 2][:], in0=keep["x1"][:, t, :], scalar=rstd[:, t:t + 1],
                                         in1=rows[:, 1, cond_of(t), :], op0=ALU.mult, op1=ALU.mult).then_inc(sc_done, 1)

            def h_half(t):
                dve.wait_ge(h2T_done, t + 1)
                dve.tensor_copy(keep["h2T"][:, 4:8, t * P:(t + 1) * P],
                                ps_h[:, 512:1024].rearrange("p (j t) -> p j t", j=4)).then_inc(h2T_dve, 1)

            mix_half(0)
            for t in range(NT + 1):
                if t + 1 < NT:
                    mix_half(t + 1)
                if t < NT:
                    residual(t)
                    scale(t)
                if t >= 1:
                    h_half(t - 1)


def route(nc, dram, keep):
    with ExitStack() as ctx:
        def sb(name, shape, dt=F32):
            return ctx.enter_context(nc.sbuf_tensor(name, shape, dt))

        def ps(name, shape):
            return ctx.enter_context(nc.psum_tensor(name, shape, F32))

        def sem(name):
            return nc.alloc_semaphore(name)

        GE = 8
        rb = sb("rb", [P, NE])
        before = sb("before", [P, GE * GE])
        upperf = sb("upperf", [P, P])
        upper = sb("upper", [P, P], BF16)
        ones = sb("ones", [P, P], BF16)
        onesf = sb("onesf", [P, NE])
        thr = sb("thr", [P, GE])
        blk = sb("blk", [P, 2])
        tok8 = sb("tok8", [P, NT, GE], I32)
        fill = sb("fill", [P, TAB, 4], I32)
        sc = sb("r_sc", [P, NT, NE])
        sel = sb("r_sel", [P, NT, NE])
        top = sb("r_top", [P, NT, GE, GE])
        gs = sb("r_gs", [P, NT, GE])
        cmp_ = sb("r_cmp", [P, NT, GE, GE])
        cm2 = sb("r_cm2", [P, NT, GE, GE])
        rank = sb("r_rank", [P, NT, GE])
        gm = sb("r_gm", [P, NT, GE])
        best = sb("r_best", [P, NT, TOPK])
        M = sb("r_M", [P, NT, NE])
        Mb = sb("r_Mb", [P, NT, NE], BF16)
        gate = sb("r_gate", [P, NT, NE])
        wsum = sb("r_wsum", [P, NT])
        over = sb("r_over", [P, NE, GE])
        nb = sb("r_nb", [P, NE])
        inc = sb("r_inc", [P, NE])
        start = sb("r_start", [P, NE])
        slot = sb("r_slot", [P, NT, NE])
        s8 = sb("r_s8", [P, NT, TOPK])
        s8i = sb("r_s8i", [P, NT, TOPK], I32)
        r8i = sb("r_r8i", [P, NT, TOPK], I32)
        r8 = sb("r_r8", [P, NT, TOPK])
        b8 = sb("r_b8", [P, NT, TOPK])
        row = sb("r_row", [P, NT, TOPK], I32)
        eq = sb("r_eq", [P, TOPK, NE])
        g8 = sb("r_g8", [P, NT, TOPK])
        recs = sb("r_recs", [P, NT, TOPK, 4], I32)
        ebc = sb("r_ebc", [P, 2, NE])
        ebf = sb("r_ebf", [P, 2])
        ebi = sb("r_ebi", [P, 2], I32)
        lasti = sb("r_lasti", [1, 1], I32)
        lastf = sb("r_lastf", [1, 3])
        ps_n = [ps("ps_n0", [P, 512]), ps("ps_n1", [P, 512])]

        wgu = sb("wgu", [P, 2, KD * FS])
        wd = sb("wd_s", [P, 2, D])
        s_sh = [sb(f"s6_{i}", [P, FS]) for i in range(2)]
        h_sh = [sb(f"h6_{i}", [P, FS]) for i in range(2)]
        hT_sh = [sb(f"hT6_{i}", [P, FS]) for i in range(2)]
        t6 = sb("t6", [P, D])
        ps_g = [ps(f"ps_g6_{i}", [P, 512]) for i in range(2)]
        ps_h = ps("ps_h6", [P, 512])
        ps_y = ps("ps_y6", [P, D])
        wgu_in, wd_in, zeroed = sem("wgu_in"), sem("wd_in"), sem("x_zeroed")
        gu_done, silu_done, h_done, hT_done, hT_kept = sem("gu6"), sem("silu6"), sem("h6"), sem("hT6"), sem("hTk6")
        down_done, t_done, x_done = sem("down6"), sem("t6_done"), sem("x6_done")

        const_in, fill_in, dve_step, sig_done = sem("r_const_in"), sem("fill_in"), sem("r_step"), sem("sig_done")
        ones_done, m_done, rank_done, recs_done, eb_done = sem("ones_done"), sem("M_done"), sem("rank_done"), sem("recs_done"), sem("eb_done")
        tab_fill, scattered, eb_out, tabs_in = sem("tab_fill"), sem("scattered"), sem("eb_out"), sem("tabs_in")

        block = ctx.enter_context(nc.Block())

        @block.sync
        def _(sp):
            sp.dma_start(wgu[:, 0, :], dram["sh_w_gate"].rearrange("(p j) f -> p (j f)", j=KD)).then_inc(wgu_in, 16)
            sp.dma_start(wgu[:, 1, :], dram["sh_w_up"].rearrange("(p j) f -> p (j f)", j=KD)).then_inc(wgu_in, 16)
            sp.dma_start(wd[:], dram["sh_w_down"].rearrange("(k p) n -> p k n", p=P)).then_inc(wd_in, 16)
            sp.dma_start(rb[:], dram["router_bias"].to_broadcast([P, NE])).then_inc(const_in, 16)
            sp.dma_start(before[:], dram["before"].to_broadcast([P, GE * GE])).then_inc(const_in, 16)
            sp.dma_start(upperf[:], dram["upper"]).then_inc(const_in, 16)
            sp.dma_start(blk[:], dram["blk"]).then_inc(const_in, 16)
            sp.dma_start(tok8[:], dram["tok8"]).then_inc(const_in, 16)
            sp.dma_start(thr[:], dram["thr"].to_broadcast([P, GE])).then_inc(const_in, 16)
            sp.dma_start(fill[:], dram["fill"].to_broadcast([P, TAB * 4]).rearrange("p (b k) -> p b k", k=4)).then_inc(fill_in, 16)
            sp.wait_ge(fill_in, 16)
            sp.dma_start(dram["table"].rearrange("(p b) k -> p b k", b=TAB), fill[:]).then_inc(tab_fill, 16)
            sp.wait_ge(eb_done, 1)
            sp.dma_start(dram["block_expert"].rearrange("(p c) -> p c", p=P), ebi[:]).then_inc(eb_out, 16)
            sp.wait_ge(eb_out, 16)
            sp.dma_start(keep["bexp"][:], dram["block_expert"].rearrange("(a n) -> a n", a=1)).then_inc(eb_out, 16)
            sp.wait_ge(scattered, 16 * NT * TOPK)
            sp.dma_start(keep["tab"][:], dram["table"].rearrange("(p b) k -> p b k", b=TAB)).then_inc(tabs_in, 16)
            sp.wait_ge(eb_out, 32)
            sp.wait_ge(tabs_in, 16)

        @block.gpsimd
        def _(pool):
            pool.memset(keep["mix"][:, 0:4 * D], 0.0).then_inc(zeroed, 1)
            pool.wait_ge(tab_fill, 16)
            for t in range(NT):
                pool.wait_ge(recs_done, t + 1)
                for j in range(TOPK):
                    pool.indirect_dma_start(out=dram["table"], out_offset=bass.IndirectOffsetOnAxis(ap=row[:, t, j:j + 1], axis=0),
                                            in_=recs[:, t, j, :], in_offset=None).then_inc(scattered, 16)
            pool.wait_ge(scattered, 16 * NT * TOPK)
            pool.wait_ge(zeroed, 1)

        @block.scalar
        def _(act):
            act.activation(sc[:], keep["logit"][:], ACT.Sigmoid).then_inc(sig_done, 1)
            nc.scalar.preload_act_table_set("silu_and_others")
            for t in range(NT):
                act.wait_ge(gu_done, t + 1)
                if t >= 2:
                    act.wait_ge(h_done, t - 1)
                act.activation(s_sh[t % 2][:], ps_g[t % 2][:, 0:FS], ACT.Silu).then_inc(silu_done, 1)
                act.wait_ge(hT_done, t + 1)
                if t >= 2:
                    act.wait_ge(down_done, t - 1)
                act.activation(hT_sh[t % 2][:], ps_h[:, 0:FS], ACT.Copy).then_inc(hT_kept, 1)

        @block.tensor
        def _(pe):
            def ranks():
                pe.wait_ge(m_done, 1)
                pe.wait_ge(const_in, 96)
                for t in range(NT):
                    out = ps_n[t // 8][:, (t % 8) * NE:(t % 8 + 1) * NE]
                    for s in range(t):
                        pe.matmul(out, ones[:], Mb[:, s, :], start=(s == 0), stop=False)
                    pe.matmul(out, upper[:], Mb[:, t, :], start=(t == 0), stop=True)
                for s in range(NT):
                    last = pe.matmul(ps_n[1][:, NE:2 * NE], ones[:], Mb[:, s, :], start=(s == 0), stop=(s == NT - 1))
                last.then_inc(rank_done, 1)

            pe.wait_ge(wgu_in, 32)
            for t in range(NT + 1):
                if t == 2:
                    ranks()
                if t < NT:
                    if t >= 2:
                        pe.wait_ge(h_done, t - 1)
                    for j in range(KD):
                        last = pe.matmul(ps_g[t % 2][:].rearrange("p (k f) -> p k f", k=2), keep["h2T"][:, j, t * P:(t + 1) * P],
                                         wgu[:, :, j * FS:(j + 1) * FS], start=(j == 0), stop=(j == KD - 1))
                    last.then_inc(gu_done, 1)
                if t >= 1:
                    n = t - 1
                    pe.wait_ge(hT_kept, n + 1)
                    if n == 0:
                        pe.wait_ge(wd_in, 16)
                    if n >= 1:
                        pe.wait_ge(t_done, n)
                    for q in range(2):
                        for k in range(2):
                            last = pe.matmul(ps_y[:, q * 512:(q + 1) * 512], hT_sh[n % 2][:, k * P:(k + 1) * P],
                                             wd[:, k, q * 512:(q + 1) * 512], start=(k == 0), stop=(k == 1))
                    last.then_inc(down_done, 1)
                if t < NT:
                    pe.wait_ge(h_done, t + 1)
                    for k in range(2):
                        last = pe.transpose(ps_h[:, k * P:(k + 1) * P], h_sh[t % 2][:, k * P:(k + 1) * P], keep["ident"][:])
                    last.then_inc(hT_done, 1)

        @block.vector
        def _(dve):
            steps = [0]

            def step(ins):
                steps[0] += 1
                ins.then_inc(dve_step, 1)
                dve.wait_ge(dve_step, steps[0])

            def shared(t):
                if t < NT:
                    dve.wait_ge(silu_done, t + 1)
                    if t >= 2:
                        dve.wait_ge(hT_done, t - 1)
                    dve.tensor_tensor(h_sh[t % 2][:], s_sh[t % 2][:], ps_g[t % 2][:, FS:2 * FS], ALU.mult).then_inc(h_done, 1)
                if t >= 1:
                    dve.wait_ge(down_done, t)
                    if t >= 2:
                        dve.wait_ge(x_done, t - 1)
                    dve.tensor_tensor(t6[:], ps_y[:], keep["g2"][:, cond_of(t - 1), :], ALU.mult).then_inc(t_done, 1)
                    dve.wait_ge(t_done, t)
                    dve.tensor_tensor(keep["x1"][:, t - 1, :], keep["x1"][:, t - 1, :], t6[:], ALU.add).then_inc(x_done, 1)

            def per_expert(ap):
                return ap.unsqueeze(1).to_broadcast([P, NT, NE])

            dve.memset(ones[:], 1.0)
            step(dve.memset(onesf[:], 1.0))
            dve.wait_ge(const_in, 96)
            dve.tensor_copy(upper[:], upperf[:])
            dve.wait_ge(sig_done, 1)
            step(dve.tensor_tensor(sel[:], sc[:], per_expert(rb[:]), ALU.add))
            for t in range(NT):
                for g in range(GE):
                    last = dve.max(top[:, t, g, :], sel[:, t, g * GE:(g + 1) * GE])
            step(last)
            step(dve.tensor_tensor(gs[:], top[:, :, :, 0], top[:, :, :, 1], ALU.add))
            other = gs[:].unsqueeze(2).to_broadcast([P, NT, GE, GE])
            own = gs[:].unsqueeze(3).to_broadcast([P, NT, GE, GE])
            dve.tensor_tensor(cmp_[:], other, own, ALU.is_gt)
            step(dve.tensor_tensor(cm2[:], other, own, ALU.is_equal))
            step(dve.tensor_tensor(cm2[:].rearrange("p t a b -> p t (a b)"), cm2[:].rearrange("p t a b -> p t (a b)"),
                                   before[:].unsqueeze(1).to_broadcast([P, NT, GE * GE]), ALU.mult))
            step(dve.tensor_tensor(cmp_[:], cmp_[:], cm2[:], ALU.add))
            step(dve.tensor_reduce(rank[:], cmp_[:], AX.X, ALU.add))
            step(dve.tensor_scalar(gm[:], rank[:], 3.5, None, ALU.is_lt))
            shared(0)
            mask = gm[:].unsqueeze(3).to_broadcast([P, NT, GE, GE])
            step(dve.tensor_tensor(sel[:].rearrange("p t (g e) -> p t g e", g=GE), sel[:].rearrange("p t (g e) -> p t g e", g=GE), mask, ALU.mult))
            step(dve.tensor_scalar(gm[:], gm[:], -1.0, 1e30, ALU.add, ALU.mult))
            step(dve.tensor_tensor(sel[:].rearrange("p t (g e) -> p t g e", g=GE), sel[:].rearrange("p t (g e) -> p t g e", g=GE), mask, ALU.add))
            for t in range(NT):
                last = dve.max(best[:, t, :], sel[:, t, :])
            step(last)
            for t in range(NT):
                last = dve.match_replace(M[:, t, :], best[:, t, :], sel[:, t, :], -3e38)
            step(last)
            step(dve.tensor_tensor(M[:], M[:], sel[:], ALU.not_equal))
            dve.tensor_copy(Mb[:], M[:]).then_inc(m_done, 1)
            step(dve.tensor_tensor(gate[:], sc[:], M[:], ALU.mult))
            step(dve.tensor_reduce(wsum[:], gate[:], AX.X, ALU.add))
            shared(1)
            step(dve.reciprocal(wsum[:], wsum[:]))
            step(dve.tensor_scalar(wsum[:], wsum[:], 2.5, None, ALU.mult))
            step(dve.tensor_tensor(gate[:], gate[:], wsum[:].unsqueeze(2).to_broadcast([P, NT, NE]), ALU.mult))
            dve.wait_ge(rank_done, 1)
            step(dve.tensor_tensor(over[:], ps_n[1][:, NE:2 * NE].unsqueeze(2).to_broadcast([P, NE, GE]),
                                   thr[:].unsqueeze(1).to_broadcast([P, NE, GE]), ALU.is_gt))
            step(dve.tensor_reduce(nb[:], over[:], AX.X, ALU.add))
            step(dve.tensor_scalar(nb[:], nb[:], 1.0, None, ALU.add))
            step(dve.tensor_tensor_scan(inc[:], onesf[:], nb[:], 0.0, ALU.mult, ALU.add))
            step(dve.tensor_tensor(start[:], inc[:], nb[:], ALU.subtract))
            step(dve.tensor_scalar(start[:], start[:], float(P), 1.0, ALU.mult, ALU.add))
            dve.tensor_tensor(slot[:, 0:8, :], ps_n[0][:].rearrange("p (t e) -> p t e", e=NE),
                              start[:].unsqueeze(1).to_broadcast([P, 8, NE]), ALU.add)
            step(dve.tensor_tensor(slot[:, 8, :], ps_n[1][:, 0:NE], start[:], ALU.add))
            step(dve.tensor_tensor(slot[:], slot[:], M[:], ALU.mult))
            for t in range(NT):
                last = dve.max(s8[:, t, :], slot[:, t, :])
            step(last)
            for c in range(2):
                last = dve.tensor_scalar(ebc[:, c, :], inc[:], blk[:, c:c + 1], None, ALU.is_le)
            step(last)
            step(dve.tensor_reduce(ebf[:], ebc[:], AX.X, ALU.add))
            step(dve.tensor_scalar(ebf[:], ebf[:], float(NE - 1), None, ALU.min))
            dve.tensor_copy(keep["bend"][:, 0:NE], inc[0:1, :])
            step(dve.tensor_scalar(lasti[:], inc[0:1, NE - 1:NE], 3.0, None, ALU.add))
            step(dve.tensor_scalar(lasti[:], lasti[:], 2, None, ALU.logical_shift_right))
            step(dve.tensor_copy(lastf[:, 0:1], lasti[:]))
            dve.tensor_scalar(lastf[:, 1:2], lastf[:, 0:1], 4.0, -1.0, ALU.mult, ALU.add)
            step(dve.tensor_scalar(lastf[:, 2:3], lastf[:, 0:1], 16.0, -16.0, ALU.mult, ALU.add))
            dve.tensor_copy(keep["bend"][:, NE:NE + 2], lastf[:, 1:3])
            dve.tensor_copy(ebi[:], ebf[:]).then_inc(eb_done, 1)
            dve.tensor_scalar(b8[:], s8[:], -1.0, None, ALU.add)
            step(dve.tensor_scalar(s8i[:], s8[:], -1.0, None, ALU.add))
            step(dve.tensor_scalar(r8i[:], s8i[:], P - 1, None, ALU.bitwise_and))
            step(dve.tensor_copy(r8[:], r8i[:]))
            step(dve.tensor_tensor(b8[:], b8[:], r8[:], ALU.subtract))
            step(dve.tensor_scalar(b8[:], b8[:], 1.0 / P, None, ALU.mult))
            step(dve.scalar_tensor_tensor(out=row[:], in0=r8[:], scalar=float(TAB), in1=b8[:], op0=ALU.mult, op1=ALU.add))
            dve.tensor_scalar(recs[:, :, :, 0], tok8[:], 3, None, ALU.logical_shift_right)
            step(dve.tensor_copy(recs[:, :, :, 1], tok8[:]))
            for t in range(NT):
                if t >= 2:
                    shared(t)
                step(dve.tensor_tensor(eq[:], slot[:, t, :].unsqueeze(1).to_broadcast([P, TOPK, NE]),
                                       s8[:, t, :].unsqueeze(2).to_broadcast([P, TOPK, NE]), ALU.is_equal))
                step(dve.tensor_tensor(eq[:], eq[:], gate[:, t, :].unsqueeze(1).to_broadcast([P, TOPK, NE]), ALU.mult))
                step(dve.tensor_reduce(g8[:, t, :], eq[:], AX.X, ALU.add))
                dve.tensor_copy(recs[:, t, :, 3], tok8[:, t, :])
                dve.tensor_copy(recs[:, t, :, 2].bitcast(F32), g8[:, t, :]).then_inc(recs_done, 1)
            shared(NT)


def experts(nc, dram, keep):
    with ExitStack() as ctx:
        def sb(name, shape, dt=F32):
            return ctx.enter_context(nc.sbuf_tensor(name, shape, dt))

        def ps(name, shape):
            return ctx.enter_context(nc.psum_tensor(name, shape, F32))

        def sem(name):
            return nc.alloc_semaphore(name)

        NW = 8
        AHEAD = 4
        FOURS = NBMAX // 4
        w = sb("w_exp", [P, NW * 3, D])
        buf = keep["mix"]
        x = [buf[:, i * D:(i + 1) * D] for i in range(4)]
        xT = [buf[:, (4 + i) * D:(5 + i) * D] for i in range(2)]
        y = [buf[:, (6 + i) * D:(7 + i) * D] for i in range(3)] + [sb("y5_3", [P, D])[:]]
        gi = [sb(f"gather_row{i}", [P, 1], I32) for i in range(4)]
        si = [sb(f"scatter_row{i}", [P, 1], I32) for i in range(4)]
        s = [sb(f"silu{i}", [P, FF]) for i in range(2)]
        h = [sb(f"hid{i}", [P, FF]) for i in range(2)]
        hT = [sb(f"hidT{i}", [P, P]) for i in range(2)]
        ps_x = ps("ps_x5", [P, D])
        ps_g = [ps(f"ps_g5_{i}", [P, 512]) for i in range(2)]
        ps_h = ps("ps_h5", [P, 512])
        ps_y = ps("ps_y5", [P, D])

        w_in = [sem(f"w_in{i}") for i in range(NW)]
        w_ready = sem("w_ready")
        x_in = [sem(f"x5_in{i}") for i in range(4)]
        y_out = [sem(f"y_out{i}") for i in range(4)]
        passed = sem("pool_passed")
        gi_done, si_done = sem("gi_done"), sem("si_done")
        xT_done, xT_act, xT_dve = sem("xT5_done"), sem("xT5_act"), sem("xT5_dve")
        gu_done, silu_done, h_done, hT_done, hT_kept = sem("gu_done"), sem("silu_done"), sem("h_done"), sem("hT_done"), sem("hT_kept")
        down_done, y_act, y_dve = sem("down_done"), sem("y_act"), sem("y_dve")

        wg = dram["exp_w_gate"].rearrange("(e p j) f -> e p (j f)", p=P, j=KD)
        wu = dram["exp_w_up"].rearrange("(e p j) f -> e p (j f)", p=P, j=KD)
        wd = dram["exp_w_down"].rearrange("(e p) n -> e p n", p=P)

        def fours(eng, body):
            blocks = eng.value_load(keep["bend"][0:1, NE - 1:NE], min_val=NE, max_val=NBMAX)
            body(0)
            with eng.Fori(1, FOURS) as i:
                with eng.If(i * 4 < blocks):
                    body(i)
            return (eng.value_load(keep["bend"][0:1, NE:NE + 1], min_val=NE - 1, max_val=NBMAX - 1),
                    eng.value_load(keep["bend"][0:1, NE + 1:NE + 2], min_val=16, max_val=16 * FOURS - 16))

        def first(i):
            return isinstance(i, int)

        block = ctx.enter_context(nc.Block())

        @block.sync
        def _(sp):
            def issue(e, slot):
                for k, src in enumerate((wg, wu, wd)):
                    sp.dma_start(w[:, 3 * slot + k, :], src[e, :, :]).then_inc(w_in[slot], 16)

            def ready(o, i):
                sp.wait_ge(w_in[i], (o + 1) * 48)
                sp.sem_inc(w_ready, 1)

            def replace(o, i, wait=True):
                if wait:
                    last = sp.value_load(keep["bend"][0:1, bass.ds(o * NW + (i - 1), 1)], min_val=0, max_val=NBMAX)
                    sp.wait_ge(down_done, last)
                issue(o * NW + (i + NW - 1), (i + NW - 1) % NW)

            issue(0, 0)
            issue(1, 1)
            sp.wait_ge(x_in[0], 16)
            ready(0, 0)
            issue(2, 2)
            ready(0, 1)
            for e in range(3, NW - 1):
                sp.wait_ge(gu_done, e - 2)
                issue(e, e)
                if e <= AHEAD:
                    ready(0, e - 1)
            for i in range(NW):
                ready((i + AHEAD) // NW, (i + AHEAD) % NW)
                replace(0, i, wait=i > 0)
            with sp.Fori(1, NE // NW - 1) as o:
                for i in range(NW):
                    ready(o + (i + AHEAD) // NW, (i + AHEAD) % NW)
                    replace(o, i)
            replace(NE // NW - 1, 0)
            for i in range(AHEAD, NW):
                ready(NE // NW - 1, i)

        @block.gpsimd
        def _(pool):
            def gather(k, b):
                pool.tensor_copy(gi[k][:], keep["tab"][:, b, 0:1]).then_inc(gi_done, 1)
                pool.wait_ge(gi_done, b + 1)
                pool.sem_inc(passed, 1)
                pool.indirect_dma_start(out=x[k], out_offset=None, in_=dram["h2"],
                                        in_offset=bass.IndirectOffsetOnAxis(ap=gi[k][:], axis=0),
                                        bounds_check=T - 1, oob_is_err=False).then_inc(x_in[k], 16)

            for k in range(4):
                gather(k, k)

            def body(i):
                for k in range(4):
                    b = i * 4 + k
                    pool.wait_ge(xT_done, b + 1)
                    pool.sem_inc(passed, 1)
                    gather(k, b + 4)
                    if not first(i):
                        pool.wait_ge(y_out[k], i * 16)
                        pool.sem_inc(passed, 1)
                    pool.tensor_copy(si[k][:], keep["tab"][:, b, 1:2]).then_inc(si_done, 1)
                    pool.wait_ge(si_done, b + 1)
                    pool.wait_ge(y_act, b + 1)
                    pool.wait_ge(y_dve, b + 1)
                    pool.sem_inc(passed, 1)
                    pool.indirect_dma_start(out=dram["y"], out_offset=bass.IndirectOffsetOnAxis(ap=si[k][:], axis=0),
                                            in_=y[k], in_offset=None,
                                            bounds_check=T * TOPK - 1, oob_is_err=False).then_inc(y_out[k], 16)

            last, before = fours(pool, body)
            for k in range(4):
                pool.wait_ge(y_out[k], before + 16)
                pool.wait_ge(x_in[k], before + 32)

        @block.tensor
        def _(pe):
            def expert_of(b):
                return pe.value_load(keep["bexp"][0:1, bass.ds(b, 1)], min_val=0, max_val=NE - 1)

            def turn_x(k, b, n):
                pe.wait_ge(x_in[k], n * 16 + 16)
                for j in range(KD):
                    last = pe.transpose(ps_x[:, j * P:(j + 1) * P], x[k][:, j:D:KD], keep["ident"][:])
                last.then_inc(xT_done, 1)

            def down(par, b, slot):
                pe.wait_ge(hT_kept, b + 1)
                for n in range(2):
                    last = pe.matmul(ps_y[:, n * 512:(n + 1) * 512], hT[par][:],
                                     w[:, slot * 3 + 2, n * 512:(n + 1) * 512], start=True, stop=True)
                last.then_inc(down_done, 1)

            def turn_h(par, b):
                pe.wait_ge(h_done, b + 1)
                pe.transpose(ps_h[:, 0:P], h[par][:], keep["ident"][:]).then_inc(hT_done, 1)

            turn_x(0, 0, 0)

            def body(i):
                former = None if first(i) else expert_of(i * 4 - 1)
                for k in range(4):
                    b, par = i * 4 + k, k % 2
                    e = expert_of(b)
                    slot = e % NW
                    if not (first(i) and k == 0):
                        turn_h(1 - par, b - 1)
                    pe.wait_ge(w_ready, e + 1)
                    pe.wait_ge(xT_act, b + 1)
                    pe.wait_ge(xT_dve, b + 1)
                    if not (first(i) and k < 2):
                        pe.wait_ge(h_done, b - 1)
                    for j in range(KD):
                        last = pe.matmul(ps_g[par][:, 0:2 * FF].rearrange("p (k f) -> p k f", k=2),
                                         xT[par][:, j * P:(j + 1) * P],
                                         w[:, bass.ds(slot * 3, 2), j * FF:(j + 1) * FF],
                                         start=(j == 0), stop=(j == KD - 1))
                    last.then_inc(gu_done, 1)
                    turn_x((k + 1) % 4, b + 1, i + (k + 1) // 4)
                    if not (first(i) and k == 0):
                        if not (first(i) and k == 1):
                            pe.wait_ge(y_act, b - 1)
                            pe.wait_ge(y_dve, b - 1)
                        down(1 - par, b - 1, former % NW)
                    former = e

            last, _ = fours(pe, body)
            slot = expert_of(last) % NW
            turn_h(1, last)
            pe.wait_ge(y_act, last)
            pe.wait_ge(y_dve, last)
            down(1, last, slot)

        def move_x(eng, copy, done, half, par, b, wait):
            eng.wait_ge(xT_done, b + 1)
            if wait:
                eng.wait_ge(gu_done, b - 1)
            copy(xT[par][:, half * 512:(half + 1) * 512], ps_x[:, half * 512:(half + 1) * 512]).then_inc(done, 1)

        def move_y(eng, copy, done, half, k, b, n):
            eng.wait_ge(down_done, b + 1)
            if n is not None:
                eng.wait_ge(y_out[k], n)
            copy(y[k][:, half * 512:(half + 1) * 512], ps_y[:, half * 512:(half + 1) * 512]).then_inc(done, 1)

        def stores_before(i, k):
            if first(i):
                return None
            return (i - 1) * 16 if k == 0 else i * 16

        @block.scalar
        def _(act):
            nc.scalar.preload_act_table_set("silu_and_others")

            def copy(out, in_):
                return act.activation(out, in_, ACT.Copy)

            move_x(act, copy, xT_act, 0, 0, 0, False)

            def body(i):
                for k in range(4):
                    b, par = i * 4 + k, k % 2
                    act.wait_ge(gu_done, b + 1)
                    if not (first(i) and k < 2):
                        act.wait_ge(h_done, b - 1)
                    act.activation(s[par][:], ps_g[par][:, 0:FF], ACT.Silu).then_inc(silu_done, 1)
                    move_x(act, copy, xT_act, 0, 1 - par, b + 1, not (first(i) and k == 0))
                    if not (first(i) and k == 0):
                        move_y(act, copy, y_act, 0, (k + 3) % 4, b - 1, stores_before(i, k))
                    act.wait_ge(hT_done, b + 1)
                    if not (first(i) and k < 2):
                        act.wait_ge(down_done, b - 1)
                    copy(hT[par][:], ps_h[:, 0:P]).then_inc(hT_kept, 1)

            last, before = fours(act, body)
            move_y(act, copy, y_act, 0, 3, last, before)

        @block.vector
        def _(dve):
            move_x(dve, dve.tensor_copy, xT_dve, 1, 0, 0, False)

            def body(i):
                for k in range(4):
                    b, par = i * 4 + k, k % 2
                    dve.wait_ge(silu_done, b + 1)
                    if not (first(i) and k < 2):
                        dve.wait_ge(hT_done, b - 1)
                    dve.scalar_tensor_tensor(out=h[par][:], in0=s[par][:], scalar=keep["tab"][:, b, 2:3].bitcast(F32),
                                             in1=ps_g[par][:, FF:2 * FF], op0=ALU.mult, op1=ALU.mult).then_inc(h_done, 1)
                    move_x(dve, dve.tensor_copy, xT_dve, 1, 1 - par, b + 1, not (first(i) and k == 0))
                    if not (first(i) and k == 0):
                        move_y(dve, dve.tensor_copy, y_dve, 1, (k + 3) % 4, b - 1, stores_before(i, k))

            last, before = fours(dve, body)
            move_y(dve, dve.tensor_copy, y_dve, 1, 3, last, before)


def combine(nc, dram, keep):
    with ExitStack() as ctx:
        def sb(name, shape, dt=F32):
            return ctx.enter_context(nc.sbuf_tensor(name, shape, dt))

        def sem(name):
            return nc.alloc_semaphore(name)

        NB = 3
        H = D // 2
        y8 = [sb(f"y8_{i}", [P, TOPK, D]) for i in range(NB)]
        r = [sb(f"r7_{i}", [P, D]) for i in range(2)]
        out = [sb(f"out7_{i}", [P, D]) for i in range(2)]
        fg = sb("fg", [P, D])
        junk = sb("junk7", [P, D])
        ssq = sb("ssq7", [P, NT])
        std = sb("std7", [P, NT])
        rstd = sb("rstd7", [P, NT])
        ps_r = [ctx.enter_context(nc.psum_tensor(f"ps_r7_{i}", [P, 512], F32)) for i in range(2)]
        low_in, high_in, fg_in = [sem(f"low_in{i}") for i in range(NB)], [sem(f"high_in{i}") for i in range(NB)], sem("fg_in")
        sum_pe, sum_dve, g_done, x_done, ssq_done, std_done, rstd_done, out_done = (
            sem("sum_pe"), sem("sum_dve"), sem("g7_done"), sem("x7_done"), sem("ssq7_done"), sem("std7_done"), sem("rstd7_done"), sem("out7_done"))
        stored = [sem(f"stored{i}") for i in range(2)]
        block = ctx.enter_context(nc.Block())

        @block.sync
        def _(sp):
            for t in range(NT):
                if t == 1:
                    sp.dma_start(fg[:], dram["final_g"].to_broadcast([P, D])).then_inc(fg_in, 16)
                if t >= NB:
                    sp.wait_ge(sum_pe, t - NB + 1)
                    sp.wait_ge(sum_dve, t - NB + 1)
                rows = dram["y"][t * P * TOPK:(t + 1) * P * TOPK, :].rearrange("(p j) n -> p j n", j=TOPK)
                sp.dma_start(y8[t % NB][:, :, 0:H], rows[:, :, 0:H]).then_inc(low_in[t % NB], 16)
                sp.dma_start(y8[t % NB][:, :, H:D], rows[:, :, H:D]).then_inc(high_in[t % NB], 16)

        @block.tensor
        def _(pe):
            for t in range(NT):
                pe.wait_ge(low_in[t % NB], 16 * (t // NB + 1))
                if t >= 2:
                    pe.wait_ge(g_done, t - 1)
                for j in range(TOPK):
                    last = pe.matmul(ps_r[t % 2][:], keep["ident"][:], y8[t % NB][:, j, 0:H], start=(j == 0), stop=(j == TOPK - 1))
                last.then_inc(sum_pe, 1)

        @block.vector
        def _(dve):
            def total(t):
                dve.wait_ge(high_in[t % NB], 16 * (t // NB + 1))
                if t >= 2:
                    dve.wait_ge(x_done, t - 1)
                dve.tensor_reduce(r[t % 2][:, H:D], y8[t % NB][:, :, H:D].rearrange("p j n -> p n j"), AX.X, ALU.add).then_inc(sum_dve, 1)
                dve.wait_ge(sum_dve, t + 1)
                g2 = keep["g2"][:, cond_of(t), :]
                dve.wait_ge(sum_pe, t + 1)
                dve.tensor_tensor(r[t % 2][:, 0:H], ps_r[t % 2][:], g2[:, 0:H], ALU.mult)
                dve.tensor_tensor(r[t % 2][:, H:D], r[t % 2][:, H:D], g2[:, H:D], ALU.mult).then_inc(g_done, 1)

            def norm(t):
                dve.wait_ge(std_done, t + 1)
                if t == 0:
                    dve.wait_ge(fg_in, 16)
                dve.reciprocal(rstd[:, t:t + 1], std[:, t:t + 1]).then_inc(rstd_done, 1)
                dve.wait_ge(rstd_done, t + 1)
                if t >= 2:
                    dve.wait_ge(stored[t % 2], 16 * (t // 2))
                dve.scalar_tensor_tensor(out=out[t % 2][:], in0=keep["x1"][:, t, :], scalar=rstd[:, t:t + 1], in1=fg[:],
                                         op0=ALU.mult, op1=ALU.mult).then_inc(out_done, 1)

            for t in range(NT + 2):
                if t < NT:
                    total(t)
                if t >= 2:
                    norm(t - 2)

        @block.gpsimd
        def _(pool):
            for t in range(NT):
                pool.wait_ge(g_done, t + 1)
                pool.tensor_tensor(keep["x1"][:, t, :], keep["x1"][:, t, :], r[t % 2][:], ALU.add).then_inc(x_done, 1)

        @block.scalar
        def _(act):
            nc.scalar.preload_act_table_set("sqrt_and_others")
            for t in range(NT + 2):
                if t < NT:
                    act.wait_ge(x_done, t + 1)
                    if t >= 1:
                        act.wait_ge(ssq_done, t)
                    act.activation(junk[:], keep["x1"][:, t, :], ACT.Square, accum_out=ssq[:, t:t + 1]).then_inc(ssq_done, 1)
                    act.wait_ge(ssq_done, t + 1)
                    act.activation(std[:, t:t + 1], ssq[:, t:t + 1], ACT.Sqrt, scale=1.0 / D, bias=keep["eps"][:]).then_inc(std_done, 1)
                if t >= 2:
                    act.wait_ge(out_done, t - 1)
                    act.dma_start(dram["y_out"](t - 2), out[t % 2][:]).then_inc(stored[t % 2], 16)
            act.wait_ge(stored[0], 16 * 5)
            act.wait_ge(stored[1], 16 * 4)


def program(nc, dram):
    with ExitStack() as ctx:
        def sb(name, shape, dt=F32):
            return ctx.enter_context(nc.sbuf_tensor(name, shape, dt))

        keep = {
            "ident": sb("ident", [P, P]),
            "eps": sb("eps", [P, 1]),
            "vcol": sb("vcol", [P, V_ROWS]),
            "mod": sb("mod", [P, 48, 2]),
            "condT": sb("condT", [P, KD, 2]),
        }
        dram["h2"] = nc.dram_tensor("h2_rows", (T, D), F32, kind="Internal").ap()
        dram["y"] = nc.dram_tensor("pair_rows", (T * TOPK, D), F32, kind="Internal").ap()
        dram["table"] = nc.dram_tensor("slot_table", (P * TAB, 4), I32, kind="Internal").ap()
        dram["block_expert"] = nc.dram_tensor("block_expert", (2 * P,), I32, kind="Internal").ap()

        def stage(build):
            with nc.cleanup_on_exit():
                build(nc, dram, keep)

        with ExitStack() as mixer:
            def sb(name, shape, dt=F32):
                return mixer.enter_context(nc.sbuf_tensor(name, shape, dt))

            keep["mix"] = sb("mix", [P, 2 * NT * 512])
            keep["gg"] = keep["mix"][:, 0:NT * 512].rearrange("p (t n) -> p t n", n=512)
            keep["qs"] = keep["mix"][:, NT * 512:].rearrange("p (t n) -> p t n", n=512)
            with ExitStack() as inner:
                def sb(name, shape, dt=F32):
                    return inner.enter_context(nc.sbuf_tensor(name, shape, dt))

                keep["vg"] = sb("vg", [P, NT, 512])
                keep["kv"] = sb("kv", [P, NT, 256])
                keep["qkT"] = sb("qkT", [P, 4, T])
                keep["loraT"] = sb("loraT", [32, T])
                stage(project)
                stage(linear_attention)
                stage(window_attention)
            with ExitStack() as late:
                def sb(name, shape, dt=F32):
                    return late.enter_context(nc.sbuf_tensor(name, shape, dt))

                keep["logit"] = sb("logit", [P, NT, NE])
                keep["tab"] = sb("tab", [P, TAB, 4], I32)
                keep["bexp"] = sb("bexp", [1, 2 * P], I32)
                keep["bend"] = sb("bend", [1, NE + 2], I32)
                keep["g2"] = sb("g2_rows", [P, 2, D])
                keep["x1"] = sb("x1", [P, NT, D])
                with nc.sbuf_tensor("h2T", [P, KD, T], F32) as h2T:
                    keep["h2T"] = h2T
                    stage(project_out)
                    stage(route)
                stage(experts)
                stage(combine)


def rope_table():
    import numpy as np

    quarter, grid_w = 16, 64
    inv_freq = (np.float32(10000.0) ** (-np.arange(quarter, dtype=np.float32) / quarter)).astype(np.float32)
    pos = np.arange(8 * P)
    table = np.zeros((8 * P, 2, 2, 2, quarter), np.float32)
    for half, at in enumerate((pos // grid_w, pos % grid_w)):
        ang = at.astype(np.float32)[:, None] * inv_freq[None, :]
        table[:, 0, half, :, :] = np.cos(ang)[:, None, :]
        table[:, 1, half, 0, :] = -np.sin(ang)
        table[:, 1, half, 1, :] = np.sin(ang)
    return np.ascontiguousarray(table.reshape(8, P, 2, 64).transpose(1, 0, 2, 3))


def band_table():
    import numpy as np

    t, s = np.arange(P)[:, None], np.arange(P)[None, :]
    band = np.zeros((P, 896), np.float32)
    band[:, P:2 * P] = np.where(s >= t, 0.0, -1e30)
    band[:, 3 * P:4 * P] = band[:, 6 * P:] = np.where(s <= t, 0.0, -1e30)
    return band


def kernel(**inputs):
    import numpy as np
    import concourse.bacc as bacc
    from concourse.bass_utils import run_bass_kernel_spmd

    a = {k: np.asarray(v) for k, v in inputs.items()}
    rows = [a["c_ctx"].reshape(8, P), a["c"].reshape(8, P), a["norm_attn_g"].reshape(8, P), a["norm_ffn_g"].reshape(8, P),
            a["b_ada"].reshape(48, P), a["gla_ba_f"].reshape(2, P), a["gla_ba_b"].reshape(2, P)]
    host = {
        "vectors": np.concatenate(rows),
        "ident": np.eye(P, dtype=np.float32),
        "gla_wa_f": a["gla_wa_f"][0], "gla_wa_b": a["gla_wa_b"][0], "gla_norm_g": a["gla_norm_g"],
        "gla_mask": np.stack([np.triu(np.ones((P, P))), np.tril(np.ones((P, P)))], 1).astype(np.int32),
        "state_f": a["state_gla_fwd"].reshape(256, P), "state_b": a["state_gla_bwd"].reshape(256, P),
        "cache_k": a["cache_swa_k"].reshape(P, P), "cache_v": a["cache_swa_v"].reshape(P, P),
        "sink": a["swa_sink"], "rope": rope_table(), "band": band_table(),
        "w_out": a["w_out"][0], "router_w": a["router_w"][0], "router_bias": a["router_bias"],
        "before": np.tril(np.ones((8, 8), np.float32), -1).reshape(1, 64),
        "upper": np.triu(np.ones((P, P), np.float32), 1),
        "blk": np.arange(2 * P, dtype=np.float32).reshape(P, 2),
        "thr": (P * np.arange(1, 9, dtype=np.float32)).reshape(1, 8),
        "tok8": (8 * np.arange(T).reshape(NT, P).T[:, :, None] + np.arange(8)).astype(np.int32),
        "fill": np.tile(np.array([NOWHERE, NOWHERE, 0, 0], np.int32), TAB).reshape(1, TAB * 4),
        "exp_w_gate": a["exp_w_gate"].reshape(NE * D, FF), "exp_w_up": a["exp_w_up"].reshape(NE * D, FF),
        "exp_w_down": a["exp_w_down"].reshape(NE * FF, D),
        "sh_w_gate": a["sh_w_gate"][0], "sh_w_up": a["sh_w_up"][0], "sh_w_down": a["sh_w_down"][0],
        "final_g": a["final_norm_g"].reshape(1, D),
        "xp": a["x_prompt"].reshape(P, D), "xs": a["x_sample"].reshape(8 * P, D),
        "w_ada": a["w_ada"][0], "w_in": a["w_in"][0],
    }
    outs = [("yp", (P, D)), ("ys", (8 * P, D)), ("new_k", (P, P)), ("new_v", (P, P)), ("new_f", (256, P)), ("new_b", (256, P))]
    nc = bacc.Bacc("TRN2", target_bir_lowering=False, num_devices=1)
    dram = {n: nc.dram_tensor("in_" + n, x.shape, mybir.dt.from_np(x.dtype), kind="ExternalInput").ap() for n, x in host.items()}
    dram["x"] = lambda t: dram["xp"] if t == 0 else dram["xs"][(t - 1) * P:t * P, :]
    for n, s in outs:
        dram[n] = nc.dram_tensor("out_" + n, s, F32, kind="ExternalOutput").ap()
    dram["y_out"] = lambda t: dram["yp"] if t == 0 else dram["ys"][(t - 1) * P:t * P, :]
    program(nc, dram)
    r = run_bass_kernel_spmd(nc, [{"in_" + n: x for n, x in host.items()}], core_ids=[0]).results[0]
    shapes = [(1, P, D), (1, 8 * P, D), (1, 1, P, 2, 64), (1, 1, P, 2, 64), (1, 1, 4, DK, DV), (1, 1, 4, DK, DV)]
    return tuple(r["out_" + n].reshape(s) for (n, _), s in zip(outs, shapes))
```
